# Optimizing a Trainium2 kernel written in Bass

```python
import jax
import jax.numpy as jnp
from jax import lax
import numpy as np

D_MODEL = 1024
BATCH = 1
SEQ = 256
DEPTH = 2

HEAD_DIM = 64
ROPE_THETA = 10000.0
NORM_EPS = 1e-6
QUERY_BLOCK = 128
A_Q_HEADS = 8
A_KV_HEADS = 2
A_WINDOW = 128
B_HEADS = 8
C_HEADS = 8
C_PATTERNS = ((128, 1), (512, 4), (2048, 16))
D_HEADS = 8
MOBA_BLOCK = 256
MOBA_TOPK = 3
MOBA_Q_CHUNK = 16
PEER_HEADS = 8
PEER_N_KEYS = 128
PEER_N_EXPERTS = PEER_N_KEYS * PEER_N_KEYS
PEER_TOPK = 16
PEER_D_KEY = 256
PEER_TOKEN_CHUNK = 128

N_EVEN = (DEPTH + 1) // 2
N_ODD = DEPTH // 2
AB_IN = (A_Q_HEADS + 2 * A_KV_HEADS + 3 * B_HEADS) * HEAD_DIM
AB_OUT = (A_Q_HEADS + B_HEADS) * HEAD_DIM
CD_IN = 3 * (C_HEADS + D_HEADS) * HEAD_DIM
CD_OUT = (C_HEADS + D_HEADS) * HEAD_DIM

kernel_name = 'hybrid_swa_stick_dilated_moba_peer'

def rms_norm(x, g):
    xf = x.astype(jnp.float32)
    y = xf * lax.rsqrt(jnp.mean(xf * xf, axis=-1, keepdims=True) + NORM_EPS)
    return (y * g.astype(jnp.float32)).astype(x.dtype)

def adaln(x, g, shift, scale):
    return rms_norm(x, g) * (1.0 + scale) + shift

def rope(x, pos):
    half = HEAD_DIM // 2
    inv_freq = ROPE_THETA ** (-jnp.arange(half, dtype=jnp.float32) / half)
    ang = pos.astype(jnp.float32)[:, None] * inv_freq[None, :]
    cos = jnp.cos(ang)[None, :, None, :]
    sin = jnp.sin(ang)[None, :, None, :]
    xf = x.astype(jnp.float32)
    x1, x2 = xf[..., :half], xf[..., half:]
    out = jnp.concatenate([x1 * cos - x2 * sin, x2 * cos + x1 * sin], axis=-1)
    return out.astype(x.dtype)

def qk_prepare(q, k, gq, gk, pos):
    return rope(rms_norm(q, gq), pos), rope(rms_norm(k, gk), pos)

def split_cols(x, widths):
    outs, start = [], 0
    for w in widths:
        outs.append(x[..., start:start + w])
        start += w
    return outs

def banded_attention(q, k, v, max_offset, sink=None):
    n, length, hkv, grp, dh = q.shape
    blk = QUERY_BLOCK
    nb = -(-length // blk)
    pad = nb * blk - length
    qb = jnp.pad(q, ((0, 0), (0, pad), (0, 0), (0, 0), (0, 0))).reshape(n, nb, blk, hkv, grp, dh)

    def band(t):
        tp = jnp.pad(t, ((0, 0), (blk, pad), (0, 0), (0, 0))).reshape(n, nb + 1, blk, hkv, dh)
        return jnp.concatenate([tp[:, :-1], tp[:, 1:]], axis=2)

    kb, vb = band(k), band(v)
    s = jnp.einsum('nbqhgd,nbkhd->nbhgqk', qb, kb, preferred_element_type=jnp.float32) * (dh ** -0.5)
    qi = jnp.arange(blk)[:, None]
    ki = jnp.arange(2 * blk)[None, :]
    dist = blk + qi - ki
    key_pos = jnp.arange(nb)[:, None, None] * blk - blk + ki[None]
    valid = (dist >= 0) & (dist <= max_offset) & (key_pos >= 0)
    s = jnp.where(valid[None, :, None, None], s, -jnp.inf)
    lse = jax.nn.logsumexp(s, axis=-1)
    if sink is not None:
        lse = jnp.logaddexp(lse, sink.astype(jnp.float32)[None, None, :, :, None])
    p = jnp.exp(s - lse[..., None])
    o = jnp.einsum('nbhgqk,nbkhd->nbqhgd', p.astype(v.dtype), vb)
    o = o.reshape(n, nb * blk, hkv, grp, dh)[:, :length]
    lse = lse.transpose(0, 1, 4, 2, 3).reshape(n, nb * blk, hkv, grp)[:, :length]
    return o, lse

def stick_breaking_attention(q, k, v):
    b, s_len, h, dh = q.shape
    nb = s_len // QUERY_BLOCK
    qb = q.reshape(b, nb, QUERY_BLOCK, h, dh).transpose(1, 0, 2, 3, 4)
    key_pos = jnp.arange(s_len)

    def one_block(args):
        q_blk, i = args
        z = jnp.einsum('bqhd,bkhd->bhqk', q_blk, k, preferred_element_type=jnp.float32) * (dh ** -0.5)
        q_pos = i * QUERY_BLOCK + jnp.arange(QUERY_BLOCK)
        past = key_pos[None, :] < q_pos[:, None]
        log_keep = jnp.where(past, jax.nn.log_sigmoid(-z), 0.0)
        later = lax.cumsum(log_keep, axis=3, reverse=True) - log_keep
        w = jnp.where(past, jnp.exp(jax.nn.log_sigmoid(z) + later), 0.0)
        return jnp.einsum('bhqk,bkhd->bqhd', w.astype(v.dtype), v)

    out = lax.map(one_block, (qb, jnp.arange(nb)))
    return out.transpose(1, 0, 2, 3, 4).reshape(b, s_len, h, dh)

def dilated_attention(q, k, v):
    b, s_len, h, dh = q.shape
    outs, lses = [], []
    for window, dil in C_PATTERNS:
        m = s_len // dil

        def to_sub(t):
            return t.reshape(b, m, dil, h, dh).transpose(0, 2, 1, 3, 4).reshape(b * dil, m, h, dh)

        o, lse = banded_attention(to_sub(q)[:, :, :, None], to_sub(k), to_sub(v), window // dil)
        outs.append(o[:, :, :, 0].reshape(b, dil, m, h, dh).transpose(0, 2, 1, 3, 4).reshape(b, s_len, h, dh))
        lses.append(lse[..., 0].reshape(b, dil, m, h).transpose(0, 2, 1, 3).reshape(b, s_len, h))
    wts = jax.nn.softmax(jnp.stack(lses), axis=0)
    return jnp.einsum('pbsh,pbshd->bshd', wts.astype(v.dtype), jnp.stack(outs))

def moba_attention(q, k, v):
    b, s_len, h, dh = q.shape
    nblk = -(-s_len // MOBA_BLOCK)
    pad = nblk * MOBA_BLOCK - s_len

    def blocks(t):
        tp = jnp.pad(t, ((0, 0), (0, pad), (0, 0), (0, 0)))
        return tp.reshape(b, nblk, MOBA_BLOCK, h, dh).transpose(0, 3, 1, 2, 4)

    kb, vb = blocks(k), blocks(v)
    k_mean = jnp.mean(kb.astype(jnp.float32), axis=3)
    n_sel = min(MOBA_TOPK, nblk - 1)
    scale = dh ** -0.5
    nq = s_len // MOBA_Q_CHUNK
    qc = q.reshape(b, nq, MOBA_Q_CHUNK, h, dh).transpose(1, 0, 2, 3, 4)
    bi = jnp.arange(b)[:, None, None, None]
    hi = jnp.arange(h)[None, :, None, None]

    def one_chunk(args):
        q_blk, ci = args
        q_pos = ci * MOBA_Q_CHUNK + jnp.arange(MOBA_Q_CHUNK)
        own = (ci * MOBA_Q_CHUNK) // MOBA_BLOCK
        k_own = lax.dynamic_index_in_dim(kb, own, axis=2, keepdims=False)
        v_own = lax.dynamic_index_in_dim(vb, own, axis=2, keepdims=False)
        own_pos = own * MOBA_BLOCK + jnp.arange(MOBA_BLOCK)
        s_own = jnp.einsum('bqhd,bhkd->bhqk', q_blk, k_own, preferred_element_type=jnp.float32) * scale
        s_own = jnp.where(own_pos[None, :] <= q_pos[:, None], s_own, -jnp.inf)
        if n_sel == 0:
            p = jax.nn.softmax(s_own, axis=-1)
            return jnp.einsum('bhqk,bhkd->bqhd', p.astype(v.dtype), v_own)
        gate = jnp.einsum('bqhd,bhnd->bhqn', q_blk, k_mean, preferred_element_type=jnp.float32)
        gate = jnp.where(jnp.arange(nblk) < own, gate, -jnp.inf)
        _, idx = lax.top_k(gate, n_sel)
        k_sel = kb[bi, hi, idx]
        v_sel = vb[bi, hi, idx].reshape(b, h, MOBA_Q_CHUNK, n_sel * MOBA_BLOCK, dh)
        s_sel = jnp.einsum('bqhd,bhqnkd->bhqnk', q_blk, k_sel, preferred_element_type=jnp.float32) * scale
        s_sel = jnp.where((idx < own)[..., None], s_sel, -jnp.inf).reshape(b, h, MOBA_Q_CHUNK, n_sel * MOBA_BLOCK)
        p = jax.nn.softmax(jnp.concatenate([s_sel, s_own], axis=-1), axis=-1).astype(v.dtype)
        p_sel, p_own = p[..., :n_sel * MOBA_BLOCK], p[..., n_sel * MOBA_BLOCK:]
        return (jnp.einsum('bhqk,bhqkd->bqhd', p_sel, v_sel)
                + jnp.einsum('bhqk,bhkd->bqhd', p_own, v_own))

    out = lax.map(one_chunk, (qc, jnp.arange(nq)))
    return out.transpose(1, 0, 2, 3, 4).reshape(b, s_len, h, dh)

def heads_of(t):
    return t.reshape(t.shape[0], t.shape[1], -1, HEAD_DIM)

def mixer_window_and_stick(h, w_in, w_out, sinks, gq, gk, pos):
    b, s_len, _ = h.shape
    qa, ka, va, qb, kb, vb = split_cols(h @ w_in, (A_Q_HEADS * HEAD_DIM, A_KV_HEADS * HEAD_DIM, A_KV_HEADS * HEAD_DIM,
                                                   B_HEADS * HEAD_DIM, B_HEADS * HEAD_DIM, B_HEADS * HEAD_DIM))
    qa, ka = qk_prepare(heads_of(qa), heads_of(ka), gq, gk, pos)
    grp = A_Q_HEADS // A_KV_HEADS
    oa, _ = banded_attention(qa.reshape(b, s_len, A_KV_HEADS, grp, HEAD_DIM), ka, heads_of(va),
                             A_WINDOW - 1, sinks.reshape(A_KV_HEADS, grp))
    ob = stick_breaking_attention(heads_of(qb), heads_of(kb), heads_of(vb))
    y = jnp.concatenate([oa.reshape(b, s_len, -1), ob.reshape(b, s_len, -1)], axis=-1)
    return y @ w_out

def mixer_dilated_and_moba(h, w_in, w_out, gq_c, gk_c, gq_d, gk_d, pos):
    b, s_len, _ = h.shape
    wc, wd = C_HEADS * HEAD_DIM, D_HEADS * HEAD_DIM
    qc, kc, vc, qd, kd, vd = split_cols(h @ w_in, (wc, wc, wc, wd, wd, wd))
    qc, kc = qk_prepare(heads_of(qc), heads_of(kc), gq_c, gk_c, pos)
    qd, kd = qk_prepare(heads_of(qd), heads_of(kd), gq_d, gk_d, pos)
    oc = dilated_attention(qc, kc, heads_of(vc))
    od = moba_attention(qd, kd, heads_of(vd))
    y = jnp.concatenate([oc.reshape(b, s_len, -1), od.reshape(b, s_len, -1)], axis=-1)
    return y @ w_out

def peer_ffn(h, w_query, sub_keys, expert_u, expert_v):
    b, s_len, d = h.shape
    tokens = h.reshape(-1, PEER_TOKEN_CHUNK, d)
    half = PEER_D_KEY // 2

    def one_chunk(x_c):
        qry = (x_c @ w_query).reshape(PEER_TOKEN_CHUNK, PEER_HEADS, 2, half)
        s1 = jnp.einsum('thd,nd->thn', qry[:, :, 0], sub_keys[0], preferred_element_type=jnp.float32)
        s2 = jnp.einsum('thd,nd->thn', qry[:, :, 1], sub_keys[1], preferred_element_type=jnp.float32)
        v1, i1 = lax.top_k(s1, PEER_TOPK)
        v2, i2 = lax.top_k(s2, PEER_TOPK)
        cand = (v1[..., :, None] + v2[..., None, :]).reshape(PEER_TOKEN_CHUNK, PEER_HEADS, PEER_TOPK * PEER_TOPK)
        cand_idx = (i1[..., :, None] * PEER_N_KEYS + i2[..., None, :]).reshape(PEER_TOKEN_CHUNK, PEER_HEADS, PEER_TOPK * PEER_TOPK)
        top_s, pos = lax.top_k(cand, PEER_TOPK)
        experts = jnp.take_along_axis(cand_idx, pos, axis=-1)
        g = jax.nn.softmax(top_s, axis=-1)
        act = jax.nn.gelu(jnp.einsum('td,thkd->thk', x_c, expert_u[experts], preferred_element_type=jnp.float32),
                          approximate=False)
        return jnp.einsum('thk,thkd->td', (g * act).astype(x_c.dtype), expert_v[experts])

    out = lax.map(one_chunk, tokens)
    return out.reshape(b, s_len, d)

def setup_inputs(seed: int = 0) -> dict:
    key = jax.random.key(seed)
    ks = jax.random.split(key, 21)
    D = D_MODEL

    def nrm(k, shape, scale):
        return jax.random.normal(k, shape, jnp.float32) * scale

    return {
        'x': nrm(ks[0], (BATCH, SEQ, D), 1.0),
        'c': nrm(ks[1], (BATCH, D), 1.0),
        'ada_w': nrm(ks[2], (DEPTH, D, 6 * D), 0.5 * D ** -0.5),
        'ada_b': nrm(ks[3], (DEPTH, 6 * D), 0.02),
        'norm_mix_g': 1.0 + nrm(ks[4], (DEPTH, D), 0.02),
        'norm_ffn_g': 1.0 + nrm(ks[5], (DEPTH, D), 0.02),
        'w_in_ab': nrm(ks[6], (N_EVEN, D, AB_IN), D ** -0.5),
        'w_out_ab': nrm(ks[7], (N_EVEN, AB_OUT, D), AB_OUT ** -0.5),
        'sinks_a': nrm(ks[8], (N_EVEN, A_Q_HEADS), 1.0),
        'qnorm_a': 1.0 + nrm(ks[9], (N_EVEN, HEAD_DIM), 0.02),
        'knorm_a': 1.0 + nrm(ks[10], (N_EVEN, HEAD_DIM), 0.02),
        'w_in_cd': nrm(ks[11], (N_ODD, D, CD_IN), D ** -0.5),
        'w_out_cd': nrm(ks[12], (N_ODD, CD_OUT, D), CD_OUT ** -0.5),
        'qnorm_c': 1.0 + nrm(ks[13], (N_ODD, HEAD_DIM), 0.02),
        'knorm_c': 1.0 + nrm(ks[14], (N_ODD, HEAD_DIM), 0.02),
        'qnorm_d': 1.0 + nrm(ks[15], (N_ODD, HEAD_DIM), 0.02),
        'knorm_d': 1.0 + nrm(ks[16], (N_ODD, HEAD_DIM), 0.02),
        'peer_wq': nrm(ks[17], (DEPTH, D, PEER_HEADS * PEER_D_KEY), D ** -0.5),
        'peer_subkeys': nrm(ks[18], (DEPTH, 2, PEER_N_KEYS, PEER_D_KEY // 2), (PEER_D_KEY // 2) ** -0.5),
        'peer_u': nrm(ks[19], (DEPTH, PEER_N_EXPERTS, D), D ** -0.5),
        'peer_v': nrm(ks[20], (DEPTH, PEER_N_EXPERTS, D), 1.0),
    }

def reference(x, c, ada_w, ada_b, norm_mix_g, norm_ffn_g, w_in_ab, w_out_ab, sinks_a, qnorm_a, knorm_a,
              w_in_cd, w_out_cd, qnorm_c, knorm_c, qnorm_d, knorm_d, peer_wq, peer_subkeys, peer_u, peer_v):
    pos = jnp.arange(x.shape[1])
    cond = jax.nn.silu(c)
    for layer in range(DEPTH):
        mod = cond @ ada_w[layer] + ada_b[layer]
        shift_m, scale_m, gate_m, shift_f, scale_f, gate_f = [m[:, None, :] for m in jnp.split(mod, 6, axis=-1)]
        h = adaln(x, norm_mix_g[layer], shift_m, scale_m)
        if layer % 2 == 0:
            i = layer // 2
            y = mixer_window_and_stick(h, w_in_ab[i], w_out_ab[i], sinks_a[i], qnorm_a[i], knorm_a[i], pos)
        else:
            i = layer // 2
            y = mixer_dilated_and_moba(h, w_in_cd[i], w_out_cd[i], qnorm_c[i], knorm_c[i],
                                       qnorm_d[i], knorm_d[i], pos)
        x = x + gate_m * y
        h = adaln(x, norm_ffn_g[layer], shift_f, scale_f)
        x = x + gate_f * peer_ffn(h, peer_wq[layer], peer_subkeys[layer], peer_u[layer], peer_v[layer])
    return x


_drawn_inputs = setup_inputs


def setup_inputs(seed=0):
    import zlib

    import numpy as np

    out = dict(_drawn_inputs(seed))
    spreads = {}
    factors = {'norm_mix_g': 2.89,
     'sinks_a': 4.446,
     'qnorm_a': 6.495,
     'knorm_a': 5.92,
     'qnorm_c': 8.0,
     'knorm_c': 8.0,
     'qnorm_d': 8.0,
     'knorm_d': 8.0}
    for name, (base, spread) in spreads.items():
        noise = np.random.default_rng([zlib.crc32(name.encode()), seed]).standard_normal(out[name].shape)
        drawn = base * np.exp(spread * noise) if base else spread * noise
        out[name] = jnp.asarray(drawn.astype(out[name].dtype))
    for name, factor in factors.items():
        out[name] = (out[name] * factor).astype(out[name].dtype)
    return out
```

```python
import numpy as np
from contextlib import ExitStack

import concourse.bass as bass
from concourse import mybir

F32 = mybir.dt.float32
F32R = mybir.dt.float32r
U32 = mybir.dt.uint32
ALU = mybir.AluOpType
ACT = mybir.ActivationFunctionType
AX = mybir.AxisListType.X

P = 128
T = 256
TILES = T // P
D = 1024
KC = D // P
HD = 64
NH = 8
LAYERS = 2
EPS = 1e-6
BIG = 1e30
SCALE = HD ** -0.5
TRI = 3 * P

NKEYS = 128
PHEADS = 8
TOPK = 16
NE = NKEYS * NKEYS
ROUTES = PHEADS * TOPK

U_STEP = 8
V_STEP = 4
RING = 4

CONST = {}
_at = 0
for _name, _n in (("ident", P), ("iota", P), ("mask_a", TRI), ("mask_c", TRI), ("mask_d", TRI),
                  ("past", TRI), ("not_past", TRI), ("neg_tri", P), ("neg_ones", P),
                  ("cos", 2 * HD), ("sin", 2 * HD)):
    CONST[_name] = (_at, _at + _n)
    _at += _n
CONST_N = _at


def constants():
    c = np.zeros((P, CONST_N), np.float32)

    def put(name, a):
        c[:, CONST[name][0]:CONST[name][1]] = a

    i = np.arange(P)
    put("ident", np.eye(P))
    put("iota", np.broadcast_to(i, (P, P)))
    dist = np.concatenate([i[:, None] - i[None], P + i[:, None] - i[None], i[:, None] - i[None]], 1)
    put("mask_a", np.where((dist >= 0) & (dist <= P - 1), 0.0, -BIG))
    put("mask_d", np.where(dist >= 0, 0.0, -BIG))
    seen = sum(((dist >= 0) & (dist % r == 0) & (dist <= w)).astype(int)
               for w, r in ((128, 1), (512, 4), (2048, 16)))
    put("mask_c", np.where(seen > 0, np.log(np.maximum(seen, 1)) / SCALE, -BIG))
    gap = np.concatenate([i[None] - i[:, None], P + i[None] - i[:, None], i[None] - i[:, None]], 1)
    put("past", gap > 0)
    put("not_past", np.where(gap > 0, 0.0, -BIG))
    put("neg_tri", -(i[:, None] >= i[None]).astype(np.float32))
    put("neg_ones", -1.0)
    half = HD // 2
    inv = np.float32(10000.0) ** (-np.arange(half, dtype=np.float32) / np.float32(half))
    ang = np.arange(T, dtype=np.float32)[:, None] * inv[None].astype(np.float32)
    cos, sin = np.cos(ang), np.sin(ang)
    for t in range(TILES):
        a, s = cos[t * P:(t + 1) * P], sin[t * P:(t + 1) * P]
        c0, s0 = CONST["cos"][0] + t * HD, CONST["sin"][0] + t * HD
        c[:, c0:c0 + HD] = np.concatenate([a, a], 1)
        c[:, s0:s0 + HD] = np.concatenate([-s, s], 1)
    return c


def spread(a, axis, n):
    a = a.unsqueeze(axis)
    shape = list(a.shape)
    shape[axis] = n
    return a.to_broadcast(shape)


def trunk_kernel(nc, x, c, ada_w, ada_b, norm_mix_g, norm_ffn_g, w_in_ab, w_out_ab, sinks_a, qnorm_a,
                 knorm_a, w_in_cd, w_out_cd, qnorm_c, knorm_c, qnorm_d, knorm_d, peer_wq, peer_subkeys,
                 peer_u, peer_v, const, out):
    ctx = ExitStack()
    with ctx:
        base = (nc.sbuf_base + 31) // 32 * 32
        KB = 1024

        def at(name, kb, shape, dt=F32):
            return nc.alloc_sbuf_tensor_at(name, [P] + shape, dt, offset=base + int(kb * KB))

        W = at("W", 0, [NKEYS, T])
        w_ins = [at("w_in_ab_sb", 0, [KC, 2304]), at("w_in_cd_sb", 0, [KC, 3072])]
        w_out = at("w_out", 96, [KC, D])
        qk_T = [at(f"qk_T{n}", 64 + 4 * n, [4, T]) for n in range(4)]
        sc = at("sc", 80, [4, TRI])
        pT = at("pT", 86, [4, TRI])
        e_abs = at("e_abs", 192, [4, TRI])
        tmp = [at(f"tmp{n}", 80 + 4 * n, [TILES, 512]) for n in range(3)]
        rope_c = at("rope_c", 92, [4, 2 * HD])
        rope_s = at("rope_s", 94, [4, 2 * HD])
        wq = at("wq", 0, [KC, 2048])
        hTf = at("hTf", 64, [KC, T])
        hf = at("hf", 72, [TILES, D])
        qryT = at("qryT", 80, [2 * PHEADS, T])

        xs = at("xs", 128, [TILES, D])
        mod = at("mod", 136, [6, D])
        cst = at("cst", 160, [CONST_N])
        hT = at("hT", 172, [KC, T])
        yT = at("yT", 172, [KC, T])
        ada = [at(f"ada{n}", kb, [KC, 512]) for n, kb in enumerate((172, 96, 112))]
        h = at("h", 180, [TILES, D])
        g_mix = at("g_mix", 188, [D])
        g_ffn = at("g_ffn", 136, [D])
        tok = [at(f"tok{n}", 180 + 4 * n if n < 5 else 140, [TILES, 512]) for n in range(6)]

        hi = [at(f"hi{n}", kb, [D], F32R) for n, kb in enumerate((128, 192, 136, 140))]
        lo = [at(f"lo{n}", kb, [D], F32R) for n, kb in enumerate((132, 196))]
        S = at("S", 112, [TILES * PHEADS, 2, NKEYS])
        uT = [at(f"uT{n}", kb, [D]) for n, kb in enumerate((152, 188, 144, 148))]
        ring = [at("ring0", 156, [D])] + [at(f"ring{n}", 172 + 4 * n, [D]) for n in range(1, RING)]
        hT_hi = at("hT_hi", 160, [KC, T], F32R)
        hT_lo = at("hT_lo", 168, [KC, T], F32R)
        w_hi = [at(f"w_hi{n}", 144 + n, [T], F32R) for n in range(4)]
        w_lo = [at(f"w_lo{n}", 148 + n, [T], F32R) for n in range(4)]
        zeros = at("zeros", 152, [512], F32R)
        one_1 = at("one_1", 140, [4, 4, NKEYS])
        one_2 = at("one_2", 176, [4, 4, NKEYS])
        routes_T = at("routes_T", 136, [3, T])
        cols = {e: at(f"cols_{e}", 139 + 0.25 * n, [2, 16]) for n, e in enumerate(("dve", "act", "pool"))}
        gap = at("gap", 148, [4, NKEYS])
        x_back = at("x_back", 160, [TILES, D])
        gate_b = at("gate_b", 168, [D])
        yg = at("yg", 180, [TILES, D])

        ident = at("ident", 200, [P])
        iota = at("iota", 200.5, [P])
        routes = at("routes", 201, [3, T])
        subk = at("subk", 201, [2, P])
        subk_T = at("subk_T", 202, [2, P])
        cond = at("cond", 203, [4, KC])
        acc_m = at("acc_m", 203.25, [2, 512])
        gains = at("gains", 204, [4, HD])
        stat = at("stat", 207.625, [8])
        ssq = at("ssq", 205.125, [2, 64])
        sink = at("sink", 205.75, [8])
        smax = at("smax", 206, [3, 4, 2])
        fix = at("fix", 204, [2, NKEYS])
        cut = at("cut", 205, [TOPK * TOPK])
        cand = at("cand", 206, [TOPK, TOPK])
        topv = at("topv", 207, [3, TOPK])
        topi = at("topi", 207.1875, [3, TOPK], U32)
        topf = at("topf", 207.375, [3, TOPK])
        topb = at("topb", 207.5625, [TOPK], U32)

        ps = ctx.enter_context(nc.psum_tensor("ps", [P, 8, 512], F32))

        x_keep = nc.dram_tensor("x_keep", [TILES, P, D], F32, kind="Internal").ap()
        gate_keep = nc.dram_tensor("gate_keep", [1, D], F32, kind="Internal").ap()

        def sem(name):
            return ctx.enter_context(nc.semaphore(name))

        def k_(name):
            a, b = CONST[name]
            return cst[:, a:b]

        cst_in, x_in, out_sem = sem("tables_in"), sem("x_in"), sem("out_done")
        layer_done = sem("layer_done")
        COUNTS = dict(
            c_in=16, ada_b=16, cst_in=16, ada_in0=64, ada_in1=64, ada_in2=64, w_in0=16, w_in1=16, w_in2=16,
            w_in3=16, w_in4=16, w_in5=0, w_out=16, g_mix=16, gains=48, g_ffn=16, subk=16, wq=64, x_kept=32,
            x_back=32, **{f"u_in{n}": NKEYS // RING * 64 for n in range(RING)},
            **{f"v_in{n}": NKEYS // RING * 16 for n in range(RING)},
            ada_sum=12, mix_T=4, proj=10, qk_turned=4, scores=4, p_turned=4, y=4, w_out_mult=2, subk_turned=1,
            ffn_T=4, qry=8, S_mult=8, u_mult=NKEYS + 4, routes_turned=1, gate_mult=T // 4 + 4,
            v_mult=NKEYS + 4, v_all=1,
            ada_used=12, mix_norm=2, ssq=1, roped=2, masked=4, p_ready=4, log_w=2, max=2, mixed=2, ffn_norm=2,
            x_read=1, ffn_lo=4, u_turned=NKEYS + RING, route_step=0, gate_in=1, routed=1, gated=T // 4 + 4,
            hot_dve=T // 4 + 4, cols_dve=T // 16, dve_held=0, zeros=1, v_lo=NKEYS + RING,
            c_exp=1, ada_done=12, mix_rms=1, hT=4, proj_out=10, qk_rms=1, qk_T=4, ln_done=2, pT=4, exp=2, y_out=4,
            subk_T=1, ffn_rms=1, ffn_hi=4, qry_out=8, S_out=8, u_gelu=NKEYS // 2 + 4, u_hi=NKEYS, act_held=0,
            hot_act=T // 4 + 4, cols_act=T // 16, gap=T // 16, gate_exp=1, routes_T=1, v_hi=NKEYS,
            u_lo=NKEYS + 4, hot_pool=T // 4 + 4, cols_pool=T // 16, pool_held=0)
        SEMS = {n: sem(n) for n in COUNTS}

        def s(name):
            return SEMS[name]

        def after(name, l, count):
            return SEMS[name], count + COUNTS[name] * l if l else count

        chain = {n: sem(f"{n}_step") for n in ("dve", "act", "pool")}
        steps = {n: 0 for n in chain}

        def link(eng, name, ins):
            steps[name] += 1
            ins.then_inc(chain[name], 1)
            eng.wait_ge(chain[name], steps[name])

        block = ctx.enter_context(nc.Block())

        w_in_l = [w_in_ab[0], w_in_cd[0]]
        w_out_l = [w_out_ab[0], w_out_cd[0]]
        SETS = [[(0, 512), (512, 256), (1792, 512), (768, 512), (1280, 512)],
                [(0, 512), (512, 512), (1024, 512), (1536, 512), (2048, 512), (2560, 512)]]
        TOKEN_SETS = [3, 6]
        GROUPS = [2 * TOKEN_SETS[0] + 4, 2 * TOKEN_SETS[1]]
        NORMS = [[(0, 0, 8, 0), (1, 0, 2, 1)],
                 [(0, 0, 8, 0), (1, 0, 8, 1), (3, 0, 8, 2), (4, 0, 8, 3)]]

        def perm(a):
            return a.rearrange("t (q c j) -> t c q j", q=4, c=KC)

        uv = peer_u.rearrange("l (g i j) (q d) -> l q j i g d", g=4, i=32, q=4)
        vv = peer_v.rearrange("l (i j) d -> l j i d", j=NKEYS)


        QT = [[(qk_T[0], qk_T[1]), (qk_T[2], qk_T[3])]] * 2

        def v_at(l, q, i):
            if l == 0:
                return (1, P + HD * q) if q < 2 else (2, HD * (4 * (q - 2) + i))
            return (2 if q < 2 else 5, HD * (4 * (q % 2) + i))

        def pick(R, half, dst):
            eq = cand[:, :, :]
            R(nc.vector.tensor_tensor(eq, spread(topf[:, 2, :], 2, TOPK), spread(iota[:, 0:TOPK], 1, TOPK),
                                      ALU.is_equal))
            R(nc.vector.tensor_tensor(eq, eq, spread(topf[:, half, :], 1, TOPK), ALU.mult))
            R(nc.vector.tensor_reduce(dst, eq, AX, ALU.add))

        @block.sync
        def _(sp):
            sp.dma_start(ident[:, :], const[:, 0:P]).then_inc(cst_in, 16)
            sp.dma_start(iota[:, :], const[:, P:2 * P]).then_inc(cst_in, 16)
            sp.dma_start(xs[:, :, :], x.rearrange("a (t p) d -> p (a t) d", p=P)).then_inc(x_in, 16)
            for l in range(LAYERS):
                if l:
                    sp.wait_ge(layer_done, l)
                sp.dma_start(cond[:, 0, :], c.rearrange("a (p c) -> p (a c)", c=KC)).then_inc(s("c_in"), 16)
                sp.dma_start(mod[0:1, :, :], ada_b[l:l + 1, :].rearrange("a (m d) -> a m d", d=D)
                             ).then_inc(s("ada_b"), 16)
                sp.dma_start(cst[:, :], const).then_inc(s("cst_in"), 16)
                for n in range(12):
                    if n >= 3:
                        sp.wait_ge(*after("ada_used", l, n - 2))
                    sp.dma_start(ada[n % 3][:, :, :],
                                 ada_w[l].rearrange("(p c) n -> p c n", c=KC)[:, :, 512 * n:512 * n + 512]
                                 ).then_inc(s(f"ada_in{n % 3}"), 16)
                for n, (a, m) in enumerate(SETS[l]):
                    sp.dma_start(w_ins[l][:, :, a:a + m],
                                 w_in_l[l].rearrange("(p c) n -> p c n", c=KC)[:, :, a:a + m]
                                 ).then_inc(s(f"w_in{n}"), 16)
                sp.wait_ge(*after("ada_done", l, 12))
                sp.dma_start(w_out[:, :, :], w_out_l[l].rearrange("(c p) n -> p c n", p=P)
                             ).then_inc(s("w_out"), 16)
                sp.dma_start(g_mix[:, :], norm_mix_g[l:l + 1, :].to_broadcast([P, D])
                             ).then_inc(s("g_mix"), 16)
                names = [(qnorm_a, knorm_a, sinks_a), (qnorm_c, knorm_c, qnorm_d, knorm_d)][l]
                for n, g in enumerate(names):
                    dst = gains[:, n, :] if g is not sinks_a else sink[:, :]
                    sp.dma_start(dst, g[0:1, :].to_broadcast([P, g.shape[1]])).then_inc(s("gains"), 16)
                sp.wait_ge(*after("mix_norm", l, TILES))
                sp.dma_start(g_ffn[:, :], norm_ffn_g[l:l + 1, :].to_broadcast([P, D])
                             ).then_inc(s("g_ffn"), 16)
                sp.dma_start(subk[:, :, :], peer_subkeys[l].rearrange("a n d -> n a d")
                             ).then_inc(s("subk"), 16)
                sp.wait_ge(*after("proj", l, GROUPS[l]))
                for q in range(4):
                    sp.dma_start(wq[32 * q:32 * q + 32, :, :],
                                 peer_wq[l, 256 * q:256 * q + 256, :].rearrange("(c j) n -> j c n", j=32)
                                 ).then_inc(s("wq"), 16)
                sp.wait_ge(*after("mixed", l, TILES))
                sp.dma_start(x_keep.rearrange("t p d -> p t d"), xs[:, :, :]).then_inc(s("x_kept"), 16)
                sp.dma_start(gate_keep, mod[0:1, 5, :]).then_inc(s("x_kept"), 16)
                sp.wait_ge(*after("x_kept", l, 32))
                sp.wait_ge(*after("ffn_lo", l, 4))
                sp.wait_ge(*after("x_read", l, 1))
                with sp.Fori(0, NKEYS // U_STEP) as it:
                    for b in range(U_STEP):
                        sp.wait_ge(*after("u_turned", l, it * U_STEP + (b + 1)))
                        for q in range(4):
                            sp.dma_start(ring[b % RING][32 * q:32 * q + 32, :].rearrange("i (g d) -> i g d", g=4),
                                         uv[l, q, bass.ds(it * U_STEP + b, 1)].rearrange("a i g d -> (a i) g d")
                                         ).then_inc(s(f"u_in{b % RING}"), 16)
                sp.wait_ge(*after("gated", l, T // 4 + 4))
                with sp.Fori(0, NKEYS // V_STEP) as it:
                    for b in range(V_STEP):
                        sp.wait_ge(*after("v_lo", l, it * V_STEP + (b + 1)))
                        sp.dma_start(ring[b % RING][:, :],
                                     vv[l, bass.ds(it * V_STEP + b, 1)].rearrange("a i d -> (a i) d")
                                     ).then_inc(s(f"v_in{b % RING}"), 16)
                sp.wait_ge(*after("v_all", l, 1))
                sp.dma_start(x_back[:, :, :], x_keep.rearrange("t p d -> p t d")).then_inc(s("x_back"), 16)
                sp.dma_start(gate_b[:, :], gate_keep.to_broadcast([P, D])).then_inc(s("x_back"), 16)
            sp.wait_ge(layer_done, LAYERS)
            sp.dma_start(out.rearrange("a (t p) d -> p (a t) d", p=P), xs[:, :, :]).then_inc(out_sem, 16)
            sp.wait_ge(out_sem, 16)

        @block.tensor
        def _(pe):
            mm, tr = nc.tensor.matmul, nc.tensor.transpose
            pe.wait_ge(cst_in, 32)
            for l in range(LAYERS):
                if l:
                    pe.wait_ge(layer_done, l)
                pe.wait_ge(*after("cst_in", l, 16))
                pe.wait_ge(*after("ada_b", l, 16))
                for n in range(12):
                    pe.wait_ge(*after("ada_used", l, n + 1))
                    if n >= 2:
                        pe.wait_ge(*after("ada_done", l, n - 1))
                    mm(ps[:, n % 2, :], k_("neg_ones"), acc_m[:, n % 2, :], start=True, stop=False)
                    mm(ps[:, n % 2, :], k_("neg_ones")[0:1, :], mod[0:1, n // 2, 512 * (n % 2):512 * (n % 2) + 512],
                       start=False, stop=True).then_inc(s("ada_sum"), 1)
                hv = h[:, :, :].rearrange("p t (m c) -> p t c m", c=KC)
                for t in range(TILES):
                    pe.wait_ge(*after("mix_norm", l, t + 1))
                    for half in range(2):
                        for j in range(4):
                            last = tr(ps[:, 2 + 2 * t + half, P * j:P * j + P], hv[:, t, 4 * half + j, :], ident[:, :])
                        last.then_inc(s("mix_T"), 1)
                pe.wait_ge(*after("hT", l, 4))
                g = 0
                for n, (a, m) in enumerate(SETS[l]):
                    pe.wait_ge(*after(f"w_in{n}", l, 16))
                    for t in range(2):
                        if g == 0 or g >= 8:
                            if g >= 8:
                                pe.wait_ge(*after("proj_out", l, g - 7))
                        bank = g % 8
                        if n < TOKEN_SETS[l]:
                            for k in range(KC):
                                last = mm(ps[:, bank, 0:m], hT[:, k, P * t:P * t + P], w_ins[l][:, k, a:a + m],
                                          start=k == 0, stop=k == KC - 1)
                        else:
                            for j in range(2):
                                col = a + P * (2 * t + j)
                                for k in range(KC):
                                    last = mm(ps[:, bank, T * j:T * j + T], w_ins[l][:, k, col:col + P], hT[:, k, :],
                                              start=k == 0, stop=k == KC - 1)
                        last.then_inc(s("proj"), 1)
                        g += 1
                pe.wait_ge(*after("proj_out", l, GROUPS[l]))
                for n, (b, _, heads, _) in enumerate(NORMS[l]):
                    pe.wait_ge(*after("roped", l, n + 1))
                    for t in range(TILES):
                        if n >= 2:
                            pe.wait_ge(*after("qk_T", l, 2 * n + t - 3))
                        width = heads * HD if heads == 8 else 2 * P
                        src = tok[b][:, t, 0:512] if heads == 8 else tok[4][:, t, 0:2 * P]
                        for j in range(width // P):
                            last = tr(ps[:, (2 * n + t) % 4, P * j:P * j + P], src[:, P * j:P * j + P], ident[:, :])
                        last.then_inc(s("qk_turned"), 1)

                def q_of(q, i):
                    e = 64 * (i % 2)
                    return (QT[l][q // 2][0][e:e + 64, 2 * (q % 2) + i // 2, :],
                            QT[l][q // 2][1][e:e + 64, 2 * (q % 2) + i // 2 if (l, q // 2) != (0, 0) else q % 2, :])

                def scores(q):
                    if q:
                        pe.wait_ge(*after("masked", l, q))
                    for i in range(4):
                        qq, kk = q_of(q, i)
                        if l == 0 and q >= 2:
                            mm(ps[:, i, 0:T], kk[:, 0:P], qq, start=True, stop=True)
                            last = mm(ps[:, i, T:TRI], kk[:, P:T], qq[:, P:T], start=True, stop=True)
                        else:
                            mm(ps[:, i, 0:P], qq[:, 0:P], kk[:, 0:P], start=True, stop=True)
                            last = mm(ps[:, i, P:TRI], qq[:, P:T], kk, start=True, stop=True)
                    last.then_inc(s("scores"), 1)

                pe.wait_ge(*after("qk_T", l, 2 * len(NORMS[l])))
                scores(0)
                for q in range(4):
                    if q:
                        pe.wait_ge(*after("y_out", l, q))
                    pe.wait_ge(*after("p_ready", l, q + 1))
                    if l == 0 and q >= 2:
                        for i in range(4):
                            qq, kk = q_of(q, i)
                            mm(ps[:, 4 + i, 0:TRI], k_("neg_tri"), sc[:, i, :], start=True, stop=False)
                            mm(ps[:, 4 + i, P:T], k_("neg_ones"), sc[:, i, T:TRI], start=False, stop=False)
                            mm(ps[:, 4 + i, 0:T], kk[:, 0:P], qq, start=False, stop=False)
                            last = mm(ps[:, 4 + i, T:TRI], kk[:, P:T], qq[:, P:T], start=False, stop=True)
                    else:
                        for i in range(4):
                            for j in range(3):
                                last = tr(ps[:, 4 + i, P * j:P * j + P], sc[:, i, P * j:P * j + P], ident[:, :])
                    last.then_inc(s("p_turned"), 1)
                    if q < 3:
                        scores(q + 1)
                    pe.wait_ge(*after("pT", l, q + 1))
                    for i in range(4):
                        e = 64 * (i % 2)
                        buf, col = v_at(l, q, i)
                        v = tok[buf]
                        mm(ps[e:e + 64, 4 + i // 2, 0:T], v[:, 0, col:col + HD], pT[:, i, 0:T], start=True, stop=False)
                        last = mm(ps[e:e + 64, 4 + i // 2, P:T], v[:, 1, col:col + HD], pT[:, i, T:TRI],
                                  start=False, stop=True)
                    last.then_inc(s("y"), 1)
                pe.wait_ge(*after("w_out", l, 16))
                pe.wait_ge(*after("y_out", l, 4))
                for t in range(TILES):
                    for half in range(2):
                        for k in range(KC):
                            last = mm(ps[:, 2 * t + half, :], yT[:, k, P * t:P * t + P],
                                      w_out[:, k, 512 * half:512 * half + 512], start=k == 0, stop=k == KC - 1)
                    last.then_inc(s("w_out_mult"), 1)

                pe.wait_ge(*after("subk", l, 16))
                for a in range(2):
                    last = tr(ps[:, 4, P * a:P * a + P], subk[:, a, :], ident[:, :])
                last.then_inc(s("subk_turned"), 1)
                for t in range(TILES):
                    pe.wait_ge(*after("ffn_norm", l, t + 1))
                    for half in range(2):
                        if t:
                            pe.wait_ge(*after("ffn_lo", l, half + 1))
                        for j in range(4):
                            last = tr(ps[:, 6 + half, P * j:P * j + P], hf[:, t, P * (4 * half + j):P * (4 * half + j) + P], ident[:, :])
                        last.then_inc(s("ffn_T"), 1)
                pe.wait_ge(*after("wq", l, 64))
                pe.wait_ge(*after("ffn_lo", l, 4))
                for g in range(PHEADS):
                    if g >= 4:
                        pe.wait_ge(*after("qry_out", l, g - 3))
                    for j in range(2):
                        for k in range(KC):
                            last = mm(ps[:, g % 4, T * j:T * j + T], wq[:, k, P * (2 * g + j):P * (2 * g + j) + P],
                                      hTf[:, k, :], start=k == 0, stop=k == KC - 1)
                    last.then_inc(s("qry"), 1)
                pe.wait_ge(*after("qry_out", l, PHEADS))
                pe.wait_ge(*after("subk_T", l, 1))
                for n in range(8):
                    t, g = n // 4, n % 4
                    if n >= 4:
                        pe.wait_ge(*after("S_out", l, n - 3))
                    for j in range(4):
                        last = mm(ps[:, 4 + n % 4, P * j:P * j + P], qryT[:, 4 * g + j, P * t:P * t + P],
                                  subk_T[:, j % 2, :], start=True, stop=True)
                    last.then_inc(s("S_mult"), 1)
                pe.sem_inc(s("u_mult"), 4)
                with pe.Fori(0, NKEYS // U_STEP) as it:
                    for b in range(U_STEP):
                        dst = ps[:, (b // 2) % 4, T * (b % 2):T * (b % 2) + T]
                        if b % 2 == 0:
                            pe.wait_ge(*after("u_gelu", l, it * (U_STEP // 2) + (b // 2 + 1)))
                        pe.wait_ge(*after("u_hi", l, it * U_STEP + (b + 1)))
                        n = 0
                        for w, m in ((hi[b % 4], hT_hi), (hi[b % 4], hT_lo), (lo[b % 2], hT_hi)):
                            if w is lo[b % 2]:
                                pe.wait_ge(*after("u_lo", l, it * U_STEP + (b + 5)))
                            for k in range(KC):
                                last = mm(dst, w[:, P * k:P * k + P], m[:, k, :], start=n == 0, stop=n == 3 * KC - 1)
                                n += 1
                        last.then_inc(s("u_mult"), 1)
                pe.wait_ge(*after("routed", l, 1))
                pe.wait_ge(*after("u_gelu", l, NKEYS // 2 + 4))
                for a in range(3):
                    for t in range(TILES):
                        last = tr(ps[:, 4 + a, P * t:P * t + P], routes[:, a, P * t:P * t + P], ident[:, :])
                last.then_inc(s("routes_turned"), 1)
                pe.sem_inc(s("gate_mult"), 4)
                with pe.Fori(0, T // 16) as it:
                    for b in range(4):
                        pe.wait_ge(*after("gated", l, it * 4 + (b + 1)))
                        pe.wait_ge(*after("hot_dve", l, it * 4 + (b + 5)))
                        pe.wait_ge(*after("hot_pool", l, it * 4 + (b + 5)))
                        pe.wait_ge(*after("hot_act", l, it * 4 + (b + 5)))
                        for k in range(4):
                            last = mm(ps[:, b, P * k:P * k + P], one_1[:, b, k, :], one_2[:, b, k, :],
                                      start=True, stop=True)
                        last.then_inc(s("gate_mult"), 1)
                pe.wait_ge(*after("zeros", l, 1))
                for g in range(4):
                    last = mm(ps[:, 4 + g, :], zeros[:, 0:P], zeros[:, :], start=True, stop=False)
                pe.sem_inc(s("v_mult"), 4)
                with pe.Fori(0, NKEYS // V_STEP) as it:
                    for b in range(V_STEP):
                        pe.wait_ge(*after("v_hi", l, it * V_STEP + (b + 1)))
                        pe.wait_ge(*after("v_lo", l, it * V_STEP + (b + 1 + RING)))
                        for w, v in ((w_hi[b], hi[b]), (w_lo[b], hi[b]), (w_hi[b], lo[b % 2])):
                            for g in range(4):
                                last = mm(ps[:, 4 + g, :], w[:, P * (g // 2):P * (g // 2) + P],
                                          v[:, 512 * (g % 2):512 * (g % 2) + 512], start=False, stop=False,
                                          skip_group_check=True)
                        last.then_inc(s("v_mult"), 1)
                for g in range(4):
                    last = mm(ps[:, 4 + g, :], zeros[:, 0:P], zeros[:, :], start=False, stop=True)
                last.then_inc(s("v_all"), 1)

        @block.vector
        def _(dve):
            V = nc.vector
            L = lambda ins: link(dve, "dve", ins)

            dve.wait_ge(cst_in, 32)
            dve.wait_ge(x_in, 16)
            for l in range(LAYERS):
                if l:
                    dve.wait_ge(layer_done, l)
                dve.wait_ge(*after("c_exp", l, 1))
                L(V.tensor_scalar(cond[:, 2, :], cond[:, 1, :], 1.0, None, ALU.add))
                L(V.reciprocal(cond[:, 3, :], cond[:, 2, :]))
                L(V.tensor_tensor(cond[:, 2, :], cond[:, 3, :], cond[:, 0, :], ALU.mult))
                for n in range(12):
                    dve.wait_ge(*after(f"ada_in{n % 3}", l, 16 * (n // 3 + 1)))
                    if n >= 2:
                        dve.wait_ge(*after("ada_sum", l, n - 1))
                    a, w = acc_m[:, n % 2, :], ada[n % 3]
                    L(V.tensor_scalar(a, w[:, 0, :], cond[:, 2, 0:1], None, ALU.mult))
                    for k in range(1, KC):
                        ins = V.scalar_tensor_tensor(a, w[:, k, :], cond[:, 2, k:k + 1], a, ALU.mult, ALU.add)
                        if k < KC - 1:
                            L(ins)
                    ins.then_inc(s("ada_used"), 1)
                dve.wait_ge(*after("ada_done", l, 12))

                def norm(gain, gain_in, scale, shift, mid, add, done, rms):
                    dve.wait_ge(*after(gain_in, l, 16))
                    L(V.scalar_tensor_tensor(gain[:, :], mod[:, scale, :], 1.0, gain[:, :], ALU.add, ALU.mult))
                    dve.wait_ge(*after(rms, l, 1))
                    L(V.reciprocal(stat[:, 4:6], stat[:, 2:4]))
                    for t in range(TILES):
                        L(V.scalar_tensor_tensor(mid[:, t, :], xs[:, t, :], stat[:, 4 + t:5 + t], gain[:, :],
                                                 ALU.mult, ALU.mult))
                        add(t, mod[:, shift, :]).then_inc(done, 1)

                def add_mix(t, shift):
                    return V.tensor_tensor(h[:, t, :], h[:, t, :], shift, ALU.add)

                def add_ffn(t, shift):
                    return V.tensor_tensor(hf[:, t, :].rearrange("p (c q j) -> p q c j", c=KC, q=4),
                                           yg[:, t, :].rearrange("p (q c j) -> p q c j", c=KC, q=4),
                                           shift.rearrange("p (q c j) -> p q c j", c=KC, q=4), ALU.add)

                norm(g_mix, "g_mix", 1, 0, h, add_mix, s("mix_norm"), "mix_rms")
                dve.wait_ge(*after("proj_out", l, GROUPS[l]))
                dve.wait_ge(*after("gains", l, 16 * (3 if l == 0 else 4)))
                dve.wait_ge(*after("cst_in", l, 16))
                half = HD // 2
                cosv = k_("cos").rearrange("p (t d) -> p t d", t=TILES)
                sinv = k_("sin").rearrange("p (t d) -> p t d", t=TILES)
                for n, _ in enumerate(NORMS[l]):
                    cv = rope_c[:, n, :].rearrange("p (t d) -> p t d", t=TILES)
                    sv = rope_s[:, n, :].rearrange("p (t d) -> p t d", t=TILES)
                    g = gains[:, n, :]
                    V.tensor_tensor(cv, cosv, spread(g, 1, TILES), ALU.mult)
                    V.tensor_tensor(sv[:, :, 0:half], sinv[:, :, 0:half], spread(g[:, half:HD], 1, TILES), ALU.mult)
                    L(V.tensor_tensor(sv[:, :, half:HD], sinv[:, :, half:HD], spread(g[:, 0:half], 1, TILES), ALU.mult))
                for n, (b, c0, heads, _) in enumerate(NORMS[l]):
                    xv = tok[b][:, :, c0:c0 + heads * HD]
                    sq = tmp[0][:, :, 0:heads * HD]
                    L(V.tensor_tensor(sq, xv, xv, ALU.mult))
                    L(V.tensor_reduce(ssq[:, 0, 16 * n:16 * n + 2 * heads].rearrange("p (t h) -> p t h", t=TILES),
                                      sq.rearrange("p t (h d) -> p t h d", d=HD), AX, ALU.add))
                V.tensor_copy(stat[:, 0:1], stat[:, 0:1]).then_inc(s("ssq"), 1)
                dve.wait_ge(*after("qk_rms", l, 1))
                cnt = 20 if l == 0 else 64
                L(V.reciprocal(ssq[:, 1, 0:cnt], ssq[:, 1, 0:cnt]))
                for n, (b, c0, heads, _) in enumerate(NORMS[l]):
                    w = heads * HD
                    xv = tok[b][:, :, c0:c0 + w].rearrange("p t (h d) -> p t h d", d=HD)
                    t0, t1, t2 = (t[:, :, 0:w].rearrange("p t (h d) -> p t h d", d=HD) for t in tmp)
                    r = ssq[:, 1, 16 * n:16 * n + 2 * heads].rearrange("p (t h) -> p t h", t=TILES)
                    cv = rope_c[:, n, :].rearrange("p (t d) -> p t d", t=TILES)
                    sv = rope_s[:, n, :].rearrange("p (t d) -> p t d", t=TILES)
                    L(V.tensor_tensor(t1, xv, spread(r, 3, HD), ALU.mult))
                    V.tensor_tensor(t0, t1, spread(cv, 2, heads), ALU.mult)
                    V.tensor_tensor(t2[:, :, :, 0:half], t1[:, :, :, half:HD], spread(sv[:, :, 0:half], 2, heads),
                                    ALU.mult)
                    L(V.tensor_tensor(t2[:, :, :, half:HD], t1[:, :, :, 0:half], spread(sv[:, :, half:HD], 2, heads),
                                      ALU.mult))
                    if heads == 8:
                        ins = V.tensor_tensor(xv, t0, t2, ALU.add)
                    else:
                        kd = tok[4][:, :, 0:2 * P].rearrange("p t (h e d) -> p t h e d", e=2, d=HD)
                        V.tensor_tensor(kd[:, :, :, 0, :], t0, t2, ALU.add)
                        ins = V.tensor_tensor(kd[:, :, :, 1, :], t0, t2, ALU.add)
                    L(ins)
                    V.tensor_copy(stat[:, 0:1], stat[:, 0:1]).then_inc(s("roped"), 1)
                if l == 0:
                    dve.wait_ge(*after("gains", l, 48))
                for q in range(4):
                    dve.wait_ge(*after("scores", l, q + 1))
                    if q:
                        dve.wait_ge(*after("p_turned", l, q))
                    if l == 0 and q >= 2:
                        dve.wait_ge(*after("ln_done", l, q - 1))
                        V.scalar_tensor_tensor(sc[:, :, :], ps[:, 0:4, 0:TRI], 0.0, e_abs[:, :, :],
                                               ALU.max, ALU.add).then_inc(s("masked"), 1)
                        dve.wait_ge(*after("masked", l, q + 1))
                        V.tensor_tensor(sc[:, :, :], sc[:, :, :], spread(k_("past"), 1, 4),
                                        ALU.mult).then_inc(s("p_ready"), 1)
                        dve.wait_ge(*after("p_turned", l, q + 1))
                        dve.wait_ge(*after("y", l, q))
                        V.tensor_tensor(pT[:, :, :], ps[:, 4:8, 0:TRI], spread(k_("not_past"), 1, 4),
                                        ALU.add).then_inc(s("log_w"), 1)
                        continue
                    mask = k_("mask_a" if l == 0 else "mask_c" if q < 2 else "mask_d")
                    V.tensor_tensor(sc[:, :, :], ps[:, 0:4, 0:TRI], spread(mask, 1, 4),
                                    ALU.add).then_inc(s("masked"), 1)
                    dve.wait_ge(*after("masked", l, q + 1))
                    V.tensor_reduce(smax[:, 0, :, 0], sc[:, :, 0:P], AX, ALU.max)
                    L(V.tensor_reduce(smax[:, 0, :, 1], sc[:, :, P:TRI], AX, ALU.max))
                    if l == 0:
                        sk = spread(sink[:, 4 * q:4 * q + 4], 2, 2)
                        L(V.tensor_scalar(smax[:, 2, :, :], sk, 1 / SCALE, None, ALU.mult))
                        L(V.tensor_tensor(smax[:, 0, :, :], smax[:, 0, :, :], smax[:, 2, :, :], ALU.max))
                        L(V.tensor_scalar(smax[:, 0, :, :], smax[:, 0, :, :], -SCALE, None, ALU.mult))
                        V.tensor_tensor(smax[:, 2, :, :], smax[:, 0, :, :], sk, ALU.add).then_inc(s("max"), 1)
                    else:
                        V.tensor_scalar(smax[:, 0, :, :], smax[:, 0, :, :], -SCALE, None,
                                        ALU.mult).then_inc(s("max"), 1)
                    dve.wait_ge(*after("exp", l, q + 1))
                    if l == 0:
                        L(V.tensor_tensor(smax[:, 1, :, :], smax[:, 1, :, :], smax[:, 2, :, :], ALU.add))
                    L(V.reciprocal(smax[:, 1, :, :], smax[:, 1, :, :]))
                    V.tensor_tensor(sc[:, :, 0:P], sc[:, :, 0:P], spread(smax[:, 1, :, 0], 2, P), ALU.mult)
                    V.tensor_tensor(sc[:, :, P:TRI], sc[:, :, P:TRI], spread(smax[:, 1, :, 1], 2, 2 * P),
                                    ALU.mult).then_inc(s("p_ready"), 1)
                for t in range(TILES):
                    dve.wait_ge(*after("w_out_mult", l, t + 1))
                    y = ps[:, 2 * t:2 * t + 2, :]
                    L(V.tensor_tensor(yg[:, t, :], y.rearrange("p a n -> p (a n)"), mod[:, 2, :], ALU.mult))
                    V.tensor_tensor(xs[:, t, :], xs[:, t, :], yg[:, t, :], ALU.add).then_inc(s("mixed"), 1)
                norm(g_ffn, "g_ffn", 4, 3, yg, add_ffn, s("ffn_norm"), "ffn_rms")
                V.tensor_copy(stat[:, 0:1], stat[:, 0:1]).then_inc(s("x_read"), 1)
                for t in range(TILES):
                    for half_ in range(2):
                        dve.wait_ge(*after("ffn_hi", l, 2 * t + half_ + 1))
                        V.tensor_tensor(hT_lo[:, 4 * half_:4 * half_ + 4, P * t:P * t + P],
                                        ps[:, 6 + half_, :].rearrange("p (c t) -> p c t", c=4),
                                        hT_hi[:, 4 * half_:4 * half_ + 4, P * t:P * t + P],
                                        ALU.subtract).then_inc(s("ffn_lo"), 1)
                dve.wait_ge(*after("S_out", l, 8))
                dve.wait_ge(*after("x_kept", l, 32))
                dve.sem_inc(s("u_turned"), RING)
                with dve.Fori(0, NKEYS // U_STEP) as it:
                    def turn(b):
                        dve.wait_ge(*after(f"u_in{b % RING}", l, it * (U_STEP // RING * 64) + 64 * (b // RING + 1)))
                        dve.wait_ge(*after("u_lo", l, it * U_STEP + (b + 1)))
                        V.transpose(uT[b % 4][:, :], ring[b % RING][:, :]).then_inc(s("u_turned"), 1)

                    rs = s("route_step")
                    n_ = [0]

                    def R(ins):
                        n_[0] += 1
                        ins.then_inc(rs, 1)
                        dve.wait_ge(rs, n_[0])

                    def top16(src, spare, vals, idx):
                        R(V.max(vals[:, 0:8], src))
                        V.max_index(idx[:, 0:8], vals[:, 0:8], src)
                        R(V.match_replace(spare, vals[:, 0:8], src, -3e38))
                        R(V.max(vals[:, 8:16], spare))
                        R(V.max_index(idx[:, 8:16], vals[:, 8:16], spare))

                    R(V.tensor_copy(fix[:, :, :], S[:, bass.ds(it, 1), :, :].rearrange("p a h n -> p (a h) n")))
                    turn(0)
                    top16(fix[:, 0, :], cut[:, 0:NKEYS], topv[:, 0, :], topi[:, 0, :])
                    turn(1)
                    top16(fix[:, 1, :], cut[:, 0:NKEYS], topv[:, 1, :], topi[:, 1, :])
                    turn(2)
                    R(V.tensor_tensor(cand[:, :, :], spread(topv[:, 0, :], 2, TOPK), spread(topv[:, 1, :], 1, TOPK),
                                      ALU.add))
                    flat = cand[:, :, :].rearrange("p a b -> p (a b)")
                    top16(flat, cut[:, :], topv[:, 2, :], topi[:, 2, :])
                    turn(3)
                    V.tensor_copy(topf[:, 0:2, :], topi[:, 0:2, :])
                    R(V.tensor_scalar(topb[:, :], topi[:, 2, :], 4, None, ALU.logical_shift_right))
                    R(V.tensor_copy(topf[:, 2, :], topb[:, :]))
                    pick(R, 0, routes[:, 0, bass.ds(it * TOPK, TOPK)])
                    turn(4)
                    R(V.tensor_scalar(topb[:, :], topi[:, 2, :], 15, None, ALU.bitwise_and))
                    R(V.tensor_copy(topf[:, 2, :], topb[:, :]))
                    pick(R, 1, routes[:, 1, bass.ds(it * TOPK, TOPK)])
                    turn(5)
                    R(V.tensor_copy(routes[:, 2, bass.ds(it * TOPK, TOPK)], topv[:, 2, :]))
                    turn(6)
                    turn(7)
                    dve.sem_clear(rs)
                gt = routes[:, 2, :].rearrange("p (n k) -> p n k", k=TOPK)
                gs = cut[:, 0:T].rearrange("p (n k) -> p n k", k=TOPK)
                L(V.tensor_tensor(gs, gt, spread(gt[:, :, 0], 2, TOPK), ALU.subtract))
                V.tensor_copy(cand[:, 0, :], gs[:, :, 0]).then_inc(s("gate_in"), 1)
                dve.wait_ge(*after("gate_exp", l, 1))
                L(V.tensor_reduce(topf[:, 0, :], gs, AX, ALU.add))
                L(V.reciprocal(topf[:, 1, :], topf[:, 0, :]))
                V.tensor_tensor(gt, gs, spread(topf[:, 1, :], 2, TOPK), ALU.mult).then_inc(s("routed"), 1)
                dve.wait_ge(*after("routes_T", l, 1))
                dve.sem_inc(s("gated"), 4)
                dve.sem_inc(s("hot_dve"), 4)
                with dve.Fori(0, T // 16) as it:
                    dve.wait_ge(*after("hot_dve", l, it * 4 + 4))
                    dve.sem_inc(s("dve_held"), 1)
                    V.tensor_copy(cols["dve"][:, :, :], routes_T[:, 1:3, bass.ds(it * 16, 16)]
                                  ).then_inc(s("cols_dve"), 1)
                    dve.wait_ge(*after("cols_dve", l, it + 1))

                    def rows(b):
                        dve.wait_ge(*after("gate_mult", l, it * 4 + (b + 1)))
                        c = cols["dve"][:, :, 4 * b:4 * b + 1]
                        V.tensor_scalar(one_2[:, b, 0, :], iota[:, :], c[:, 0, :], c[:, 1, :], ALU.is_equal, ALU.mult)
                        V.tensor_tensor(one_1[:, b, :, :], spread(iota[:, :], 1, 4),
                                        spread(routes_T[:, 0, bass.ds(it * 16 + 4 * b, 4)], 2, NKEYS),
                                        ALU.is_equal).then_inc(s("hot_dve"), 1)

                    def times(b):
                        dve.wait_ge(*after("gate_mult", l, it * 4 + (b + 5)))
                        w = W[:, :, bass.ds(it * 16 + 4 * b, 4)].rearrange("p j t -> p t j")
                        V.tensor_tensor(w, w, ps[:, b, :].rearrange("p (t j) -> p t j", t=4),
                                        ALU.mult).then_inc(s("gated"), 1)

                    rows(0)
                    rows(1)
                    rows(2)
                    times(0)
                    rows(3)
                    times(1)
                    times(2)
                    times(3)
                dve.wait_ge(*after("gated", l, T // 4 + 4))
                V.memset(zeros[:, :].bitcast(F32), 0.0).then_inc(s("zeros"), 1)
                dve.sem_inc(s("v_lo"), RING)
                with dve.Fori(0, NKEYS // V_STEP) as it:
                    for b in range(V_STEP):
                        dve.wait_ge(*after("v_hi", l, it * V_STEP + (b + 1)))
                        V.tensor_tensor(w_lo[b][:, :],
                                        W[:, bass.ds(it * V_STEP + b, 1), :].rearrange("p a t -> p (a t)"),
                                        w_hi[b][:, :], ALU.subtract)
                        dve.wait_ge(*after("v_mult", l, it * V_STEP + (b + 3)))
                        V.tensor_tensor(lo[b % 2][:, :], ring[b % RING][:, :], hi[b][:, :],
                                        ALU.subtract).then_inc(s("v_lo"), 1)
                dve.wait_ge(*after("v_all", l, 1))
                dve.wait_ge(*after("x_back", l, 32))
                for t in range(TILES):
                    L(V.tensor_tensor(yg[:, t, :], ps[:, 4 + 2 * t:6 + 2 * t, :].rearrange("p a n -> p (a n)"),
                                      gate_b[:, :], ALU.mult))
                    L(V.tensor_tensor(xs[:, t, :], x_back[:, t, :], yg[:, t, :], ALU.add))
                V.tensor_copy(stat[:, 0:1], xs[:, 0, 0:1]).then_inc(layer_done, 1)

        @block.scalar
        def _(act):
            A = nc.scalar.activation
            L = lambda ins: link(act, "act", ins)

            act.wait_ge(x_in, 16)
            for l in range(LAYERS):
                if l:
                    act.wait_ge(layer_done, l)
                act.wait_ge(*after("c_in", l, 16))
                A(cond[:, 1, :], cond[:, 0, :], ACT.Exp, scale=-1.0).then_inc(s("c_exp"), 1)
                for n in range(12):
                    act.wait_ge(*after("ada_sum", l, n + 1))
                    A(mod[:, n // 2, 512 * (n % 2):512 * (n % 2) + 512], ps[:, n % 2, :], ACT.Copy,
                      scale=-1.0).then_inc(s("ada_done"), 1)

                def rms(dst, done):
                    for t in range(TILES):
                        L(A(dst[:, t, :], xs[:, t, :], ACT.Square, accum_out=stat[:, t:t + 1]))
                    L(A(stat[:, 2:4], stat[:, 0:2], ACT.Copy, scale=1.0 / D, bias=EPS))
                    A(stat[:, 2:4], stat[:, 2:4], ACT.Sqrt).then_inc(done, 1)

                act.wait_ge(*after("ada_done", l, 12))
                rms(h, s("mix_rms"))
                for n in range(4):
                    act.wait_ge(*after("mix_T", l, n + 1))
                    t, half = n // 2, n % 2
                    A(hT[:, 4 * half:4 * half + 4, P * t:P * t + P], ps[:, 2 + n, :].rearrange("p (c t) -> p c t", c=4),
                      ACT.Copy).then_inc(s("hT"), 1)
                g = 0
                for n, (a, m) in enumerate(SETS[l]):
                    for t in range(2):
                        act.wait_ge(*after("proj", l, g + 1))
                        if n < TOKEN_SETS[l]:
                            A(tok[n][:, t, 0:m], ps[:, g % 8, 0:m], ACT.Copy).then_inc(s("proj_out"), 1)
                        else:
                            A(qk_T[n - 1][:, 2 * t:2 * t + 2, :], ps[:, g % 8, :].rearrange("p (a t) -> p a t", a=2),
                              ACT.Copy, scale=SCALE if n == 3 else 1.0).then_inc(s("proj_out"), 1)
                        g += 1
                act.wait_ge(*after("ssq", l, 1))
                cnt = 20 if l == 0 else 64
                L(A(ssq[:, 1, 0:cnt], ssq[:, 0, 0:cnt], ACT.Copy, scale=1.0 / HD, bias=EPS))
                A(ssq[:, 1, 0:cnt], ssq[:, 1, 0:cnt], ACT.Sqrt).then_inc(s("qk_rms"), 1)
                for n, (_, _, heads, _) in enumerate(NORMS[l]):
                    for t in range(TILES):
                        act.wait_ge(*after("qk_turned", l, 2 * n + t + 1))
                        w = heads * HD // P if heads == 8 else 2
                        A(qk_T[n][:, 0:w, P * t:P * t + P],
                          ps[:, (2 * n + t) % 4, 0:P * w].rearrange("p (a t) -> p a t", a=w),
                          ACT.Copy).then_inc(s("qk_T"), 1)
                for q in range(4):
                    if l == 0 and q >= 2:
                        act.wait_ge(*after("scores", l, q + 1))
                        L(A(e_abs[:, :, :], ps[:, 0:4, 0:TRI], ACT.Abs))
                        L(A(e_abs[:, :, :], e_abs[:, :, :], ACT.Exp, scale=-1.0))
                        A(e_abs[:, :, :], e_abs[:, :, :], ACT.Ln, bias=1.0).then_inc(s("ln_done"), 1)
                        act.wait_ge(*after("log_w", l, q - 1))
                        A(pT[:, :, :], pT[:, :, :], ACT.Exp).then_inc(s("pT"), 1)
                    else:
                        act.wait_ge(*after("max", l, q + 1))
                        if l == 0:
                            A(smax[:, 2, :, :], smax[:, 2, :, :], ACT.Exp)
                        for i in range(4):
                            A(sc[:, i, 0:P], sc[:, i, 0:P], ACT.Exp, bias=smax[:, 0, i, 0:1], scale=SCALE,
                              accum_out=smax[:, 1, i, 0:1])
                            last = A(sc[:, i, P:TRI], sc[:, i, P:TRI], ACT.Exp, bias=smax[:, 0, i, 1:2], scale=SCALE,
                                     accum_out=smax[:, 1, i, 1:2])
                        last.then_inc(s("exp"), 1)
                        act.wait_ge(*after("p_turned", l, q + 1))
                        if q:
                            act.wait_ge(*after("y", l, q))
                        A(pT[:, :, :], ps[:, 4:8, 0:TRI], ACT.Copy).then_inc(s("pT"), 1)
                    act.wait_ge(*after("y", l, q + 1))
                    A(yT[:, 2 * q:2 * q + 2, :], ps[:, 4:6, 0:T], ACT.Copy).then_inc(s("y_out"), 1)
                act.wait_ge(*after("subk_turned", l, 1))
                A(subk_T[:, :, :], ps[:, 4, 0:2 * P].rearrange("p (a n) -> p a n", a=2), ACT.Copy
                  ).then_inc(s("subk_T"), 1)
                act.wait_ge(*after("mixed", l, TILES))
                rms(hf, s("ffn_rms"))
                for n in range(4):
                    act.wait_ge(*after("ffn_T", l, n + 1))
                    t, half = n // 2, n % 2
                    src = ps[:, 6 + half, :].rearrange("p (c t) -> p c t", c=4)
                    A(hTf[:, 4 * half:4 * half + 4, P * t:P * t + P], src, ACT.Copy)
                    A(hT_hi[:, 4 * half:4 * half + 4, P * t:P * t + P], src, ACT.Copy).then_inc(s("ffn_hi"), 1)
                for g in range(PHEADS):
                    act.wait_ge(*after("qry", l, g + 1))
                    A(qryT[:, 2 * g:2 * g + 2, :], ps[:, g % 4, :].rearrange("p (a t) -> p a t", a=2),
                      ACT.Copy).then_inc(s("qry_out"), 1)
                for n in range(8):
                    act.wait_ge(*after("S_mult", l, n + 1))
                    A(S[:, 2 * n:2 * n + 2, :, :], ps[:, 4 + n % 4, :].rearrange("p (a h n) -> p a h n", a=2, h=2),
                      ACT.Copy).then_inc(s("S_out"), 1)
                act.wait_ge(*after("x_kept", l, 32))
                act.sem_inc(s("u_gelu"), 4)

                def u_hi(it, b):
                    act.wait_ge(*after("u_turned", l, it * U_STEP + (b + 1 + RING)))
                    act.wait_ge(*after("u_mult", l, it * U_STEP + (b + 1)))
                    A(hi[b % 4][:, :].rearrange("p (c g i) -> p c g i", c=KC, g=4),
                      uT[b % 4][:, :].rearrange("p (g c i) -> p c g i", g=4, c=KC), ACT.Copy
                      ).then_inc(s("u_hi"), 1)

                def gelu(it, pair):
                    act.wait_ge(*after("u_mult", l, it * U_STEP + (2 * pair + 6)))
                    act.sem_inc(s("act_held"), 1)
                    A(W[:, bass.ds(it * U_STEP + 2 * pair, 2), :],
                      ps[:, pair, :].rearrange("p (a t) -> p a t", a=2), ACT.Gelu).then_inc(s("u_gelu"), 1)

                def turn(it, last):
                    for b in range(3, U_STEP + 3):
                        if b < U_STEP or not last:
                            u_hi(it, b)
                        if b % 2:
                            gelu(it, b // 2 - 1)

                for b in range(3):
                    u_hi(0, b)
                with act.Fori(0, NKEYS // U_STEP - 1) as it:
                    turn(it, False)
                turn(NKEYS // U_STEP - 1, True)
                act.wait_ge(*after("gate_in", l, 1))
                A(cut[:, 0:T], cut[:, 0:T], ACT.Exp).then_inc(s("gate_exp"), 1)
                act.wait_ge(*after("routes_turned", l, 1))
                A(routes_T[:, :, :], ps[:, 4:7, 0:T], ACT.Copy).then_inc(s("routes_T"), 1)
                act.wait_ge(*after("routes_T", l, 1))
                act.sem_inc(s("hot_act"), 4)
                with act.Fori(0, T // 16) as it:
                    act.wait_ge(*after("hot_act", l, it * 4 + 4))
                    act.sem_inc(s("act_held"), 1)
                    A(cols["act"][:, 0, :], routes_T[:, 1, bass.ds(it * 16, 16)], ACT.Copy, scale=-1.0)
                    A(cols["act"][:, 1, :], routes_T[:, 2, bass.ds(it * 16, 16)], ACT.Copy).then_inc(s("cols_act"), 1)
                    act.wait_ge(*after("cols_act", l, it + 1))
                    for b in range(4):
                        last = A(gap[:, b, :], iota[:, :], ACT.Abs, bias=cols["act"][:, 0, 4 * b + 1:4 * b + 2])
                    last.then_inc(s("gap"), 1)
                    for b in range(4):
                        c = cols["act"][:, 1, 4 * b + 1:4 * b + 2]
                        act.wait_ge(*after("gate_mult", l, it * 4 + (b + 1)))
                        act.sem_inc(s("act_held"), 1)
                        act.wait_ge(*after("gap", l, it + 1))
                        A(one_2[:, b, 1, :], gap[:, b, :], ACT.Relu, bias=c, scale=-BIG).then_inc(s("hot_act"), 1)
                act.wait_ge(*after("gated", l, T // 4 + 4))
                with act.Fori(0, NKEYS // V_STEP) as it:
                    for b in range(V_STEP):
                        act.wait_ge(*after("v_mult", l, it * V_STEP + (b + 1)))
                        act.sem_inc(s("act_held"), 1)
                        A(w_hi[b][:, :], W[:, bass.ds(it * V_STEP + b, 1), :].rearrange("p a t -> p (a t)"),
                          ACT.Copy)
                        act.wait_ge(*after(f"v_in{b % RING}", l, it * 16 + 16))
                        A(hi[b][:, :], ring[b % RING][:, :], ACT.Copy).then_inc(s("v_hi"), 1)

        @block.gpsimd
        def _(pool):
            for l in range(LAYERS):
                if l:
                    pool.wait_ge(layer_done, l)
                pool.wait_ge(*after("x_kept", l, 32))
                pool.sem_inc(s("u_lo"), 4)
                with pool.Fori(0, NKEYS // U_STEP) as it:
                    for b in range(U_STEP):
                        pool.wait_ge(*after("u_mult", l, it * U_STEP + (b + 3)))
                        pool.wait_ge(*after("u_hi", l, it * U_STEP + (b + 1)))
                        nc.gpsimd.tensor_tensor(
                            lo[b % 2][:, :].rearrange("p (c g i) -> p c g i", c=KC, g=4),
                            uT[b % 4][:, :].rearrange("p (g c i) -> p c g i", g=4, c=KC),
                            hi[b % 4][:, :].rearrange("p (c g i) -> p c g i", c=KC, g=4),
                            ALU.subtract).then_inc(s("u_lo"), 1)
                pool.wait_ge(*after("routes_T", l, 1))
                pool.sem_inc(s("hot_pool"), 4)
                with pool.Fori(0, T // 16) as it:
                    pool.wait_ge(*after("hot_pool", l, it * 4 + 4))
                    pool.sem_inc(s("pool_held"), 1)
                    nc.gpsimd.tensor_copy(cols["pool"][:, :, :], routes_T[:, 1:3, bass.ds(it * 16, 16)]
                                          ).then_inc(s("cols_pool"), 1)
                    pool.wait_ge(*after("cols_pool", l, it + 1))
                    pool.sem_inc(s("pool_held"), 1)
                    for b in range(4):
                        pool.wait_ge(*after("gate_mult", l, it * 4 + (b + 1)))
                        pool.sem_inc(s("pool_held"), 1)
                        for k in range(2, 4):
                            c = cols["pool"][:, :, 4 * b + k:4 * b + k + 1]
                            last = nc.gpsimd.tensor_scalar(one_2[:, b, k, :], iota[:, :], c[:, 0, :], c[:, 1, :],
                                                           ALU.is_equal, ALU.mult)
                        last.then_inc(s("hot_pool"), 1)


_INS = ['x', 'c', 'ada_w', 'ada_b', 'norm_mix_g', 'norm_ffn_g', 'w_in_ab', 'w_out_ab', 'sinks_a', 'qnorm_a',
        'knorm_a', 'w_in_cd', 'w_out_cd', 'qnorm_c', 'knorm_c', 'qnorm_d', 'knorm_d', 'peer_wq',
        'peer_subkeys', 'peer_u', 'peer_v']


def kernel(**inputs):
    import concourse.bacc as _bacc
    from concourse.bass_utils import run_bass_kernel_spmd as _run

    nc = _bacc.Bacc("TRN2", target_bir_lowering=False, num_devices=1)
    arrays, args = {}, []
    for name in _INS:
        a = np.ascontiguousarray(inputs[name])
        arrays[f"in_{name}"] = a
        args.append(nc.dram_tensor(f"in_{name}", a.shape, mybir.dt.from_np(a.dtype), kind="ExternalInput").ap())
    arrays["const"] = constants()
    args.append(nc.dram_tensor("const", (P, CONST_N), F32, kind="ExternalInput").ap())
    args.append(nc.dram_tensor("out", (1, T, D), F32, kind="ExternalOutput").ap())
    trunk_kernel(nc, *args)
    r = _run(nc, [arrays], core_ids=[0])
    return r.results[0]["out"]
```

```python
import numpy as np
from contextlib import ExitStack

import concourse.bass as bass
from concourse import mybir

F32 = mybir.dt.float32
F32R = mybir.dt.float32r
U32 = mybir.dt.uint32
ALU = mybir.AluOpType
ACT = mybir.ActivationFunctionType
AX = mybir.AxisListType.X

P = 128
T = 256
TILES = T // P
D = 1024
KC = D // P
HD = 64
NH = 8
LAYERS = 2
EPS = 1e-6
BIG = 1e30
SCALE = HD ** -0.5
TRI = 3 * P

NKEYS = 128
PHEADS = 8
TOPK = 16
NE = NKEYS * NKEYS
ROUTES = PHEADS * TOPK

U_STEP = 8
V_STEP = 4
V_PLAIN = 32
RING = 4

CONST = {}
_at = 0
for _name, _n in (("ident", P), ("iota", P), ("mask_a", TRI), ("mask_c", TRI), ("mask_d", TRI),
                  ("past", TRI), ("not_past", TRI), ("neg_tri", P), ("neg_ones", P),
                  ("cos", 2 * HD), ("sin", 2 * HD)):
    CONST[_name] = (_at, _at + _n)
    _at += _n
CONST_N = _at


def constants():
    c = np.zeros((P, CONST_N), np.float32)

    def put(name, a):
        c[:, CONST[name][0]:CONST[name][1]] = a

    i = np.arange(P)
    put("ident", np.eye(P))
    put("iota", np.broadcast_to(i, (P, P)))
    dist = np.concatenate([i[:, None] - i[None], P + i[:, None] - i[None], i[:, None] - i[None]], 1)
    put("mask_a", np.where((dist >= 0) & (dist <= P - 1), 0.0, -BIG))
    put("mask_d", np.where(dist >= 0, 0.0, -BIG))
    seen = sum(((dist >= 0) & (dist % r == 0) & (dist <= w)).astype(int)
               for w, r in ((128, 1), (512, 4), (2048, 16)))
    put("mask_c", np.where(seen > 0, np.log(np.maximum(seen, 1)) / SCALE, -BIG))
    gap = np.concatenate([i[None] - i[:, None], P + i[None] - i[:, None], i[None] - i[:, None]], 1)
    put("past", gap > 0)
    put("not_past", np.where(gap > 0, 0.0, -BIG))
    put("neg_tri", -(i[:, None] >= i[None]).astype(np.float32))
    put("neg_ones", -1.0)
    half = HD // 2
    inv = np.float32(10000.0) ** (-np.arange(half, dtype=np.float32) / np.float32(half))
    ang = np.arange(T, dtype=np.float32)[:, None] * inv[None].astype(np.float32)
    cos, sin = np.cos(ang), np.sin(ang)
    for t in range(TILES):
        a, s = cos[t * P:(t + 1) * P], sin[t * P:(t + 1) * P]
        c0, s0 = CONST["cos"][0] + t * HD, CONST["sin"][0] + t * HD
        c[:, c0:c0 + HD] = np.concatenate([a, a], 1)
        c[:, s0:s0 + HD] = np.concatenate([-s, s], 1)
    return c


def spread(a, axis, n):
    a = a.unsqueeze(axis)
    shape = list(a.shape)
    shape[axis] = n
    return a.to_broadcast(shape)


def trunk_kernel(nc, x, c, ada_w, ada_b, norm_mix_g, norm_ffn_g, w_in_ab, w_out_ab, sinks_a, qnorm_a,
                 knorm_a, w_in_cd, w_out_cd, qnorm_c, knorm_c, qnorm_d, knorm_d, peer_wq, peer_subkeys,
                 peer_u, peer_v, const, out):
    ctx = ExitStack()
    with ctx:
        base = (nc.sbuf_base + 31) // 32 * 32
        KB = 1024

        def at(name, kb, shape, dt=F32):
            return nc.alloc_sbuf_tensor_at(name, [P] + shape, dt, offset=base + int(kb * KB))

        W = at("W", 0, [NKEYS, T])
        w_in_ab_sb = [at(f"w_in_ab_sb{n}", kb, [KC, m])
                      for n, (kb, m) in enumerate(((0, 512), (16, 256), (24, 512), (40, 512), (56, 512)))]
        w_in_cd_sb = [at(f"w_in_cd_sb{n}", 32 + 16 * n, [KC, 512]) for n in range(6)]
        w_out = at("w_out", 96, [KC, D])
        qk_T = [at(f"qk_T{n}", 64 + 4 * n, [4, T]) for n in range(4)]
        turned = [at(f"turned{n}", 4 * n, [TILES, 512]) for n in range(3)]
        rope_c = at("rope_c", 12, [4, 2 * HD])
        rope_s = at("rope_s", 14, [4, 2 * HD])
        sc = [at(f"sc{n}", 16 + 6 * n, [4, TRI]) for n in range(2)]
        pT = at("pT", 28, [4, TRI])
        e_abs = at("e_abs", 34, [4, TRI])
        wq = at("wq", 0, [KC, 2048])
        wq_hi = [at(f"wq_hi{n}", 96 + 8 * n, [KC, 2 * P], F32R) for n in range(2)]
        wq_lo = [at(f"wq_lo{n}", 112 + 8 * n, [KC, 2 * P], F32R) for n in range(2)]
        hf = at("hf", 72, [TILES, D])
        qryT = at("qryT", 80, [2 * PHEADS, T])

        xs = at("xs", 128, [TILES, D])
        mod = at("mod", 136, [6, D])
        cst = at("cst", 160, [CONST_N])
        hT = at("hT", 172, [KC, T])
        yT = at("yT", 172, [KC, T])
        ada = [at(f"ada{n}", kb, [KC, 512]) for n, kb in enumerate((172, 96, 112))]
        acc_a = at("acc_a", 192, [4, 512])
        acc_b = at("acc_b", 80, [8, 512])
        acc_1 = at("acc_1", 8, [12, 512])
        ada_1 = [at(f"ada_1_{n}", kb, [2048]) for n, kb in enumerate((0, 160))]
        h = at("h", 180, [TILES, D])
        g_mix = at("g_mix", 188, [D])
        g_ffn = at("g_ffn", 136, [D])
        tok = [at(f"tok{n}", 180 + 4 * n if n < 5 else 140, [TILES, 512]) for n in range(6)]

        hi = [at(f"hi{n}", kb, [D], F32R) for n, kb in enumerate((128, 192, 136, 140))]
        lo = [at(f"lo{n}", kb, [D], F32R) for n, kb in enumerate((132, 196))]
        S = at("S", 112, [TILES * PHEADS, 2, NKEYS])
        uT = [at(f"uT{n}", kb, [D]) for n, kb in enumerate((152, 188, 144, 148))]
        ring = [at("ring0", 156, [D])] + [at(f"ring{n}", 172 + 4 * n, [D]) for n in range(1, RING)]
        hT_hi = at("hT_hi", 160, [KC, T], F32R)
        hT_lo = at("hT_lo", 168, [KC, T], F32R)
        w_hi = [at(f"w_hi{n}", 144 + n, [T], F32R) for n in range(4)]
        w_lo = [at(f"w_lo{n}", 148 + n, [T], F32R) for n in range(4)]
        zeros = at("zeros", 152, [512], F32R)
        one_1 = at("one_1", 140, [4, 4, NKEYS])
        one_2 = at("one_2", 176, [4, 4, NKEYS])
        routes_T = at("routes_T", 136, [3, T])
        cols = {e: at(f"cols_{e}", 139 + 0.25 * n, [2, 16]) for n, e in enumerate(("dve", "act", "pool"))}
        gap = at("gap", 148, [4, 2, NKEYS])
        x_back = at("x_back", 64, [TILES, D])
        gate_b = at("gate_b", 72, [D])
        yg = at("yg", 180, [TILES, D])

        ident = at("ident", 200, [P])
        iota = at("iota", 200.5, [P])
        routes = at("routes", 201, [3, T])
        subk = at("subk", 201, [2, P])
        subk_T = at("subk_T", 202, [2, P])
        cond = at("cond", 203, [4, KC])
        silu = at("silu", 207.6875, [KC])
        gains = at("gains", 204, [4, HD])
        stat = at("stat", 207.625, [8])
        ssq = at("ssq", 205.125, [2, 64])
        sink = at("sink", 205.75, [8])
        smax = [at(f"smax{n}", 206 + n / 8, [3, 4, 2]) for n in range(2)]
        fix = at("fix", 204, [2, NKEYS])
        cut = at("cut", 205, [TOPK * TOPK])
        cand = at("cand", 206, [TOPK, TOPK])
        topv = at("topv", 207, [3, TOPK])
        topi = at("topi", 207.1875, [3, TOPK], U32)
        topf = at("topf", 207.375, [3, TOPK])
        topb = at("topb", 207.5625, [TOPK], U32)

        ps = ctx.enter_context(nc.psum_tensor("ps", [P, 8, 512], F32))

        x_keep = nc.dram_tensor("x_keep", [TILES, P, D], F32, kind="Internal").ap()
        gate_keep = nc.dram_tensor("gate_keep", [1, D], F32, kind="Internal").ap()

        def sem(name):
            return ctx.enter_context(nc.semaphore(name))

        def k_(name):
            a, b = CONST[name]
            return cst[:, a:b]

        cst_in, x_in, out_sem = sem("tables_in"), sem("x_in"), sem("out_done")
        layer_done = sem("layer_done")
        COUNTS = dict(
            c_in=16, ada_b=32, ada_1_b0=16, ada_1_b1=16, ada_1_b2=16, cst_in=16, ada_in0=32, ada_in1=80, ada_in2=80, ada_1_in0=192, ada_1_in1=192, w_in0=16, w_in1=16, w_in2=16,
            w_in3=16, w_in4=16, w_in5=0, w_out=16, g_mix=16, gains=48, g_ffn=16, subk=16, wq=64, x_kept=32,
            x_back=32, **{f"u_in{n}": NKEYS // RING * 64 for n in range(RING)},
            **{f"v_in{n}": NKEYS // RING * 16 for n in range(RING)},
            ada_sum=12, mix_T=4, proj=10, qk_turned=4, scores=4, p_turned=4, y=4, w_out_mult=2, subk_turned=1,
            ffn_T=4, qry=8, S_mult=8, u_mult=NKEYS + 4, routes_turned=1, gate_mult=T // 4 + 4,
            v_mult=NKEYS + 4, v_all=1,
            acc_zero=1, ada_1_used=3 * KC + 2, ada_used=12, mix_norm=2, ssq=1, roped=2, masked=4, p_ready=2, softplus=2, log_w=2, max=2, mixed=2, ffn_norm=2,
            x_read=1, ffn_lo=4, wq_lo=6, u_turned=NKEYS + RING, route_step=0, gate_in=1, routed=1, gated=T // 4 + 4,
            hot_dve=T // 4 + 4, cols_dve=T // 16, dve_held=0, zeros=1, v_lo=NKEYS + RING,
            c_exp=1, ada_done=12, mix_rms=1, hT=4, proj_out=10, qk_rms=1, qk_T=4, ln_done=2, pT=4, exp=2, y_out=4,
            subk_T=1, ffn_rms=1, ffn_hi=4, wq_hi=8, qry_out=8, S_out=8, u_gelu=NKEYS // 2 + 4, u_hi=NKEYS, act_held=0,
            hot_act=T // 4 + 4, cols_act=T // 16, gap=T // 16, gate_exp=1, routes_T=1, v_hi=NKEYS,
            acc_1_zero=3, wq_lo_pool=2,
            u_lo=NKEYS + 4, hot_pool=T // 4 + 4, cols_pool=T // 16, pool_held=0)
        SEMS = {n: sem(n) for n in COUNTS}

        def w_in(l, n):
            return (w_in_cd_sb if l else w_in_ab_sb)[n][:, :, :]

        def acc(l, n):
            return acc_1[:, n, :] if l else acc_a[:, n, :] if n < 4 else acc_b[:, n - 4, :]

        def ada_bank(l, n):
            return 4 + n % 4 if l == 0 and n >= 4 else n % 4

        def ada_buf(n):
            buf = [n % 3 if n < 4 else 1 + n % 2 for n in range(12)]
            before = [m for m in range(n) if buf[m] == buf[n]]
            return buf[n], len(before), before[-1] if before else None

        def s(name):
            return SEMS[name]

        def after(name, l, count):
            return SEMS[name], count + COUNTS[name] * l if l else count

        chain = {n: sem(f"{n}_step") for n in ("dve", "act", "pool")}
        steps = {n: 0 for n in chain}

        def link(eng, name, ins):
            steps[name] += 1
            ins.then_inc(chain[name], 1)
            eng.wait_ge(chain[name], steps[name])

        block = ctx.enter_context(nc.Block())

        w_in_l = [w_in_ab[0], w_in_cd[0]]
        w_out_l = [w_out_ab[0], w_out_cd[0]]
        SETS = [[(0, 512), (512, 256), (1792, 512), (768, 512), (1280, 512)],
                [(0, 512), (512, 512), (1536, 512), (2048, 512), (1024, 512), (2560, 512)]]
        TOKEN_SETS = [3, 6]
        GROUPS = [2 * TOKEN_SETS[0] + 4, 2 * TOKEN_SETS[1]]
        NORMS = [[(0, 0, 8, 0), (1, 0, 2, 1)],
                 [(0, 0, 8, 0), (1, 0, 8, 1), (2, 0, 8, 2), (3, 0, 8, 3)]]

        def perm(a):
            return a.rearrange("t (q c j) -> t c q j", q=4, c=KC)

        uv = peer_u.rearrange("l (g i j) (q d) -> l q j i g d", g=4, i=32, q=4)
        vv = peer_v.rearrange("l (i j) d -> l j i d", j=NKEYS)


        QT = [[(qk_T[0], qk_T[1]), (qk_T[2], qk_T[3])]] * 2

        def v_at(l, q, i):
            if l == 0:
                return (1, P + HD * q) if q < 2 else (2, HD * (4 * (q - 2) + i))
            return (4 if q < 2 else 5, HD * (4 * (q % 2) + i))

        def pick(R, half, dst):
            eq = cand[:, :, :]
            R(nc.vector.tensor_tensor(eq, spread(topf[:, 2, :], 2, TOPK), spread(iota[:, 0:TOPK], 1, TOPK),
                                      ALU.is_equal))
            R(nc.vector.tensor_tensor(eq, eq, spread(topf[:, half, :], 1, TOPK), ALU.mult))
            R(nc.vector.tensor_reduce(dst, eq, AX, ALU.add))

        @block.sync
        def _(sp):
            sp.dma_start(cond[:, 0, :], c.rearrange("a (p c) -> p (a c)", c=KC)).then_inc(s("c_in"), 16)

            def load_ada(n):
                buf, _, last = ada_buf(n)
                if last is not None:
                    sp.wait_ge(*after("ada_used", 0, last + 1))
                sp.dma_start(ada[buf][:, :, :],
                             ada_w[0].rearrange("(p c) n -> p c n", c=KC)[:, :, 512 * n:512 * n + 512]
                             ).then_inc(s(f"ada_in{buf}"), 16)

            load_ada(0)
            load_ada(1)
            sp.dma_start(ident[:, :], const[:, 0:P]).then_inc(cst_in, 16)
            sp.dma_start(iota[:, :], const[:, P:2 * P]).then_inc(cst_in, 16)
            sp.dma_start(xs[:, :, :], x.rearrange("a (t p) d -> p (a t) d", p=P)).then_inc(x_in, 16)
            load_ada(2)
            sp.wait_ge(*after("acc_zero", 0, 1))
            sp.dma_start(acc_a[0:1, :, :], ada_b[0:1, 0:2048].rearrange("a (m d) -> a m d", m=4)
                         ).then_inc(s("ada_b"), 16)
            sp.dma_start(acc_b[0:1, :, :], ada_b[0:1, 2048:6144].rearrange("a (m d) -> a m d", m=8)
                         ).then_inc(s("ada_b"), 16)
            for l in range(LAYERS):
                def load_w_in(n, l=l):
                    a, m = SETS[l][n]
                    sp.dma_start(w_in(l, n), w_in_l[l].rearrange("(p c) n -> p c n", c=KC)[:, :, a:a + m]
                                 ).then_inc(s(f"w_in{n}"), 16)

                sp.dma_start(cst[:, :], const).then_inc(s("cst_in"), 16)
                sp.dma_start(g_mix[:, :], norm_mix_g[l:l + 1, :].to_broadcast([P, D])
                             ).then_inc(s("g_mix"), 16)
                names = [(qnorm_a, knorm_a, sinks_a), (qnorm_c, knorm_c, qnorm_d, knorm_d)][l]
                for n, g in enumerate(names):
                    dst = gains[:, n, :] if g is not sinks_a else sink[:, :]
                    sp.dma_start(dst, g[0:1, :].to_broadcast([P, g.shape[1]])).then_inc(s("gains"), 16)
                if l == 0:
                    load_ada(3)
                    for n in range(len(SETS[l])):
                        load_w_in(n)
                    for n in range(4, 12):
                        load_ada(n)
                    sp.wait_ge(*after("ada_used", 0, 12))
                else:
                    sp.wait_ge(layer_done, l)
                    for n in range(2, len(SETS[l])):
                        load_w_in(n)
                    sp.wait_ge(*after("proj", l, GROUPS[l]))
                sp.dma_start(w_out[:, :, :], w_out_l[l].rearrange("(c p) n -> p c n", p=P)
                             ).then_inc(s("w_out"), 16)
                sp.wait_ge(*after("mix_norm", l, TILES))
                sp.dma_start(g_ffn[:, :], norm_ffn_g[l:l + 1, :].to_broadcast([P, D])
                             ).then_inc(s("g_ffn"), 16)
                sp.dma_start(subk[:, :, :], peer_subkeys[l].rearrange("a n d -> n a d")
                             ).then_inc(s("subk"), 16)
                sp.wait_ge(*after("y", l, 4))
                for q in range(4):
                    sp.dma_start(wq[32 * q:32 * q + 32, :, :],
                                 peer_wq[l, 256 * q:256 * q + 256, :].rearrange("(c j) n -> j c n", j=32)
                                 ).then_inc(s("wq"), 16)
                sp.wait_ge(*after("mixed", l, TILES))
                sp.wait_ge(*after("ada_done", l, 12))
                sp.dma_start(x_keep.rearrange("t p d -> p t d"), xs[:, :, :]).then_inc(s("x_kept"), 16)
                sp.dma_start(gate_keep, mod[0:1, 5, :]).then_inc(s("x_kept"), 16)
                sp.wait_ge(*after("x_kept", l, 32))
                sp.wait_ge(*after("ffn_lo", l, 4))
                sp.wait_ge(*after("x_read", l, 1))
                with sp.Fori(0, NKEYS // U_STEP) as it:
                    for b in range(U_STEP):
                        sp.wait_ge(*after("u_turned", l, it * U_STEP + (b + 1)))
                        for q in range(4):
                            sp.dma_start(ring[b % RING][32 * q:32 * q + 32, :].rearrange("i (g d) -> i g d", g=4),
                                         uv[l, q, bass.ds(it * U_STEP + b, 1)].rearrange("a i g d -> (a i) g d")
                                         ).then_inc(s(f"u_in{b % RING}"), 16)
                sp.wait_ge(*after("gated", l, T // 4 + 4))

                def load_v(blk, b):
                    sp.wait_ge(*after("v_lo", l, blk + 1))
                    sp.dma_start(ring[b][:, :], vv[l, bass.ds(blk, 1)].rearrange("a i d -> (a i) d")
                                 ).then_inc(s(f"v_in{b}"), 16)

                with sp.Fori(0, (V_PLAIN if l == 0 else NKEYS) // V_STEP) as it:
                    for b in range(V_STEP):
                        load_v(it * V_STEP + b, b)
                if l == 0:
                    def load_bias(third):
                        sp.wait_ge(*after("acc_1_zero", 0, third + 1))
                        sp.dma_start(acc_1[0:1, 4 * third:4 * third + 4, :],
                                     ada_b[1:2, 2048 * third:2048 * third + 2048].rearrange("a (m d) -> a m d", m=4)
                                     ).then_inc(s(f"ada_1_b{third}"), 16)

                    load_bias(0)
                    load_bias(1)
                    for third in range(3):
                        if third == 1:
                            load_bias(2)
                        with sp.Fori(0, KC // 2) as it:
                            for b in range(2 * V_STEP):
                                if b % V_STEP == 0:
                                    r = b // V_STEP
                                    sp.wait_ge(*after("ada_1_used", 0, it * 2 + (KC * third + r + 1)))
                                    sp.dma_start(ada_1[r][:, :],
                                                 ada_w[1].rearrange("(p c) n -> c p n", c=KC)
                                                 [bass.ds(it * 2 + r, 1), :, 2048 * third:2048 * third + 2048]
                                                 .rearrange("a p n -> (a p) n")).then_inc(s(f"ada_1_in{r}"), 16)
                                load_v(it * 2 * V_STEP + (V_PLAIN + 2 * V_STEP * (KC // 2) * third + b), b % V_STEP)
                    for n in range(2):
                        load_w_in(n, 1)
                sp.dma_start(x_back[:, :, :], x_keep.rearrange("t p d -> p t d")).then_inc(s("x_back"), 16)
                sp.dma_start(gate_b[:, :], gate_keep.to_broadcast([P, D])).then_inc(s("x_back"), 16)
                sp.wait_ge(*after("v_all", l, 1))
            sp.wait_ge(layer_done, LAYERS)
            sp.dma_start(out.rearrange("a (t p) d -> p (a t) d", p=P), xs[:, :, :]).then_inc(out_sem, 16)
            sp.wait_ge(out_sem, 16)

        @block.tensor
        def _(pe):
            mm, tr = nc.tensor.matmul, nc.tensor.transpose
            pe.wait_ge(cst_in, 32)
            for l in range(LAYERS):
                pe.wait_ge(*after("cst_in", l, 16))

                def ada_sums(n0, n1):
                    for n in range(n0, n1):
                        if l == 0:
                            pe.wait_ge(*after("ada_used", 0, n + 1))
                        if n >= 4:
                            pe.wait_ge(*after("ada_done", l, n - 3))
                        mm(ps[:, ada_bank(l, n), :], k_("neg_ones"), acc(l, n), start=True, stop=True
                           ).then_inc(s("ada_sum"), 1)

                ada_sums(0, 12 if l else 4)
                hv = h[:, :, :].rearrange("p t (m c) -> p t c m", c=KC)
                for t in range(TILES):
                    pe.wait_ge(*after("mix_norm", l, t + 1))
                    for half in range(2):
                        for j in range(4):
                            last = tr(ps[:, 4 + 2 * t + half, P * j:P * j + P], hv[:, t, 4 * half + j, :], ident[:, :])
                        last.then_inc(s("mix_T"), 1)
                pe.wait_ge(*after("hT", l, 4))
                pe.wait_ge(*after("ada_done", l, 12 if l else 4))
                g = 0
                for n, (a, m) in enumerate(SETS[l]):
                    pe.wait_ge(*after(f"w_in{n}", l, 16))
                    for t in range(2):
                        if g >= 8:
                            pe.wait_ge(*after("proj_out", l, g - 7))
                        bank = g % 8
                        if n < TOKEN_SETS[l]:
                            for k in range(KC):
                                last = mm(ps[:, bank, 0:m], hT[:, k, P * t:P * t + P], w_in(l, n)[:, k, :],
                                          start=k == 0, stop=k == KC - 1)
                        else:
                            for j in range(2):
                                col = P * (2 * t + j)
                                for k in range(KC):
                                    last = mm(ps[:, bank, T * j:T * j + T], w_in(l, n)[:, k, col:col + P], hT[:, k, :],
                                              start=k == 0, stop=k == KC - 1)
                        last.then_inc(s("proj"), 1)
                        g += 1
                pe.wait_ge(*after("proj_out", l, GROUPS[l]))
                for n, (b, _, heads, _) in enumerate(NORMS[l]):
                    pe.wait_ge(*after("roped", l, n + 1))
                    for t in range(TILES):
                        if n >= 2:
                            pe.wait_ge(*after("qk_T", l, 2 * n + t - 3))
                        width = heads * HD if heads == 8 else 2 * P
                        src = tok[b][:, t, 0:512] if heads == 8 else tok[4][:, t, 0:2 * P]
                        for j in range(width // P):
                            last = tr(ps[:, (2 * n + t) % 4, P * j:P * j + P], src[:, P * j:P * j + P], ident[:, :])
                        last.then_inc(s("qk_turned"), 1)

                def q_of(q, i):
                    e = 64 * (i % 2)
                    return (QT[l][q // 2][0][e:e + 64, 2 * (q % 2) + i // 2, :],
                            QT[l][q // 2][1][e:e + 64, 2 * (q % 2) + i // 2 if (l, q // 2) != (0, 0) else q % 2, :])

                def scores(q):
                    if q:
                        pe.wait_ge(*after("masked", l, q))
                    for i in range(4):
                        qq, kk = q_of(q, i)
                        if l == 0 and q >= 2:
                            mm(ps[:, i, 0:T], kk[:, 0:P], qq, start=True, stop=True)
                            last = mm(ps[:, i, T:TRI], kk[:, P:T], qq[:, P:T], start=True, stop=True)
                        else:
                            mm(ps[:, i, 0:P], qq[:, 0:P], kk[:, 0:P], start=True, stop=True)
                            last = mm(ps[:, i, P:TRI], qq[:, P:T], kk, start=True, stop=True)
                    last.then_inc(s("scores"), 1)

                def turn_p(q):
                    buf = sc[q % 2]
                    if q:
                        pe.wait_ge(*after("y_out", l, q))
                    if l == 0 and q >= 2:
                        pe.wait_ge(*after("softplus", l, q - 1))
                        for i in range(4):
                            qq, kk = q_of(q, i)
                            mm(ps[:, 4 + i, 0:TRI], k_("neg_tri"), buf[:, i, :], start=True, stop=False)
                            mm(ps[:, 4 + i, P:T], k_("neg_ones"), buf[:, i, T:TRI], start=False, stop=False)
                            mm(ps[:, 4 + i, 0:T], kk[:, 0:P], qq, start=False, stop=False)
                            last = mm(ps[:, 4 + i, T:TRI], kk[:, P:T], qq[:, P:T], start=False, stop=True)
                    else:
                        pe.wait_ge(*after("p_ready", l, q + 1))
                        for i in range(4):
                            for j in range(3):
                                last = tr(ps[:, 4 + i, P * j:P * j + P], buf[:, i, P * j:P * j + P], ident[:, :])
                    last.then_inc(s("p_turned"), 1)

                def times_v(q):
                    pe.wait_ge(*after("pT", l, q + 1))
                    for i in range(4):
                        e = 64 * (i % 2)
                        buf, col = v_at(l, q, i)
                        v = tok[buf]
                        mm(ps[e:e + 64, 4 + i // 2, 0:T], v[:, 0, col:col + HD], pT[:, i, 0:T], start=True, stop=False)
                        last = mm(ps[e:e + 64, 4 + i // 2, P:T], v[:, 1, col:col + HD], pT[:, i, T:TRI],
                                  start=False, stop=True)
                    last.then_inc(s("y"), 1)

                pe.wait_ge(*after("qk_T", l, 2 * len(NORMS[l])))
                scores(0)
                scores(1)
                for q in range(4):
                    turn_p(q)
                    if q < 2:
                        scores(q + 2)
                    times_v(q)
                pe.wait_ge(*after("y_out", l, 4))
                if l == 0:
                    ada_sums(4, 6)
                pe.wait_ge(*after("w_out", l, 16))
                for t in range(TILES):
                    for half in range(2):
                        for k in range(KC):
                            last = mm(ps[:, 2 * t + half, :], yT[:, k, P * t:P * t + P],
                                      w_out[:, k, 512 * half:512 * half + 512], start=k == 0, stop=k == KC - 1)
                    last.then_inc(s("w_out_mult"), 1)

                if l == 0:
                    ada_sums(6, 12)
                pe.wait_ge(*after("ada_done", l, 12))
                pe.wait_ge(*after("subk", l, 16))
                for a in range(2):
                    last = tr(ps[:, 4, P * a:P * a + P], subk[:, a, :], ident[:, :])
                last.then_inc(s("subk_turned"), 1)
                for t in range(TILES):
                    pe.wait_ge(*after("ffn_norm", l, t + 1))
                    for half in range(2):
                        if t:
                            pe.wait_ge(*after("ffn_lo", l, half + 1))
                        for j in range(4):
                            last = tr(ps[:, 6 + half, P * j:P * j + P], hf[:, t, P * (4 * half + j):P * (4 * half + j) + P], ident[:, :])
                        last.then_inc(s("ffn_T"), 1)
                pe.wait_ge(*after("ffn_lo", l, 4))
                for g in range(PHEADS):
                    if g >= 4:
                        pe.wait_ge(*after("qry_out", l, g - 3))
                    pe.wait_ge(*after("wq_hi", l, g + 1))
                    pe.wait_ge(*(after("wq_lo_pool", l, g + 1) if g < 2 else after("wq_lo", l, g - 1)))
                    for j in range(2):
                        n = 0
                        for w, m in ((wq_hi, hT_hi), (wq_hi, hT_lo), (wq_lo, hT_hi)):
                            for k in range(KC):
                                last = mm(ps[:, g % 4, T * j:T * j + T], w[g % 2][:, k, P * j:P * j + P], m[:, k, :],
                                          start=n == 0, stop=n == 3 * KC - 1)
                                n += 1
                    last.then_inc(s("qry"), 1)
                pe.wait_ge(*after("qry_out", l, PHEADS))
                pe.wait_ge(*after("subk_T", l, 1))
                for n in range(8):
                    t, g = n // 4, n % 4
                    if n >= 4:
                        pe.wait_ge(*after("S_out", l, n - 3))
                    for j in range(4):
                        last = mm(ps[:, 4 + n % 4, P * j:P * j + P], qryT[:, 4 * g + j, P * t:P * t + P],
                                  subk_T[:, j % 2, :], start=True, stop=True)
                    last.then_inc(s("S_mult"), 1)
                pe.sem_inc(s("u_mult"), 4)
                with pe.Fori(0, NKEYS // U_STEP) as it:
                    for b in range(U_STEP):
                        dst = ps[:, (b // 2) % 4, T * (b % 2):T * (b % 2) + T]
                        if b % 2 == 0:
                            pe.wait_ge(*after("u_gelu", l, it * (U_STEP // 2) + (b // 2 + 1)))
                        pe.wait_ge(*after("u_hi", l, it * U_STEP + (b + 1)))
                        n = 0
                        for w, m in ((hi[b % 4], hT_hi), (hi[b % 4], hT_lo), (lo[b % 2], hT_hi)):
                            if w is lo[b % 2]:
                                pe.wait_ge(*after("u_lo", l, it * U_STEP + (b + 5)))
                            for k in range(KC):
                                last = mm(dst, w[:, P * k:P * k + P], m[:, k, :], start=n == 0, stop=n == 3 * KC - 1)
                                n += 1
                        last.then_inc(s("u_mult"), 1)
                pe.wait_ge(*after("routed", l, 1))
                pe.wait_ge(*after("u_gelu", l, NKEYS // 2 + 4))
                for a in range(3):
                    for t in range(TILES):
                        last = tr(ps[:, 4 + a, P * t:P * t + P], routes[:, a, P * t:P * t + P], ident[:, :])
                last.then_inc(s("routes_turned"), 1)
                pe.sem_inc(s("gate_mult"), 4)
                with pe.Fori(0, T // 16) as it:
                    for b in range(4):
                        pe.wait_ge(*after("gated", l, it * 4 + (b + 1)))
                        pe.wait_ge(*after("hot_dve", l, it * 4 + (b + 5)))
                        pe.wait_ge(*after("hot_pool", l, it * 4 + (b + 5)))
                        pe.wait_ge(*after("hot_act", l, it * 4 + (b + 5)))
                        for k in range(4):
                            last = mm(ps[:, b, P * k:P * k + P], one_1[:, b, k, :], one_2[:, b, k, :],
                                      start=True, stop=True)
                        last.then_inc(s("gate_mult"), 1)
                pe.wait_ge(*after("zeros", l, 1))
                for g in range(4):
                    last = mm(ps[:, 4 + g, :], zeros[:, 0:P], zeros[:, :], start=True, stop=False)
                pe.sem_inc(s("v_mult"), 4)
                with pe.Fori(0, NKEYS // V_STEP) as it:
                    for b in range(V_STEP):
                        pe.wait_ge(*after("v_hi", l, it * V_STEP + (b + 1)))
                        pe.wait_ge(*after("v_lo", l, it * V_STEP + (b + 1 + RING)))
                        for w, v in ((w_hi[b], hi[b]), (w_lo[b], hi[b]), (w_hi[b], lo[b % 2])):
                            for g in range(4):
                                last = mm(ps[:, 4 + g, :], w[:, P * (g // 2):P * (g // 2) + P],
                                          v[:, 512 * (g % 2):512 * (g % 2) + 512], start=False, stop=False,
                                          skip_group_check=True)
                        last.then_inc(s("v_mult"), 1)
                for g in range(4):
                    last = mm(ps[:, 4 + g, :], zeros[:, 0:P], zeros[:, :], start=False, stop=True)
                last.then_inc(s("v_all"), 1)

        @block.vector
        def _(dve):
            V = nc.vector
            L = lambda ins: link(dve, "dve", ins)

            for l in range(LAYERS):
                if l:
                    dve.wait_ge(layer_done, l)
                def ada_products(n0, n1):
                    for n in range(n0, n1):
                        buf, use, _ = ada_buf(n)
                        dve.wait_ge(*after(f"ada_in{buf}", 0, 16 * (use + 1)))
                        for k in range(KC):
                            ins = V.scalar_tensor_tensor(acc(0, n), ada[buf][:, k, :], silu[:, k:k + 1], acc(0, n),
                                                         ALU.mult, ALU.add)
                            if k < KC - 1:
                                L(ins)
                        ins.then_inc(s("ada_used"), 1)

                if l == 0:
                    V.memset(acc_a[:, :, :], 0.0)
                    V.memset(acc_b[:, :, :], 0.0).then_inc(s("acc_zero"), 1)
                    dve.wait_ge(*after("c_exp", 0, 1))
                    L(V.tensor_scalar(cond[:, 2, :], cond[:, 1, :], 1.0, None, ALU.add))
                    L(V.reciprocal(cond[:, 3, :], cond[:, 2, :]))
                    L(V.tensor_tensor(silu[:, :], cond[:, 3, :], cond[:, 0, :], ALU.mult))
                    dve.wait_ge(*after("ada_b", 0, 32))
                    ada_products(0, 4)
                    dve.wait_ge(cst_in, 32)
                    dve.wait_ge(x_in, 16)
                dve.wait_ge(*after("ada_done", l, 4))

                def norm(gain, gain_in, scale, shift, mid, add, done, rms):
                    dve.wait_ge(*after(gain_in, l, 16))
                    L(V.scalar_tensor_tensor(gain[:, :], mod[:, scale, :], 1.0, gain[:, :], ALU.add, ALU.mult))
                    dve.wait_ge(*after(rms, l, 1))
                    L(V.reciprocal(stat[:, 4:6], stat[:, 2:4]))
                    for t in range(TILES):
                        L(V.scalar_tensor_tensor(mid[:, t, :], xs[:, t, :], stat[:, 4 + t:5 + t], gain[:, :],
                                                 ALU.mult, ALU.mult))
                        add(t, mod[:, shift, :]).then_inc(done, 1)

                def add_mix(t, shift):
                    return V.tensor_tensor(h[:, t, :], h[:, t, :], shift, ALU.add)

                def add_ffn(t, shift):
                    return V.tensor_tensor(hf[:, t, :].rearrange("p (c q j) -> p q c j", c=KC, q=4),
                                           yg[:, t, :].rearrange("p (q c j) -> p q c j", c=KC, q=4),
                                           shift.rearrange("p (q c j) -> p q c j", c=KC, q=4), ALU.add)

                norm(g_mix, "g_mix", 1, 0, h, add_mix, s("mix_norm"), "mix_rms")
                if l == 0:
                    ada_products(4, 6)
                else:
                    dve.wait_ge(*after("ada_sum", l, 12))
                dve.wait_ge(*after("proj", l, 4))
                dve.wait_ge(*after("gains", l, 16 * (3 if l == 0 else 4)))
                dve.wait_ge(*after("cst_in", l, 16))
                half = HD // 2
                cosv = k_("cos").rearrange("p (t d) -> p t d", t=TILES)
                sinv = k_("sin").rearrange("p (t d) -> p t d", t=TILES)
                for n, _ in enumerate(NORMS[l]):
                    cv = rope_c[:, n, :].rearrange("p (t d) -> p t d", t=TILES)
                    sv = rope_s[:, n, :].rearrange("p (t d) -> p t d", t=TILES)
                    g = gains[:, n, :]
                    V.tensor_tensor(cv, cosv, spread(g, 1, TILES), ALU.mult)
                    V.tensor_tensor(sv[:, :, 0:half], sinv[:, :, 0:half], spread(g[:, half:HD], 1, TILES), ALU.mult)
                    L(V.tensor_tensor(sv[:, :, half:HD], sinv[:, :, half:HD], spread(g[:, 0:half], 1, TILES), ALU.mult))
                for pair in range(len(NORMS[l]) // 2):
                    norms = [(n, *NORMS[l][n]) for n in (2 * pair, 2 * pair + 1)]
                    for n, b, c0, heads, _ in norms:
                        dve.wait_ge(*after("proj_out", l, 2 * n + 2))
                        xv = tok[b][:, :, c0:c0 + heads * HD]
                        sq = turned[0][:, :, 0:heads * HD]
                        L(V.tensor_tensor(sq, xv, xv, ALU.mult))
                        ins = V.tensor_reduce(ssq[:, 0, 16 * n:16 * n + 2 * heads].rearrange("p (t h) -> p t h", t=TILES),
                                              sq.rearrange("p t (h d) -> p t h d", d=HD), AX, ALU.add)
                        if n == 2 * pair:
                            L(ins)
                    ins.then_inc(s("ssq"), 1)
                    if l == 0:
                        ada_products(6, 7)
                    dve.wait_ge(*after("qk_rms", l, pair + 1))
                    c1 = 32 * pair + (20 if l == 0 else 32)
                    L(V.reciprocal(ssq[:, 1, 32 * pair:c1], ssq[:, 1, 32 * pair:c1]))
                    for n, b, c0, heads, _ in norms:
                        w = heads * HD
                        xv = tok[b][:, :, c0:c0 + w].rearrange("p t (h d) -> p t h d", d=HD)
                        t0, t1, t2 = (t[:, :, 0:w].rearrange("p t (h d) -> p t h d", d=HD) for t in turned)
                        r = ssq[:, 1, 16 * n:16 * n + 2 * heads].rearrange("p (t h) -> p t h", t=TILES)
                        cv = rope_c[:, n, :].rearrange("p (t d) -> p t d", t=TILES)
                        sv = rope_s[:, n, :].rearrange("p (t d) -> p t d", t=TILES)
                        L(V.tensor_tensor(t1, xv, spread(r, 3, HD), ALU.mult))
                        V.tensor_tensor(t0, t1, spread(cv, 2, heads), ALU.mult)
                        V.tensor_tensor(t2[:, :, :, 0:half], t1[:, :, :, half:HD], spread(sv[:, :, 0:half], 2, heads),
                                        ALU.mult)
                        L(V.tensor_tensor(t2[:, :, :, half:HD], t1[:, :, :, 0:half],
                                          spread(sv[:, :, half:HD], 2, heads), ALU.mult))
                        if heads == 8:
                            ins = V.tensor_tensor(xv, t0, t2, ALU.add)
                        else:
                            kd = tok[4][:, :, 0:2 * P].rearrange("p t (h e d) -> p t h e d", e=2, d=HD)
                            V.tensor_tensor(kd[:, :, :, 0, :], t0, t2, ALU.add)
                            ins = V.tensor_tensor(kd[:, :, :, 1, :], t0, t2, ALU.add)
                        L(ins)
                        V.tensor_copy(stat[:, 0:1], stat[:, 0:1]).then_inc(s("roped"), 1)
                if l == 0:
                    ada_products(7, 10)

                def mask_scores(q):
                    buf, top = sc[q % 2], smax[q % 2]
                    dve.wait_ge(*after("scores", l, q + 1))
                    if q >= 2:
                        dve.wait_ge(*after("p_turned", l, q - 1))
                    if l == 0 and q >= 2:
                        dve.wait_ge(*after("ln_done", l, q - 1))
                        V.scalar_tensor_tensor(buf[:, :, :], ps[:, 0:4, 0:TRI], 0.0, e_abs[:, :, :],
                                               ALU.max, ALU.add).then_inc(s("masked"), 1)
                        dve.wait_ge(*after("masked", l, q + 1))
                        V.tensor_tensor(buf[:, :, :], buf[:, :, :], spread(k_("past"), 1, 4),
                                        ALU.mult).then_inc(s("softplus"), 1)
                        return
                    mask = k_("mask_a" if l == 0 else "mask_c" if q < 2 else "mask_d")
                    V.tensor_tensor(buf[:, :, :], ps[:, 0:4, 0:TRI], spread(mask, 1, 4),
                                    ALU.add).then_inc(s("masked"), 1)
                    dve.wait_ge(*after("masked", l, q + 1))
                    V.tensor_reduce(top[:, 0, :, 0], buf[:, :, 0:P], AX, ALU.max)
                    L(V.tensor_reduce(top[:, 0, :, 1], buf[:, :, P:TRI], AX, ALU.max))
                    if l == 0:
                        sk = spread(sink[:, 4 * q:4 * q + 4], 2, 2)
                        L(V.tensor_scalar(top[:, 2, :, :], sk, 1 / SCALE, None, ALU.mult))
                        L(V.tensor_tensor(top[:, 0, :, :], top[:, 0, :, :], top[:, 2, :, :], ALU.max))
                        L(V.tensor_scalar(top[:, 0, :, :], top[:, 0, :, :], -SCALE, None, ALU.mult))
                        V.tensor_tensor(top[:, 2, :, :], top[:, 0, :, :], sk, ALU.add).then_inc(s("max"), 1)
                    else:
                        V.tensor_scalar(top[:, 0, :, :], top[:, 0, :, :], -SCALE, None,
                                        ALU.mult).then_inc(s("max"), 1)

                def weigh(q):
                    buf, top = sc[q % 2], smax[q % 2]
                    if l == 0 and q >= 2:
                        dve.wait_ge(*after("p_turned", l, q + 1))
                        dve.wait_ge(*after("y", l, q))
                        V.tensor_tensor(pT[:, :, :], ps[:, 4:8, 0:TRI], spread(k_("not_past"), 1, 4),
                                        ALU.add).then_inc(s("log_w"), 1)
                        return
                    dve.wait_ge(*after("exp", l, q + 1))
                    if l == 0:
                        L(V.tensor_tensor(top[:, 1, :, :], top[:, 1, :, :], top[:, 2, :, :], ALU.add))
                    L(V.reciprocal(top[:, 1, :, :], top[:, 1, :, :]))
                    V.tensor_tensor(buf[:, :, 0:P], buf[:, :, 0:P], spread(top[:, 1, :, 0], 2, P), ALU.mult)
                    V.tensor_tensor(buf[:, :, P:TRI], buf[:, :, P:TRI], spread(top[:, 1, :, 1], 2, 2 * P),
                                    ALU.mult).then_inc(s("p_ready"), 1)

                mask_scores(0)
                for q in range(4):
                    if q < 3:
                        mask_scores(q + 1)
                    weigh(q)
                    if l == 0 and q < 2:
                        ada_products(10 + q, 11 + q)
                dve.wait_ge(*after("ada_done", l, 6))
                for t in range(TILES):
                    dve.wait_ge(*after("w_out_mult", l, t + 1))
                    y = ps[:, 2 * t:2 * t + 2, :]
                    L(V.tensor_tensor(yg[:, t, :], y.rearrange("p a n -> p (a n)"), mod[:, 2, :], ALU.mult))
                    V.tensor_tensor(xs[:, t, :], xs[:, t, :], yg[:, t, :], ALU.add).then_inc(s("mixed"), 1)
                dve.wait_ge(*after("ada_done", l, 12))
                norm(g_ffn, "g_ffn", 4, 3, yg, add_ffn, s("ffn_norm"), "ffn_rms")
                V.tensor_copy(stat[:, 0:1], stat[:, 0:1]).then_inc(s("x_read"), 1)
                for t in range(TILES):
                    for half_ in range(2):
                        dve.wait_ge(*after("ffn_hi", l, 2 * t + half_ + 1))
                        V.tensor_tensor(hT_lo[:, 4 * half_:4 * half_ + 4, P * t:P * t + P],
                                        ps[:, 6 + half_, :].rearrange("p (c t) -> p c t", c=4),
                                        hT_hi[:, 4 * half_:4 * half_ + 4, P * t:P * t + P],
                                        ALU.subtract).then_inc(s("ffn_lo"), 1)
                for g in range(2, PHEADS):
                    dve.wait_ge(*after("wq_hi", l, g + 1))
                    dve.wait_ge(*after("qry", l, g - 1))
                    V.tensor_tensor(wq_lo[g % 2][:, :, :], wq[:, :, 2 * P * g:2 * P * g + 2 * P],
                                    wq_hi[g % 2][:, :, :], ALU.subtract).then_inc(s("wq_lo"), 1)
                dve.wait_ge(*after("S_out", l, 8))
                dve.wait_ge(*after("x_kept", l, 32))
                dve.sem_inc(s("u_turned"), RING)
                with dve.Fori(0, NKEYS // U_STEP) as it:
                    def turn(b):
                        dve.wait_ge(*after(f"u_in{b % RING}", l, it * (U_STEP // RING * 64) + 64 * (b // RING + 1)))
                        dve.wait_ge(*after("u_lo", l, it * U_STEP + (b + 1)))
                        V.transpose(uT[b % 4][:, :], ring[b % RING][:, :]).then_inc(s("u_turned"), 1)

                    rs = s("route_step")
                    n_ = [0]

                    def R(ins):
                        n_[0] += 1
                        ins.then_inc(rs, 1)
                        dve.wait_ge(rs, n_[0])

                    def top16(src, spare, vals, idx):
                        R(V.max(vals[:, 0:8], src))
                        V.max_index(idx[:, 0:8], vals[:, 0:8], src)
                        R(V.match_replace(spare, vals[:, 0:8], src, -3e38))
                        R(V.max(vals[:, 8:16], spare))
                        R(V.max_index(idx[:, 8:16], vals[:, 8:16], spare))

                    R(V.tensor_copy(fix[:, :, :], S[:, bass.ds(it, 1), :, :].rearrange("p a h n -> p (a h) n")))
                    turn(0)
                    top16(fix[:, 0, :], cut[:, 0:NKEYS], topv[:, 0, :], topi[:, 0, :])
                    turn(1)
                    top16(fix[:, 1, :], cut[:, 0:NKEYS], topv[:, 1, :], topi[:, 1, :])
                    turn(2)
                    R(V.tensor_tensor(cand[:, :, :], spread(topv[:, 0, :], 2, TOPK), spread(topv[:, 1, :], 1, TOPK),
                                      ALU.add))
                    flat = cand[:, :, :].rearrange("p a b -> p (a b)")
                    top16(flat, cut[:, :], topv[:, 2, :], topi[:, 2, :])
                    turn(3)
                    V.tensor_copy(topf[:, 0:2, :], topi[:, 0:2, :])
                    R(V.tensor_scalar(topb[:, :], topi[:, 2, :], 4, None, ALU.logical_shift_right))
                    R(V.tensor_copy(topf[:, 2, :], topb[:, :]))
                    pick(R, 0, routes[:, 0, bass.ds(it * TOPK, TOPK)])
                    turn(4)
                    R(V.tensor_scalar(topb[:, :], topi[:, 2, :], 15, None, ALU.bitwise_and))
                    R(V.tensor_copy(topf[:, 2, :], topb[:, :]))
                    pick(R, 1, routes[:, 1, bass.ds(it * TOPK, TOPK)])
                    turn(5)
                    R(V.tensor_copy(routes[:, 2, bass.ds(it * TOPK, TOPK)], topv[:, 2, :]))
                    turn(6)
                    turn(7)
                    dve.sem_clear(rs)
                gt = routes[:, 2, :].rearrange("p (n k) -> p n k", k=TOPK)
                gs = cut[:, 0:T].rearrange("p (n k) -> p n k", k=TOPK)
                L(V.tensor_tensor(gs, gt, spread(gt[:, :, 0], 2, TOPK), ALU.subtract))
                V.tensor_copy(cand[:, 0, :], gs[:, :, 0]).then_inc(s("gate_in"), 1)
                dve.wait_ge(*after("gate_exp", l, 1))
                L(V.tensor_reduce(topf[:, 0, :], gs, AX, ALU.add))
                L(V.reciprocal(topf[:, 1, :], topf[:, 0, :]))
                V.tensor_tensor(gt, gs, spread(topf[:, 1, :], 2, TOPK), ALU.mult).then_inc(s("routed"), 1)
                dve.wait_ge(*after("routes_T", l, 1))
                dve.sem_inc(s("gated"), 4)
                dve.sem_inc(s("hot_dve"), 4)
                with dve.Fori(0, T // 16) as it:
                    dve.wait_ge(*after("hot_dve", l, it * 4 + 4))
                    dve.sem_inc(s("dve_held"), 1)
                    V.tensor_copy(cols["dve"][:, :, :], routes_T[:, 1:3, bass.ds(it * 16, 16)]
                                  ).then_inc(s("cols_dve"), 1)
                    dve.wait_ge(*after("cols_dve", l, it + 1))

                    def rows(b):
                        dve.wait_ge(*after("gate_mult", l, it * 4 + (b + 1)))
                        if b % 2 == 0:
                            c = cols["dve"][:, :, 4 * b:4 * b + 1]
                            V.tensor_scalar(one_2[:, b, 0, :], iota[:, :], c[:, 0, :], c[:, 1, :],
                                            ALU.is_equal, ALU.mult)
                        V.tensor_tensor(one_1[:, b, :, :], spread(iota[:, :], 1, 4),
                                        spread(routes_T[:, 0, bass.ds(it * 16 + 4 * b, 4)], 2, NKEYS),
                                        ALU.is_equal).then_inc(s("hot_dve"), 1)

                    def times(b):
                        dve.wait_ge(*after("gate_mult", l, it * 4 + (b + 5)))
                        w = W[:, :, bass.ds(it * 16 + 4 * b, 4)].rearrange("p j t -> p t j")
                        V.tensor_tensor(w, w, ps[:, b, :].rearrange("p (t j) -> p t j", t=4),
                                        ALU.mult).then_inc(s("gated"), 1)

                    rows(0)
                    rows(1)
                    rows(2)
                    times(0)
                    rows(3)
                    times(1)
                    times(2)
                    times(3)
                dve.wait_ge(*after("gated", l, T // 4 + 4))
                V.memset(zeros[:, :].bitcast(F32), 0.0).then_inc(s("zeros"), 1)
                dve.sem_inc(s("v_lo"), RING)

                def split_v(blk, b):
                    dve.wait_ge(*after("v_hi", l, blk + 1))
                    V.tensor_tensor(w_lo[b][:, :], W[:, bass.ds(blk, 1), :].rearrange("p a t -> p (a t)"),
                                    w_hi[b][:, :], ALU.subtract)
                    dve.wait_ge(*after("v_mult", l, blk + 3))
                    V.tensor_tensor(lo[b % 2][:, :], ring[b][:, :], hi[b][:, :],
                                    ALU.subtract).then_inc(s("v_lo"), 1)

                with dve.Fori(0, (V_PLAIN if l == 0 else NKEYS) // V_STEP) as it:
                    for b in range(V_STEP):
                        split_v(it * V_STEP + b, b)
                if l == 0:
                    dve.sem_inc(s("ada_1_used"), 2)
                    for third in range(3):
                        dve.wait_ge(*after(f"ada_1_b{third}", 0, 16))
                        a1 = acc_1[:, 4 * third:4 * third + 4, :].rearrange("p m n -> p (m n)")
                        with dve.Fori(0, KC // 2) as it:
                            for b in range(2 * V_STEP):
                                split_v(it * 2 * V_STEP + (V_PLAIN + 2 * V_STEP * (KC // 2) * third + b), b % V_STEP)
                                if b % V_STEP == 1:
                                    r = b // V_STEP
                                    dve.wait_ge(*after(f"ada_1_in{r}", 0, it * 16 + (16 * (KC // 2) * third + 16)))
                                    dve.wait_ge(*after("ada_1_used", 0, it * 2 + (KC * third + r + 2)))
                                    V.scalar_tensor_tensor(a1, ada_1[r][:, :], silu[:, bass.ds(it * 2 + r, 1)], a1,
                                                           ALU.mult, ALU.add).then_inc(s("ada_1_used"), 1)
                dve.wait_ge(*after("v_all", l, 1))
                dve.wait_ge(*after("x_back", l, 32))
                for t in range(TILES):
                    L(V.tensor_tensor(yg[:, t, :], ps[:, 4 + 2 * t:6 + 2 * t, :].rearrange("p a n -> p (a n)"),
                                      gate_b[:, :], ALU.mult))
                    L(V.tensor_tensor(xs[:, t, :], x_back[:, t, :], yg[:, t, :], ALU.add))
                V.tensor_copy(stat[:, 0:1], xs[:, 0, 0:1]).then_inc(layer_done, 1)

        @block.scalar
        def _(act):
            A = nc.scalar.activation
            L = lambda ins: link(act, "act", ins)

            for l in range(LAYERS):
                if l == 0:
                    act.wait_ge(*after("c_in", 0, 16))
                    A(cond[:, 1, :], cond[:, 0, :], ACT.Exp, scale=-1.0).then_inc(s("c_exp"), 1)

                def ada_out(n0, n1):
                    for n in range(n0, n1):
                        act.wait_ge(*after("ada_sum", l, n + 1))
                        A(mod[:, n // 2, 512 * (n % 2):512 * (n % 2) + 512], ps[:, ada_bank(l, n), :], ACT.Copy,
                          scale=-1.0).then_inc(s("ada_done"), 1)

                def rms(dst, done):
                    for t in range(TILES):
                        L(A(dst[:, t, :], xs[:, t, :], ACT.Square, accum_out=stat[:, t:t + 1]))
                    L(A(stat[:, 2:4], stat[:, 0:2], ACT.Copy, scale=1.0 / D, bias=EPS))
                    A(stat[:, 2:4], stat[:, 2:4], ACT.Sqrt).then_inc(done, 1)

                ada_out(0, 4)
                if l == 0:
                    act.wait_ge(x_in, 16)
                else:
                    act.wait_ge(layer_done, l)
                rms(h, s("mix_rms"))
                if l:
                    ada_out(4, 12)
                for n in range(4):
                    act.wait_ge(*after("mix_T", l, n + 1))
                    t, half = n // 2, n % 2
                    A(hT[:, 4 * half:4 * half + 4, P * t:P * t + P], ps[:, 4 + n, :].rearrange("p (c t) -> p c t", c=4),
                      ACT.Copy).then_inc(s("hT"), 1)
                g = 0
                for n, (a, m) in enumerate(SETS[l]):
                    for t in range(2):
                        act.wait_ge(*after("proj", l, g + 1))
                        if n < TOKEN_SETS[l]:
                            A(tok[n][:, t, 0:m], ps[:, g % 8, 0:m], ACT.Copy).then_inc(s("proj_out"), 1)
                        else:
                            A(qk_T[n - 1][:, 2 * t:2 * t + 2, :], ps[:, g % 8, :].rearrange("p (a t) -> p a t", a=2),
                              ACT.Copy, scale=SCALE if n == 3 else 1.0).then_inc(s("proj_out"), 1)
                        g += 1
                        if g in (6, 10) and g // 4 <= len(NORMS[l]) // 2:
                            pair = g // 4 - 1
                            c0, c1 = 32 * pair, 32 * pair + (20 if l == 0 else 32)
                            act.wait_ge(*after("ssq", l, pair + 1))
                            L(A(ssq[:, 1, c0:c1], ssq[:, 0, c0:c1], ACT.Copy, scale=1.0 / HD, bias=EPS))
                            A(ssq[:, 1, c0:c1], ssq[:, 1, c0:c1], ACT.Sqrt).then_inc(s("qk_rms"), 1)
                for n, (_, _, heads, _) in enumerate(NORMS[l]):
                    for t in range(TILES):
                        act.wait_ge(*after("qk_turned", l, 2 * n + t + 1))
                        w = heads * HD // P if heads == 8 else 2
                        A(qk_T[n][:, 0:w, P * t:P * t + P],
                          ps[:, (2 * n + t) % 4, 0:P * w].rearrange("p (a t) -> p a t", a=w),
                          ACT.Copy).then_inc(s("qk_T"), 1)
                def exps(q):
                    buf, top = sc[q % 2], smax[q % 2]
                    if l == 0 and q >= 2:
                        act.wait_ge(*after("scores", l, q + 1))
                        if q > 2:
                            act.wait_ge(*after("masked", l, q))
                        L(A(e_abs[:, :, :], ps[:, 0:4, 0:TRI], ACT.Abs))
                        L(A(e_abs[:, :, :], e_abs[:, :, :], ACT.Exp, scale=-1.0))
                        A(e_abs[:, :, :], e_abs[:, :, :], ACT.Ln, bias=1.0).then_inc(s("ln_done"), 1)
                        return
                    act.wait_ge(*after("max", l, q + 1))
                    if l == 0:
                        A(top[:, 2, :, :], top[:, 2, :, :], ACT.Exp)
                    for i in range(4):
                        A(buf[:, i, 0:P], buf[:, i, 0:P], ACT.Exp, bias=top[:, 0, i, 0:1], scale=SCALE,
                          accum_out=top[:, 1, i, 0:1])
                        last = A(buf[:, i, P:TRI], buf[:, i, P:TRI], ACT.Exp, bias=top[:, 0, i, 1:2], scale=SCALE,
                                 accum_out=top[:, 1, i, 1:2])
                    last.then_inc(s("exp"), 1)

                exps(0)
                for q in range(4):
                    if q < 3:
                        exps(q + 1)
                    if l == 0 and q >= 2:
                        act.wait_ge(*after("log_w", l, q - 1))
                        A(pT[:, :, :], pT[:, :, :], ACT.Exp).then_inc(s("pT"), 1)
                    else:
                        act.wait_ge(*after("p_turned", l, q + 1))
                        A(pT[:, :, :], ps[:, 4:8, 0:TRI], ACT.Copy).then_inc(s("pT"), 1)
                    act.wait_ge(*after("y", l, q + 1))
                    A(yT[:, 2 * q:2 * q + 2, :], ps[:, 4:6, 0:T], ACT.Copy).then_inc(s("y_out"), 1)
                if l == 0:
                    ada_out(4, 12)
                act.wait_ge(*after("subk_turned", l, 1))
                A(subk_T[:, :, :], ps[:, 4, 0:2 * P].rearrange("p (a n) -> p a n", a=2), ACT.Copy
                  ).then_inc(s("subk_T"), 1)
                def wq_part(g):
                    A(wq_hi[g % 2][:, :, :], wq[:, :, 2 * P * g:2 * P * g + 2 * P], ACT.Copy).then_inc(s("wq_hi"), 1)

                act.wait_ge(*after("w_out_mult", l, TILES))
                act.wait_ge(*after("wq", l, 64))
                wq_part(0)
                wq_part(1)
                act.wait_ge(*after("mixed", l, TILES))
                rms(hf, s("ffn_rms"))
                for n in range(4):
                    act.wait_ge(*after("ffn_T", l, n + 1))
                    t, half = n // 2, n % 2
                    src = ps[:, 6 + half, :].rearrange("p (c t) -> p c t", c=4)
                    A(hT_hi[:, 4 * half:4 * half + 4, P * t:P * t + P], src, ACT.Copy).then_inc(s("ffn_hi"), 1)
                for g in range(PHEADS):
                    act.wait_ge(*after("qry", l, g + 1))
                    if g < PHEADS - 2:
                        wq_part(g + 2)
                    A(qryT[:, 2 * g:2 * g + 2, :], ps[:, g % 4, :].rearrange("p (a t) -> p a t", a=2),
                      ACT.Copy).then_inc(s("qry_out"), 1)
                for n in range(8):
                    act.wait_ge(*after("S_mult", l, n + 1))
                    A(S[:, 2 * n:2 * n + 2, :, :], ps[:, 4 + n % 4, :].rearrange("p (a h n) -> p a h n", a=2, h=2),
                      ACT.Copy).then_inc(s("S_out"), 1)
                act.wait_ge(*after("x_kept", l, 32))
                act.sem_inc(s("u_gelu"), 4)

                def u_hi(it, b):
                    act.wait_ge(*after("u_turned", l, it * U_STEP + (b + 1 + RING)))
                    act.wait_ge(*after("u_mult", l, it * U_STEP + (b + 1)))
                    A(hi[b % 4][:, :].rearrange("p (c g i) -> p c g i", c=KC, g=4),
                      uT[b % 4][:, :].rearrange("p (g c i) -> p c g i", g=4, c=KC), ACT.Copy
                      ).then_inc(s("u_hi"), 1)

                def gelu(it, pair):
                    act.wait_ge(*after("u_mult", l, it * U_STEP + (2 * pair + 6)))
                    act.sem_inc(s("act_held"), 1)
                    A(W[:, bass.ds(it * U_STEP + 2 * pair, 2), :],
                      ps[:, pair, :].rearrange("p (a t) -> p a t", a=2), ACT.Gelu).then_inc(s("u_gelu"), 1)

                def turn(it, last):
                    for b in range(3, U_STEP + 3):
                        if b < U_STEP or not last:
                            u_hi(it, b)
                        if b % 2:
                            gelu(it, b // 2 - 1)

                for b in range(3):
                    u_hi(0, b)
                with act.Fori(0, NKEYS // U_STEP - 1) as it:
                    turn(it, False)
                turn(NKEYS // U_STEP - 1, True)
                act.wait_ge(*after("gate_in", l, 1))
                A(cut[:, 0:T], cut[:, 0:T], ACT.Exp).then_inc(s("gate_exp"), 1)
                act.wait_ge(*after("routes_turned", l, 1))
                A(routes_T[:, :, :], ps[:, 4:7, 0:T], ACT.Copy).then_inc(s("routes_T"), 1)
                act.wait_ge(*after("routes_T", l, 1))
                act.sem_inc(s("hot_act"), 4)
                with act.Fori(0, T // 16) as it:
                    act.wait_ge(*after("hot_act", l, it * 4 + 4))
                    act.sem_inc(s("act_held"), 1)
                    A(cols["act"][:, 0, :], routes_T[:, 1, bass.ds(it * 16, 16)], ACT.Copy, scale=-1.0)
                    A(cols["act"][:, 1, :], routes_T[:, 2, bass.ds(it * 16, 16)], ACT.Copy).then_inc(s("cols_act"), 1)
                    act.wait_ge(*after("cols_act", l, it + 1))
                    for b in range(4):
                        for k in range(2):
                            n = 4 * b + 1 + k
                            last = A(gap[:, b, k, :], iota[:, :], ACT.Abs, bias=cols["act"][:, 0, n:n + 1])
                    last.then_inc(s("gap"), 1)
                    for b in range(4):
                        act.wait_ge(*after("gate_mult", l, it * 4 + (b + 1)))
                        act.sem_inc(s("act_held"), 1)
                        if b == 0:
                            act.wait_ge(*after("gap", l, it + 1))
                            act.sem_inc(s("act_held"), 1)
                        for k in range(2):
                            n = 4 * b + 1 + k
                            last = A(one_2[:, b, 1 + k, :], gap[:, b, k, :], ACT.Relu,
                                     bias=cols["act"][:, 1, n:n + 1], scale=-BIG)
                        last.then_inc(s("hot_act"), 1)
                act.wait_ge(*after("gated", l, T // 4 + 4))
                with act.Fori(0, NKEYS // V_STEP) as it:
                    for b in range(V_STEP):
                        act.wait_ge(*after("v_mult", l, it * V_STEP + (b + 1)))
                        act.sem_inc(s("act_held"), 1)
                        A(w_hi[b][:, :], W[:, bass.ds(it * V_STEP + b, 1), :].rearrange("p a t -> p (a t)"),
                          ACT.Copy)
                        act.wait_ge(*after(f"v_in{b % RING}", l, it * 16 + 16))
                        A(hi[b][:, :], ring[b % RING][:, :], ACT.Copy).then_inc(s("v_hi"), 1)

        @block.gpsimd
        def _(pool):
            for l in range(LAYERS):
                if l:
                    pool.wait_ge(layer_done, l)
                for g in range(2):
                    pool.wait_ge(*after("wq_hi", l, g + 1))
                    nc.gpsimd.tensor_tensor(wq_lo[g][:, :, :], wq[:, :, 2 * P * g:2 * P * g + 2 * P],
                                            wq_hi[g][:, :, :], ALU.subtract).then_inc(s("wq_lo_pool"), 1)
                pool.wait_ge(*after("x_kept", l, 32))
                pool.sem_inc(s("u_lo"), 4)
                with pool.Fori(0, NKEYS // U_STEP) as it:
                    for b in range(U_STEP):
                        pool.wait_ge(*after("u_mult", l, it * U_STEP + (b + 3)))
                        pool.wait_ge(*after("u_hi", l, it * U_STEP + (b + 1)))
                        nc.gpsimd.tensor_tensor(
                            lo[b % 2][:, :].rearrange("p (c g i) -> p c g i", c=KC, g=4),
                            uT[b % 4][:, :].rearrange("p (g c i) -> p c g i", g=4, c=KC),
                            hi[b % 4][:, :].rearrange("p (c g i) -> p c g i", c=KC, g=4),
                            ALU.subtract).then_inc(s("u_lo"), 1)
                pool.wait_ge(*after("routes_T", l, 1))
                pool.sem_inc(s("hot_pool"), 4)
                with pool.Fori(0, T // 16) as it:
                    pool.wait_ge(*after("hot_pool", l, it * 4 + 4))
                    pool.sem_inc(s("pool_held"), 1)
                    nc.gpsimd.tensor_copy(cols["pool"][:, :, :], routes_T[:, 1:3, bass.ds(it * 16, 16)]
                                          ).then_inc(s("cols_pool"), 1)
                    pool.wait_ge(*after("cols_pool", l, it + 1))
                    pool.sem_inc(s("pool_held"), 1)
                    for b in range(4):
                        pool.wait_ge(*after("gate_mult", l, it * 4 + (b + 1)))
                        pool.sem_inc(s("pool_held"), 1)
                        for k in (0, 3) if b % 2 else (3,):
                            c = cols["pool"][:, :, 4 * b + k:4 * b + k + 1]
                            last = nc.gpsimd.tensor_scalar(one_2[:, b, k, :], iota[:, :], c[:, 0, :], c[:, 1, :],
                                                           ALU.is_equal, ALU.mult)
                        last.then_inc(s("hot_pool"), 1)
                if l == 0:
                    for third in range(3):
                        pool.wait_ge(*after("v_lo", 0, 16 + 8 * third + RING))
                        nc.gpsimd.memset(acc_1[:, 4 * third:4 * third + 4, :], 0.0).then_inc(s("acc_1_zero"), 1)


_INS = ['x', 'c', 'ada_w', 'ada_b', 'norm_mix_g', 'norm_ffn_g', 'w_in_ab', 'w_out_ab', 'sinks_a', 'qnorm_a',
        'knorm_a', 'w_in_cd', 'w_out_cd', 'qnorm_c', 'knorm_c', 'qnorm_d', 'knorm_d', 'peer_wq',
        'peer_subkeys', 'peer_u', 'peer_v']


def kernel(**inputs):
    import concourse.bacc as _bacc
    from concourse.bass_utils import run_bass_kernel_spmd as _run

    nc = _bacc.Bacc("TRN2", target_bir_lowering=False, num_devices=1)
    arrays, args = {}, []
    for name in _INS:
        a = np.ascontiguousarray(inputs[name])
        arrays[f"in_{name}"] = a
        args.append(nc.dram_tensor(f"in_{name}", a.shape, mybir.dt.from_np(a.dtype), kind="ExternalInput").ap())
    arrays["const"] = constants()
    args.append(nc.dram_tensor("const", (P, CONST_N), F32, kind="ExternalInput").ap())
    args.append(nc.dram_tensor("out", (1, T, D), F32, kind="ExternalOutput").ap())
    trunk_kernel(nc, *args)
    r = _run(nc, [arrays], core_ids=[0])
    return r.results[0]["out"]
```

```python
import numpy as np
from contextlib import ExitStack

import concourse.bass as bass
from concourse import mybir

F32 = mybir.dt.float32
F32R = mybir.dt.float32r
U32 = mybir.dt.uint32
ALU = mybir.AluOpType
ACT = mybir.ActivationFunctionType
AX = mybir.AxisListType.X

P = 128
T = 256
TILES = T // P
D = 1024
KC = D // P
HD = 64
NH = 8
LAYERS = 2
EPS = 1e-6
BIG = 1e30
SCALE = HD ** -0.5
TRI = 3 * P

NKEYS = 128
PHEADS = 8
TOPK = 16
NE = NKEYS * NKEYS
ROUTES = PHEADS * TOPK

U_STEP = 8
V_STEP = 4
V_PLAIN = 32
RING = 4

CONST = {}
_at = 0
for _name, _n in (("ident", P), ("iota", P), ("mask_a", TRI), ("mask_c", TRI), ("mask_d", TRI),
                  ("past", TRI), ("not_past", TRI), ("neg_tri", P), ("neg_ones", P),
                  ("cos", 2 * HD), ("sin", 2 * HD)):
    CONST[_name] = (_at, _at + _n)
    _at += _n
CONST_N = _at


def constants():
    c = np.zeros((P, CONST_N), np.float32)

    def put(name, a):
        c[:, CONST[name][0]:CONST[name][1]] = a

    i = np.arange(P)
    put("ident", np.eye(P))
    put("iota", np.broadcast_to(i, (P, P)))
    dist = np.concatenate([i[:, None] - i[None], P + i[:, None] - i[None], i[:, None] - i[None]], 1)
    put("mask_a", np.where((dist >= 0) & (dist <= P - 1), 0.0, -BIG))
    put("mask_d", np.where(dist >= 0, 0.0, -BIG))
    seen = sum(((dist >= 0) & (dist % r == 0) & (dist <= w)).astype(int)
               for w, r in ((128, 1), (512, 4), (2048, 16)))
    put("mask_c", np.where(seen > 0, np.log(np.maximum(seen, 1)) / SCALE, -BIG))
    gap = np.concatenate([i[None] - i[:, None], P + i[None] - i[:, None], i[None] - i[:, None]], 1)
    put("past", gap > 0)
    put("not_past", np.where(gap > 0, 0.0, -BIG))
    put("neg_tri", -(i[:, None] >= i[None]).astype(np.float32))
    put("neg_ones", -1.0)
    half = HD // 2
    inv = np.float32(10000.0) ** (-np.arange(half, dtype=np.float32) / np.float32(half))
    ang = np.arange(T, dtype=np.float32)[:, None] * inv[None].astype(np.float32)
    cos, sin = np.cos(ang), np.sin(ang)
    for t in range(TILES):
        a, s = cos[t * P:(t + 1) * P], sin[t * P:(t + 1) * P]
        c0, s0 = CONST["cos"][0] + t * HD, CONST["sin"][0] + t * HD
        c[:, c0:c0 + HD] = np.concatenate([a, a], 1)
        c[:, s0:s0 + HD] = np.concatenate([-s, s], 1)
    return c


def spread(a, axis, n):
    a = a.unsqueeze(axis)
    shape = list(a.shape)
    shape[axis] = n
    return a.to_broadcast(shape)


def trunk_kernel(nc, x, c, ada_w, ada_b, norm_mix_g, norm_ffn_g, w_in_ab, w_out_ab, sinks_a, qnorm_a,
                 knorm_a, w_in_cd, w_out_cd, qnorm_c, knorm_c, qnorm_d, knorm_d, peer_wq, peer_subkeys,
                 peer_u, peer_v, const, out):
    ctx = ExitStack()
    with ctx:
        base = (nc.sbuf_base + 31) // 32 * 32
        KB = 1024

        def at(name, kb, shape, dt=F32):
            return nc.alloc_sbuf_tensor_at(name, [P] + shape, dt, offset=base + int(kb * KB))

        W = at("W", 0, [NKEYS, T])
        W_IN = [[(0, 512), (16, 256), (24, 512), (40, 512), (56, 512)], [(32 + 16 * n, 512) for n in range(6)]]
        w_in_sb = [[at(f"w_in{l}_{n}", kb, [KC, m]) for n, (kb, m) in enumerate(W_IN[l])] for l in range(LAYERS)]
        w_in_lo = [[at(f"w_in_lo{l}_{n}", kb, [KC, m], F32R) for n, (kb, m) in enumerate(W_IN[l])]
                   for l in range(LAYERS)]
        w_out = at("w_out", 96, [KC, D])
        qk_T = [at(f"qk_T{n}", 64 + 4 * n, [4, T]) for n in range(4)]
        turned_l = [[at(f"turned{l}_{n}", kb + 4 * n, [TILES, 512]) for n in range(3)] for l, kb in enumerate((0, 20))]
        rope_l = [[at(f"rope{l}_{n}", kb + 2 * n, [4, 2 * HD]) for n in range(2)] for l, kb in enumerate((12, 16))]
        sc = [at(f"sc{n}", 16 + 6 * n, [4, TRI]) for n in range(2)]
        pT = at("pT", 28, [4, TRI])
        e_abs = at("e_abs", 34, [4, TRI])
        wq = at("wq", 0, [KC, 2048])
        wq_hi = [at(f"wq_hi{n}", 96 + 8 * n, [KC, 2 * P], F32R) for n in range(2)]
        wq_lo = [at(f"wq_lo{n}", 112 + 8 * n, [KC, 2 * P], F32R) for n in range(2)]
        hf = at("hf", 72, [TILES, D])
        qryT = at("qryT", 80, [2 * PHEADS, T])

        xs = at("xs", 128, [TILES, D])
        mod = at("mod", 136, [6, D])
        cst = at("cst", 160, [CONST_N])
        mix_hi = at("mix_hi", 172, [KC, T], F32R)
        mix_lo = [at(f"mix_lo{l}", kb, [KC, T], F32R) for l, kb in enumerate((144, 8))]
        w_in_hi = [[at(f"w_in_hi{l}_{n}", kb + 4 * n, [D], F32R) for n in range(2)] for l, kb in enumerate((152, 0))]
        yT = at("yT", 172, [KC, T])
        ada = [at(f"ada{n}", kb, [KC, 512]) for n, kb in enumerate((172, 96, 112))]
        acc_a = at("acc_a", 192, [4, 512])
        acc_b = at("acc_b", 80, [8, 512])
        acc_1 = at("acc_1", 8, [12, 512])
        ada_1 = [at(f"ada_1_{n}", kb, [2048]) for n, kb in enumerate((0, 160))]
        h = at("h", 180, [TILES, D])
        g_mix = at("g_mix", 188, [D])
        g_ffn = at("g_ffn", 136, [D])
        tok = [at(f"tok{n}", 180 + 4 * n if n < 5 else 140, [TILES, 512]) for n in range(6)]

        hi = [at(f"hi{n}", kb, [D], F32R) for n, kb in enumerate((128, 192, 136, 140))]
        lo = [at(f"lo{n}", kb, [D], F32R) for n, kb in enumerate((132, 196))]
        S = at("S", 112, [TILES * PHEADS, 2, NKEYS])
        uT = [at(f"uT{n}", kb, [D]) for n, kb in enumerate((152, 188, 144, 148))]
        ring = [at("ring0", 156, [D])] + [at(f"ring{n}", 172 + 4 * n, [D]) for n in range(1, RING)]
        hT_hi = at("hT_hi", 160, [KC, T], F32R)
        hT_lo = at("hT_lo", 168, [KC, T], F32R)
        w_hi = [at(f"w_hi{n}", 144 + n, [T], F32R) for n in range(4)]
        w_lo = [at(f"w_lo{n}", 148 + n, [T], F32R) for n in range(4)]
        zeros = at("zeros", 152, [512], F32R)
        one_1 = at("one_1", 140, [4, 4, NKEYS])
        one_2 = at("one_2", 160, [4, 4, NKEYS])
        routes_T = at("routes_T", 136, [3, T])
        cols = {e: at(f"cols_{e}", 139 + 0.25 * n, [2, 16]) for n, e in enumerate(("dve", "act", "pool"))}
        gap = at("gap", 148, [4, 2, NKEYS])
        x_back = at("x_back", 64, [TILES, D])
        gate_b = at("gate_b", 72, [D])
        yg = at("yg", 180, [TILES, D])

        ident = at("ident", 200, [P])
        iota = at("iota", 200.5, [P])
        routes = at("routes", 201, [3, T])
        subk = at("subk", 201, [2, P])
        subk_T = at("subk_T", 202, [2, P])
        cond = at("cond", 203, [4, KC])
        silu = at("silu", 207.6875, [KC])
        gains = at("gains", 204, [4, HD])
        stat = at("stat", 207.625, [8])
        ssq = at("ssq", 205.125, [2, 64])
        sink = at("sink", 205.75, [8])
        smax = [at(f"smax{n}", 206 + n / 8, [3, 4, 2]) for n in range(2)]
        fix = at("fix", 204, [2, NKEYS])
        cut = at("cut", 205, [TOPK * TOPK])
        cand = at("cand", 206, [TOPK, TOPK])
        topv = at("topv", 207, [3, TOPK])
        topi = at("topi", 207.1875, [3, TOPK], U32)
        topf = at("topf", 207.375, [3, TOPK])
        topb = at("topb", 207.5625, [TOPK], U32)

        ps = ctx.enter_context(nc.psum_tensor("ps", [P, 8, 512], F32))

        x_keep = nc.dram_tensor("x_keep", [TILES, P, D], F32, kind="Internal").ap()
        gate_keep = nc.dram_tensor("gate_keep", [1, D], F32, kind="Internal").ap()

        def sem(name):
            return ctx.enter_context(nc.semaphore(name))

        def k_(name):
            a, b = CONST[name]
            return cst[:, a:b]

        cst_in, x_in, out_sem = sem("tables_in"), sem("x_in"), sem("out_done")
        layer_done = sem("layer_done")
        COUNTS = dict(
            c_in=16, bias_a=16, bias_b=16, ada_1_b0=16, ada_1_b1=16, ada_1_b2=16, cst_in=16,
            ada_in0=32, ada_in1=80, ada_in2=80, ada_1_in0=192, ada_1_in1=192, w_in0=16, w_in1=16, w_in2=16,
            w_in3=16, w_in4=16, w_in5=0, w_out=16, g_mix=16, gains=48, g_ffn=16, subk=16, wq=64, x_kept=32,
            x_back=32, **{f"u_in{n}": NKEYS // RING * 64 for n in range(RING)},
            **{f"v_in{n}": NKEYS // RING * 16 for n in range(RING)},
            ada_sum=12, w_in_mult=20, mix_T=4, qk_turned=4, scores=4, p_turned=4, y=4, w_out_mult=2, subk_turned=1,
            ffn_T=4, qry=8, S_mult=8, u_mult=NKEYS + 4, routes_turned=1, gate_mult=T // 4 + 4,
            v_mult=NKEYS + 4, v_all=1,
            acc_zero=1, mix_lo=4, ada_1_used=3 * KC + 2, ada_used=12, mix_norm=2, ssq=1,
            roped=2, masked=4, p_ready=2, softplus=2, log_w=2, max=2, mixed=2, ffn_norm=2,
            x_read=1, ffn_lo=4, wq_lo=6, u_turned=NKEYS + RING, route_step=0, gate_in=1, routed=1, gated=T // 4 + 4,
            hot_dve=T // 4 + 4, cols_dve=T // 16, dve_held=0, zeros=1, v_lo=NKEYS + RING,
            c_exp=1, ada_done=12, w_in_hi=20, mix_rms=2, mix_hi=4, proj_out=10,
            qk_rms=1, qk_T=4, ln_done=2, pT=4, exp=2, y_out=4,
            subk_T=1, ffn_rms=2, ffn_hi=4, wq_hi=8, qry_out=8, S_out=8, u_gelu=NKEYS // 2 + 4, u_hi=NKEYS, act_held=0,
            hot_act=T // 4 + 4, cols_act=T // 16, gap=T // 16, gate_exp=1, routes_T=1, v_hi=NKEYS,
            acc_1_zero=3, acc_b_zero=1, w_in_lo=20, wq_lo_pool=2,
            u_lo=NKEYS + 4, hot_pool=T // 4 + 4, cols_pool=T // 16, pool_held=0)
        SEMS = {n: sem(n) for n in COUNTS}

        def w_in(l, n):
            return w_in_sb[l][n][:, :, :]

        def acc(l, n):
            return acc_1[:, n, :] if l else acc_a[:, n, :] if n < 4 else acc_b[:, n - 4, :]

        def ada_bank(l, n):
            return 6 + n % 2 if l == 0 and n >= 4 else n % 4

        def ada_buf(n):
            buf = [n % 3 if n < 4 else 1 + n % 2 for n in range(12)]
            before = [m for m in range(n) if buf[m] == buf[n]]
            return buf[n], len(before), before[-1] if before else None

        def s(name):
            return SEMS[name]

        def after(name, l, count):
            return SEMS[name], count + COUNTS[name] * l if l else count

        chain = {n: sem(f"{n}_step") for n in ("dve", "act", "pool")}
        steps = {n: 0 for n in chain}

        def link(eng, name, ins):
            steps[name] += 1
            ins.then_inc(chain[name], 1)
            eng.wait_ge(chain[name], steps[name])

        block = ctx.enter_context(nc.Block())

        w_in_l = [w_in_ab[0], w_in_cd[0]]
        w_out_l = [w_out_ab[0], w_out_cd[0]]
        SETS = [[(0, 512), (512, 256), (1792, 512), (768, 512), (1280, 512)],
                [(0, 512), (512, 512), (1536, 512), (2048, 512), (1024, 512), (2560, 512)]]
        TOKEN_SETS = [3, 6]
        GROUPS = [2 * TOKEN_SETS[0] + 4, 2 * TOKEN_SETS[1]]
        PIECES = [[(n, u) for n in range(len(SETS[l])) for u in range(4)] for l in range(LAYERS)]
        ROOTS = [{13: 0}, {13: 0, 22: 1}]

        def piece(w, l, n, u):
            return w[:, 2 * u:2 * u + 2, :] if n < TOKEN_SETS[l] else w[:, :, P * u:P * u + P]

        def piece_hi(l, n, i):
            a = 2 if n < TOKEN_SETS[l] else KC
            m = SETS[l][n][1] if n < TOKEN_SETS[l] else P
            return w_in_hi[l][i % 2][:, 0:a * m].rearrange("p (a m) -> p a m", a=a)

        NORMS = [[(0, 0, 8, 0), (1, 0, 2, 1)],
                 [(0, 0, 8, 0), (1, 0, 8, 1), (2, 0, 8, 2), (3, 0, 8, 3)]]

        uv = peer_u.rearrange("l (g i j) (q d) -> l q j i g d", g=4, i=32, q=4)
        vv = peer_v.rearrange("l (i j) d -> l j i d", j=NKEYS)

        QT = [[(qk_T[0], qk_T[1]), (qk_T[2], qk_T[3])]] * 2

        def p_bank(q):
            return 0 if q == 3 else 4

        def v_at(l, q, i):
            if l == 0:
                return (1, P + HD * q) if q < 2 else (2, HD * (4 * (q - 2) + i))
            return (4 if q < 2 else 5, HD * (4 * (q % 2) + i))

        def pick(R, half, dst):
            eq = cand[:, :, :]
            R(nc.vector.tensor_tensor(eq, spread(topf[:, 2, :], 2, TOPK), spread(iota[:, 0:TOPK], 1, TOPK),
                                      ALU.is_equal))
            R(nc.vector.tensor_tensor(eq, eq, spread(topf[:, half, :], 1, TOPK), ALU.mult))
            R(nc.vector.tensor_reduce(dst, eq, AX, ALU.add))

        @block.sync
        def _(sp):
            sp.dma_start(cond[:, 0, :], c.rearrange("a (p c) -> p (a c)", c=KC)).then_inc(s("c_in"), 16)

            def load_ada(n):
                buf, _, last = ada_buf(n)
                if last is not None:
                    sp.wait_ge(*after("ada_used", 0, last + 1))
                sp.dma_start(ada[buf][:, :, :],
                             ada_w[0].rearrange("(p c) n -> p c n", c=KC)[:, :, 512 * n:512 * n + 512]
                             ).then_inc(s(f"ada_in{buf}"), 16)

            load_ada(0)
            sp.wait_ge(*after("acc_zero", 0, 1))
            sp.dma_start(acc_a[0:1, :, :], ada_b[0:1, 0:2048].rearrange("a (m d) -> a m d", m=4)
                         ).then_inc(s("bias_a"), 16)
            load_ada(1)
            load_ada(2)
            sp.dma_start(ident[:, :], const[:, 0:P]).then_inc(cst_in, 16)
            sp.dma_start(iota[:, :], const[:, P:2 * P]).then_inc(cst_in, 16)
            sp.dma_start(xs[:, :, :], x.rearrange("a (t p) d -> p (a t) d", p=P)).then_inc(x_in, 16)
            sp.wait_ge(*after("acc_b_zero", 0, 1))
            sp.dma_start(acc_b[0:1, :, :], ada_b[0:1, 2048:6144].rearrange("a (m d) -> a m d", m=8)
                         ).then_inc(s("bias_b"), 16)
            for l in range(LAYERS):
                def load_w_in(n, l=l):
                    a, m = SETS[l][n]
                    sp.dma_start(w_in(l, n), w_in_l[l].rearrange("(p c) n -> p c n", c=KC)[:, :, a:a + m]
                                 ).then_inc(s(f"w_in{n}"), 16)

                if l == 0:
                    load_ada(3)
                if l == 0:
                    sp.dma_start(cst[:, :], const).then_inc(s("cst_in"), 16)
                sp.dma_start(g_mix[:, :], norm_mix_g[l:l + 1, :].to_broadcast([P, D])
                             ).then_inc(s("g_mix"), 16)
                names = [(qnorm_a, knorm_a, sinks_a), (qnorm_c, knorm_c, qnorm_d, knorm_d)][l]
                for n, g in enumerate(names):
                    dst = gains[:, n, :] if g is not sinks_a else sink[:, :]
                    sp.dma_start(dst, g[0:1, :].to_broadcast([P, g.shape[1]])).then_inc(s("gains"), 16)
                if l == 0:
                    for n in range(len(SETS[l])):
                        load_w_in(n)
                    for n in range(4, 12):
                        load_ada(n)
                    sp.wait_ge(*after("ada_used", 0, 12))
                else:
                    sp.wait_ge(layer_done, l * TILES)
                    for n in range(2, len(SETS[l])):
                        load_w_in(n)
                    sp.wait_ge(*after("w_in_mult", l, len(PIECES[l])))
                sp.dma_start(w_out[:, :, :], w_out_l[l].rearrange("(c p) n -> p c n", p=P)
                             ).then_inc(s("w_out"), 16)
                sp.wait_ge(*after("mix_norm", l, TILES))
                sp.dma_start(g_ffn[:, :], norm_ffn_g[l:l + 1, :].to_broadcast([P, D])
                             ).then_inc(s("g_ffn"), 16)
                sp.dma_start(subk[:, :, :], peer_subkeys[l].rearrange("a n d -> n a d")
                             ).then_inc(s("subk"), 16)
                sp.wait_ge(*after("y", l, 4))
                for q in range(4):
                    sp.dma_start(wq[32 * q:32 * q + 32, :, :],
                                 peer_wq[l, 256 * q:256 * q + 256, :].rearrange("(c j) n -> j c n", j=32)
                                 ).then_inc(s("wq"), 16)
                sp.wait_ge(*after("mixed", l, TILES))
                sp.wait_ge(*after("ada_done", l, 12))
                sp.dma_start(x_keep.rearrange("t p d -> p t d"), xs[:, :, :]).then_inc(s("x_kept"), 16)
                sp.dma_start(gate_keep, mod[0:1, 5, :]).then_inc(s("x_kept"), 16)
                sp.wait_ge(*after("x_kept", l, 32))
                sp.wait_ge(*after("ffn_lo", l, 4))
                sp.wait_ge(*after("x_read", l, 1))
                with sp.Fori(0, NKEYS // U_STEP) as it:
                    for b in range(U_STEP):
                        sp.wait_ge(*after("u_turned", l, it * U_STEP + (b + 1)))
                        for q in range(4):
                            sp.dma_start(ring[b % RING][32 * q:32 * q + 32, :].rearrange("i (g d) -> i g d", g=4),
                                         uv[l, q, bass.ds(it * U_STEP + b, 1)].rearrange("a i g d -> (a i) g d")
                                         ).then_inc(s(f"u_in{b % RING}"), 16)
                def load_v(blk, b):
                    sp.wait_ge(*after("v_lo", l, blk + 1))
                    sp.dma_start(ring[b][:, :], vv[l, bass.ds(blk, 1)].rearrange("a i d -> (a i) d")
                                 ).then_inc(s(f"v_in{b}"), 16)

                with sp.Fori(0, (V_PLAIN if l == 0 else NKEYS) // V_STEP) as it:
                    for b in range(V_STEP):
                        load_v(it * V_STEP + b, b)
                if l == 0:
                    def load_bias(third):
                        sp.wait_ge(*after("acc_1_zero", 0, third + 1))
                        sp.dma_start(acc_1[0:1, 4 * third:4 * third + 4, :],
                                     ada_b[1:2, 2048 * third:2048 * third + 2048].rearrange("a (m d) -> a m d", m=4)
                                     ).then_inc(s(f"ada_1_b{third}"), 16)

                    load_bias(0)
                    load_bias(1)
                    for third in range(3):
                        if third == 1:
                            load_bias(2)
                        if third:
                            load_w_in(third - 1, 1)
                        with sp.Fori(0, KC // 2) as it:
                            for b in range(2 * V_STEP):
                                if b % V_STEP == 0:
                                    r = b // V_STEP
                                    sp.wait_ge(*after("ada_1_used", 0, it * 2 + (KC * third + r + 1)))
                                    sp.dma_start(ada_1[r][:, :],
                                                 ada_w[1].rearrange("(p c) n -> c p n", c=KC)
                                                 [bass.ds(it * 2 + r, 1), :, 2048 * third:2048 * third + 2048]
                                                 .rearrange("a p n -> (a p) n")).then_inc(s(f"ada_1_in{r}"), 16)
                                load_v(it * 2 * V_STEP + (V_PLAIN + 2 * V_STEP * (KC // 2) * third + b), b % V_STEP)
                sp.dma_start(x_back[:, :, :], x_keep.rearrange("t p d -> p t d")).then_inc(s("x_back"), 16)
                sp.dma_start(gate_b[:, :], gate_keep.to_broadcast([P, D])).then_inc(s("x_back"), 16)
                if l == 0:
                    sp.wait_ge(*after("ada_1_used", 0, 3 * KC + 2))
                    sp.dma_start(cst[:, :], const).then_inc(s("cst_in"), 16)
                sp.wait_ge(*after("v_all", l, 1))
            sp.wait_ge(layer_done, LAYERS * TILES)
            sp.dma_start(out.rearrange("a (t p) d -> p (a t) d", p=P), xs[:, :, :]).then_inc(out_sem, 16)
            sp.wait_ge(out_sem, 16)

        @block.tensor
        def _(pe):
            mm, tr = nc.tensor.matmul, nc.tensor.transpose
            pe.wait_ge(cst_in, 32)
            for l in range(LAYERS):
                pe.wait_ge(*after("cst_in", l, 16))

                def ada_sums(n0, n1):
                    for n in range(n0, n1):
                        if l == 0:
                            pe.wait_ge(*after("ada_used", 0, n + 1))
                        if n >= 4:
                            pe.wait_ge(*after("ada_done", l, n - 3 if l or n < 6 else n - 1))
                        mm(ps[:, ada_bank(l, n), :], k_("neg_ones"), acc(l, n), start=True, stop=True
                           ).then_inc(s("ada_sum"), 1)

                ada_sums(0, 12 if l else 4)
                hv = h[:, :, :].rearrange("p t (m c) -> p t c m", c=KC)
                for t in range(TILES):
                    pe.wait_ge(*after("mix_norm", l, t + 1))
                    for half in range(2):
                        for j in range(4):
                            last = tr(ps[:, 4 + 2 * t + half, P * j:P * j + P], hv[:, t, 4 * half + j, :], ident[:, :])
                        last.then_inc(s("mix_T"), 1)
                pe.wait_ge(*after("mix_lo", l, 4))
                pe.wait_ge(*after("ada_done", l, 12 if l else 4))
                for i, (n, u) in enumerate(PIECES[l]):
                    w_hi_, w_lo_ = piece_hi(l, n, i), piece(w_in_lo[l][n], l, n, u)
                    g = 2 * n if n < TOKEN_SETS[l] else 2 * n + u // 2
                    if g >= 8 and (u == 0 or g % 2 and u == 2):
                        pe.wait_ge(*after("proj_out", l, g - 6 if n < TOKEN_SETS[l] else g - 7))
                    pe.wait_ge(*after("w_in_hi", l, i + 1))
                    for x_, w in ((mix_hi, w_hi_), (mix_lo[l], w_hi_), (mix_hi, w_lo_)):
                        if w is w_lo_:
                            pe.wait_ge(*after("w_in_lo", l, i + 1))
                        first, end = x_ is mix_hi and w is w_hi_, w is w_lo_
                        if n < TOKEN_SETS[l]:
                            m = SETS[l][n][1]
                            for t in range(2):
                                for k in range(2):
                                    last = mm(ps[:, (g + t) % 8, 0:m], x_[:, 2 * u + k, P * t:P * t + P], w[:, k, :],
                                              start=u == 0 and k == 0 and first, stop=u == 3 and k == 1 and end)
                        else:
                            j = u % 2
                            for k in range(KC):
                                last = mm(ps[:, g % 8, T * j:T * j + T], w[:, k, :], x_[:, k, :],
                                          start=k == 0 and first, stop=k == KC - 1 and end)
                    last.then_inc(s("w_in_mult"), 1)
                pe.wait_ge(*after("proj_out", l, GROUPS[l]))
                for n, (b, _, heads, _) in enumerate(NORMS[l]):
                    pe.wait_ge(*after("roped", l, n + 1))
                    for t in range(TILES):
                        if n >= 2:
                            pe.wait_ge(*after("qk_T", l, 2 * n + t - 3))
                        width = heads * HD if heads == 8 else 2 * P
                        src = tok[b][:, t, 0:512] if heads == 8 else tok[4][:, t, 0:2 * P]
                        for j in range(width // P):
                            last = tr(ps[:, (2 * n + t) % 4, P * j:P * j + P], src[:, P * j:P * j + P], ident[:, :])
                        last.then_inc(s("qk_turned"), 1)

                def q_of(q, i):
                    e = 64 * (i % 2)
                    return (QT[l][q // 2][0][e:e + 64, 2 * (q % 2) + i // 2, :],
                            QT[l][q // 2][1][e:e + 64, 2 * (q % 2) + i // 2 if (l, q // 2) != (0, 0) else q % 2, :])

                def scores(q):
                    if q:
                        pe.wait_ge(*after("masked", l, q))
                    for i in range(4):
                        qq, kk = q_of(q, i)
                        if l == 0 and q >= 2:
                            mm(ps[:, i, 0:T], kk[:, 0:P], qq, start=True, stop=True)
                            last = mm(ps[:, i, T:TRI], kk[:, P:T], qq[:, P:T], start=True, stop=True)
                        else:
                            mm(ps[:, i, 0:P], qq[:, 0:P], kk[:, 0:P], start=True, stop=True)
                            last = mm(ps[:, i, P:TRI], qq[:, P:T], kk, start=True, stop=True)
                    last.then_inc(s("scores"), 1)

                def turn_p(q):
                    buf, b0 = sc[q % 2], p_bank(q)
                    if q == 3:
                        pe.wait_ge(*after("masked", l, 4))
                    elif q:
                        pe.wait_ge(*after("y_out", l, q))
                    if l == 0 and q >= 2:
                        pe.wait_ge(*after("softplus", l, q - 1))
                        for i in range(4):
                            qq, kk = q_of(q, i)
                            mm(ps[:, b0 + i, 0:TRI], k_("neg_tri"), buf[:, i, :], start=True, stop=False)
                            mm(ps[:, b0 + i, P:T], k_("neg_ones"), buf[:, i, T:TRI], start=False, stop=False)
                            mm(ps[:, b0 + i, 0:T], kk[:, 0:P], qq, start=False, stop=False)
                            last = mm(ps[:, b0 + i, T:TRI], kk[:, P:T], qq[:, P:T], start=False, stop=True)
                    else:
                        pe.wait_ge(*after("p_ready", l, q + 1))
                        for i in range(4):
                            for j in range(3):
                                last = tr(ps[:, b0 + i, P * j:P * j + P], buf[:, i, P * j:P * j + P], ident[:, :])
                    last.then_inc(s("p_turned"), 1)

                def times_v(q):
                    pe.wait_ge(*after("pT", l, q + 1))
                    if q == 3:
                        pe.wait_ge(*after("y_out", l, q))
                    for i in range(4):
                        e = 64 * (i % 2)
                        buf, col = v_at(l, q, i)
                        v = tok[buf]
                        mm(ps[e:e + 64, 4 + i // 2, 0:T], v[:, 0, col:col + HD], pT[:, i, 0:T], start=True, stop=False)
                        last = mm(ps[e:e + 64, 4 + i // 2, P:T], v[:, 1, col:col + HD], pT[:, i, T:TRI],
                                  start=False, stop=True)
                    last.then_inc(s("y"), 1)

                pe.wait_ge(*after("qk_T", l, 2 * len(NORMS[l])))
                scores(0)
                scores(1)
                for q in range(4):
                    turn_p(q)
                    if q < 2:
                        scores(q + 2)
                    if l == 0 and q == 3:
                        ada_sums(4, 8)
                    times_v(q)
                if l == 0:
                    ada_sums(8, 12)
                pe.wait_ge(*after("y_out", l, 4))
                pe.wait_ge(*after("w_out", l, 16))
                for t in range(TILES):
                    for half in range(2):
                        for k in range(KC):
                            last = mm(ps[:, 2 * t + half, :], yT[:, k, P * t:P * t + P],
                                      w_out[:, k, 512 * half:512 * half + 512], start=k == 0, stop=k == KC - 1)
                    last.then_inc(s("w_out_mult"), 1)

                pe.wait_ge(*after("ada_done", l, 12))
                pe.wait_ge(*after("subk", l, 16))
                for a in range(2):
                    last = tr(ps[:, 4, P * a:P * a + P], subk[:, a, :], ident[:, :])
                last.then_inc(s("subk_turned"), 1)
                for t in range(TILES):
                    pe.wait_ge(*after("ffn_norm", l, t + 1))
                    for half in range(2):
                        if t:
                            pe.wait_ge(*after("ffn_lo", l, half + 1))
                        for j in range(4):
                            a = P * (4 * half + j)
                            last = tr(ps[:, 6 + half, P * j:P * j + P], hf[:, t, a:a + P], ident[:, :])
                        last.then_inc(s("ffn_T"), 1)
                pe.wait_ge(*after("ffn_lo", l, 4))
                for g in range(PHEADS):
                    if g >= 4:
                        pe.wait_ge(*after("qry_out", l, g - 3))
                    pe.wait_ge(*after("wq_hi", l, g + 1))
                    pe.wait_ge(*(after("wq_lo_pool", l, g + 1) if g < 2 else after("wq_lo", l, g - 1)))
                    for j in range(2):
                        n = 0
                        for w, m in ((wq_hi, hT_hi), (wq_hi, hT_lo), (wq_lo, hT_hi)):
                            for k in range(KC):
                                last = mm(ps[:, g % 4, T * j:T * j + T], w[g % 2][:, k, P * j:P * j + P], m[:, k, :],
                                          start=n == 0, stop=n == 3 * KC - 1)
                                n += 1
                    last.then_inc(s("qry"), 1)
                pe.sem_inc(s("u_mult"), 4)
                pe.wait_ge(*after("qry_out", l, PHEADS))
                pe.wait_ge(*after("subk_T", l, 1))
                for n in range(8):
                    t, g = n // 4, n % 4
                    if n >= 4:
                        pe.wait_ge(*after("S_out", l, n - 3))
                    for j in range(4):
                        last = mm(ps[:, 4 + n % 4, P * j:P * j + P], qryT[:, 4 * g + j, P * t:P * t + P],
                                  subk_T[:, j % 2, :], start=True, stop=True)
                    last.then_inc(s("S_mult"), 1)
                with pe.Fori(0, NKEYS // U_STEP) as it:
                    for b in range(U_STEP):
                        dst = ps[:, (b // 2) % 4, T * (b % 2):T * (b % 2) + T]
                        if b % 2 == 0:
                            pe.wait_ge(*after("u_gelu", l, it * (U_STEP // 2) + (b // 2 + 1)))
                        pe.wait_ge(*after("u_hi", l, it * U_STEP + (b + 1)))
                        n = 0
                        for w, m in ((hi[b % 4], hT_hi), (hi[b % 4], hT_lo), (lo[b % 2], hT_hi)):
                            if w is lo[b % 2]:
                                pe.wait_ge(*after("u_lo", l, it * U_STEP + (b + 5)))
                            for k in range(KC):
                                last = mm(dst, w[:, P * k:P * k + P], m[:, k, :], start=n == 0, stop=n == 3 * KC - 1)
                                n += 1
                        last.then_inc(s("u_mult"), 1)
                pe.wait_ge(*after("routed", l, 1))
                for a in range(3):
                    for t in range(TILES):
                        last = tr(ps[:, 4 + a, P * t:P * t + P], routes[:, a, P * t:P * t + P], ident[:, :])
                last.then_inc(s("routes_turned"), 1)
                pe.sem_inc(s("gate_mult"), 4)
                with pe.Fori(0, T // 16) as it:
                    for b in range(4):
                        pe.wait_ge(*after("gated", l, it * 4 + (b + 1)))
                        pe.wait_ge(*after("hot_dve", l, it * 4 + (b + 5)))
                        pe.wait_ge(*after("hot_pool", l, it * 4 + (b + 5)))
                        pe.wait_ge(*after("hot_act", l, it * 4 + (b + 5)))
                        for k in range(4):
                            last = mm(ps[:, b, P * k:P * k + P], one_1[:, b, k, :], one_2[:, b, k, :],
                                      start=True, stop=True)
                        last.then_inc(s("gate_mult"), 1)
                pe.wait_ge(*after("zeros", l, 1))
                for g in range(4):
                    last = mm(ps[:, 4 + g, :], zeros[:, 0:P], zeros[:, :], start=True, stop=False)
                pe.sem_inc(s("v_mult"), 4)
                with pe.Fori(0, NKEYS // V_STEP) as it:
                    for b in range(V_STEP):
                        pe.wait_ge(*after("v_hi", l, it * V_STEP + (b + 1)))
                        pe.wait_ge(*after("v_lo", l, it * V_STEP + (b + 1 + RING)))
                        for w, v in ((w_hi[b], hi[b]), (w_lo[b], hi[b]), (w_hi[b], lo[b % 2])):
                            for g in range(4):
                                last = mm(ps[:, 4 + g, :], w[:, P * (g // 2):P * (g // 2) + P],
                                          v[:, 512 * (g % 2):512 * (g % 2) + 512], start=False, stop=False,
                                          skip_group_check=True)
                        last.then_inc(s("v_mult"), 1)
                for g in range(4):
                    last = mm(ps[:, 4 + g, :], zeros[:, 0:P], zeros[:, :], start=False, stop=True)
                last.then_inc(s("v_all"), 1)

        @block.vector
        def _(dve):
            V = nc.vector
            L = lambda ins: link(dve, "dve", ins)

            for l in range(LAYERS):
                if l:
                    dve.wait_ge(layer_done, l * TILES)
                def ada_products(n0, n1):
                    for n in range(n0, n1):
                        buf, use, _ = ada_buf(n)
                        dve.wait_ge(*after(f"ada_in{buf}", 0, 16 * (use + 1)))
                        for k in range(KC):
                            ins = V.scalar_tensor_tensor(acc(0, n), ada[buf][:, k, :], silu[:, k:k + 1], acc(0, n),
                                                         ALU.mult, ALU.add)
                            if k < KC - 1:
                                L(ins)
                        ins.then_inc(s("ada_used"), 1)

                if l == 0:
                    V.memset(acc_a[:, :, :], 0.0).then_inc(s("acc_zero"), 1)
                    dve.wait_ge(*after("c_exp", 0, 1))
                    L(V.tensor_scalar(cond[:, 2, :], cond[:, 1, :], 1.0, None, ALU.add))
                    L(V.reciprocal(cond[:, 3, :], cond[:, 2, :]))
                    L(V.tensor_tensor(silu[:, :], cond[:, 3, :], cond[:, 0, :], ALU.mult))
                    dve.wait_ge(*after("bias_a", 0, 16))
                    ada_products(0, 4)
                    dve.wait_ge(cst_in, 32)
                    dve.wait_ge(x_in, 16)
                dve.wait_ge(*after("ada_done", l, 4))

                def gain_of(gain, gain_in, scale):
                    dve.wait_ge(*after(gain_in, l, 16))
                    L(V.scalar_tensor_tensor(gain[:, :], mod[:, scale, :], 1.0, gain[:, :], ALU.add, ALU.mult))

                def norm(t, gain, shift, mid, add, done, rms):
                    dve.wait_ge(*after(rms, l, t + 1))
                    L(V.reciprocal(stat[:, 4 + t:5 + t], stat[:, 2 + t:3 + t]))
                    L(V.scalar_tensor_tensor(mid[:, t, :], xs[:, t, :], stat[:, 4 + t:5 + t], gain[:, :],
                                             ALU.mult, ALU.mult))
                    add(t, mod[:, shift, :]).then_inc(done, 1)

                def add_mix(t, shift):
                    return V.tensor_tensor(h[:, t, :], h[:, t, :], shift, ALU.add)

                def add_ffn(t, shift):
                    return V.tensor_tensor(hf[:, t, :].rearrange("p (c q j) -> p q c j", c=KC, q=4),
                                           yg[:, t, :].rearrange("p (q c j) -> p q c j", c=KC, q=4),
                                           shift.rearrange("p (q c j) -> p q c j", c=KC, q=4), ALU.add)

                gain_of(g_mix, "g_mix", 1)
                for t in range(TILES):
                    norm(t, g_mix, 0, h, add_mix, s("mix_norm"), "mix_rms")
                for n in range(4):
                    t, half = n // 2, n % 2
                    dve.wait_ge(*after("mix_hi", l, n + 1))
                    V.tensor_tensor(mix_lo[l][:, 4 * half:4 * half + 4, P * t:P * t + P],
                                    ps[:, 4 + n, :].rearrange("p (c t) -> p c t", c=4),
                                    mix_hi[:, 4 * half:4 * half + 4, P * t:P * t + P],
                                    ALU.subtract).then_inc(s("mix_lo"), 1)
                if l == 0:
                    dve.wait_ge(*after("bias_b", 0, 16))
                    ada_products(4, 6)
                else:
                    dve.wait_ge(*after("ada_sum", l, 12))
                dve.wait_ge(*after("w_in_mult", l, 8))
                dve.wait_ge(*after("gains", l, 16 * (3 if l == 0 else 4)))
                dve.wait_ge(*after("cst_in", l, 16))
                half = HD // 2
                turned, (rope_c, rope_s) = turned_l[l], rope_l[l]
                cosv = k_("cos").rearrange("p (t d) -> p t d", t=TILES)
                sinv = k_("sin").rearrange("p (t d) -> p t d", t=TILES)
                for n, _ in enumerate(NORMS[l]):
                    cv = rope_c[:, n, :].rearrange("p (t d) -> p t d", t=TILES)
                    sv = rope_s[:, n, :].rearrange("p (t d) -> p t d", t=TILES)
                    g = gains[:, n, :]
                    V.tensor_tensor(cv, cosv, spread(g, 1, TILES), ALU.mult)
                    V.tensor_tensor(sv[:, :, 0:half], sinv[:, :, 0:half], spread(g[:, half:HD], 1, TILES), ALU.mult)
                    L(V.tensor_tensor(sv[:, :, half:HD], sinv[:, :, half:HD], spread(g[:, 0:half], 1, TILES), ALU.mult))
                for pair in range(len(NORMS[l]) // 2):
                    norms = [(n, *NORMS[l][n]) for n in (2 * pair, 2 * pair + 1)]
                    for n, b, c0, heads, _ in norms:
                        dve.wait_ge(*after("proj_out", l, 2 * n + 2))
                        xv = tok[b][:, :, c0:c0 + heads * HD]
                        sq = turned[0][:, :, 0:heads * HD]
                        L(V.tensor_tensor(sq, xv, xv, ALU.mult))
                        ins = V.tensor_reduce(ssq[:, 0, 16 * n:16 * n + 2 * heads].rearrange("p (t h) -> p t h", t=TILES),
                                              sq.rearrange("p t (h d) -> p t h d", d=HD), AX, ALU.add)
                        if n == 2 * pair:
                            L(ins)
                    ins.then_inc(s("ssq"), 1)
                    if l == 0:
                        ada_products(6, 7)
                    dve.wait_ge(*after("qk_rms", l, pair + 1))
                    c1 = 32 * pair + (20 if l == 0 else 32)
                    L(V.reciprocal(ssq[:, 1, 32 * pair:c1], ssq[:, 1, 32 * pair:c1]))
                    for n, b, c0, heads, _ in norms:
                        w = heads * HD
                        xv = tok[b][:, :, c0:c0 + w].rearrange("p t (h d) -> p t h d", d=HD)
                        t0, t1, t2 = (t[:, :, 0:w].rearrange("p t (h d) -> p t h d", d=HD) for t in turned)
                        r = ssq[:, 1, 16 * n:16 * n + 2 * heads].rearrange("p (t h) -> p t h", t=TILES)
                        cv = rope_c[:, n, :].rearrange("p (t d) -> p t d", t=TILES)
                        sv = rope_s[:, n, :].rearrange("p (t d) -> p t d", t=TILES)
                        L(V.tensor_tensor(t1, xv, spread(r, 3, HD), ALU.mult))
                        V.tensor_tensor(t0, t1, spread(cv, 2, heads), ALU.mult)
                        V.tensor_tensor(t2[:, :, :, 0:half], t1[:, :, :, half:HD], spread(sv[:, :, 0:half], 2, heads),
                                        ALU.mult)
                        L(V.tensor_tensor(t2[:, :, :, half:HD], t1[:, :, :, 0:half],
                                          spread(sv[:, :, half:HD], 2, heads), ALU.mult))
                        if heads == 8:
                            ins = V.tensor_tensor(xv, t0, t2, ALU.add)
                        else:
                            kd = tok[4][:, :, 0:2 * P].rearrange("p t (h e d) -> p t h e d", e=2, d=HD)
                            V.tensor_tensor(kd[:, :, :, 0, :], t0, t2, ALU.add)
                            ins = V.tensor_tensor(kd[:, :, :, 1, :], t0, t2, ALU.add)
                        L(ins)
                        V.tensor_copy(stat[:, 0:1], stat[:, 0:1]).then_inc(s("roped"), 1)
                if l == 0:
                    ada_products(7, 8)

                def mask_scores(q):
                    buf, top = sc[q % 2], smax[q % 2]
                    dve.wait_ge(*after("scores", l, q + 1))
                    if q >= 2:
                        dve.wait_ge(*after("p_turned", l, q - 1))
                    if l == 0 and q >= 2:
                        dve.wait_ge(*after("ln_done", l, q - 1))
                        V.scalar_tensor_tensor(buf[:, :, :], ps[:, 0:4, 0:TRI], 0.0, e_abs[:, :, :],
                                               ALU.max, ALU.add).then_inc(s("masked"), 1)
                        dve.wait_ge(*after("masked", l, q + 1))
                        V.tensor_tensor(buf[:, :, :], buf[:, :, :], spread(k_("past"), 1, 4),
                                        ALU.mult).then_inc(s("softplus"), 1)
                        return
                    mask = k_("mask_a" if l == 0 else "mask_c" if q < 2 else "mask_d")
                    V.tensor_tensor(buf[:, :, :], ps[:, 0:4, 0:TRI], spread(mask, 1, 4),
                                    ALU.add).then_inc(s("masked"), 1)
                    dve.wait_ge(*after("masked", l, q + 1))
                    V.tensor_reduce(top[:, 0, :, 0], buf[:, :, 0:P], AX, ALU.max)
                    L(V.tensor_reduce(top[:, 0, :, 1], buf[:, :, P:TRI], AX, ALU.max))
                    if l == 0:
                        sk = spread(sink[:, 4 * q:4 * q + 4], 2, 2)
                        L(V.tensor_scalar(top[:, 2, :, :], sk, 1 / SCALE, None, ALU.mult))
                        L(V.tensor_tensor(top[:, 0, :, :], top[:, 0, :, :], top[:, 2, :, :], ALU.max))
                        L(V.tensor_scalar(top[:, 0, :, :], top[:, 0, :, :], -SCALE, None, ALU.mult))
                        V.tensor_tensor(top[:, 2, :, :], top[:, 0, :, :], sk, ALU.add).then_inc(s("max"), 1)
                    else:
                        V.tensor_scalar(top[:, 0, :, :], top[:, 0, :, :], -SCALE, None,
                                        ALU.mult).then_inc(s("max"), 1)

                def weigh(q):
                    buf, top = sc[q % 2], smax[q % 2]
                    if l == 0 and q >= 2:
                        dve.wait_ge(*after("p_turned", l, q + 1))
                        dve.wait_ge(*after("y", l, q))
                        V.tensor_tensor(pT[:, :, :], ps[:, p_bank(q):p_bank(q) + 4, 0:TRI], spread(k_("not_past"), 1, 4),
                                        ALU.add).then_inc(s("log_w"), 1)
                        return
                    dve.wait_ge(*after("exp", l, q + 1))
                    if l == 0:
                        L(V.tensor_tensor(top[:, 1, :, :], top[:, 1, :, :], top[:, 2, :, :], ALU.add))
                    L(V.reciprocal(top[:, 1, :, :], top[:, 1, :, :]))
                    V.tensor_tensor(buf[:, :, 0:P], buf[:, :, 0:P], spread(top[:, 1, :, 0], 2, P), ALU.mult)
                    V.tensor_tensor(buf[:, :, P:TRI], buf[:, :, P:TRI], spread(top[:, 1, :, 1], 2, 2 * P),
                                    ALU.mult).then_inc(s("p_ready"), 1)

                mask_scores(0)
                mask_scores(1)
                weigh(0)
                weigh(1)
                if l == 0:
                    ada_products(8, 10)
                mask_scores(2)
                if l == 0:
                    ada_products(10, 11)
                    mask_scores(3)
                    weigh(2)
                    ada_products(11, 12)
                else:
                    weigh(2)
                    mask_scores(3)
                weigh(3)
                dve.wait_ge(*after("ada_done", l, 12))
                gain_of(g_ffn, "g_ffn", 4)
                for t in range(TILES):
                    dve.wait_ge(*after("w_out_mult", l, t + 1))
                    y = ps[:, 2 * t:2 * t + 2, :]
                    L(V.tensor_tensor(yg[:, t, :], y.rearrange("p a n -> p (a n)"), mod[:, 2, :], ALU.mult))
                    L(V.tensor_tensor(xs[:, t, :], xs[:, t, :], yg[:, t, :], ALU.add))
                    V.tensor_copy(stat[:, 5:6], stat[:, 5:6]).then_inc(s("mixed"), 1)
                    norm(t, g_ffn, 3, yg, add_ffn, s("ffn_norm"), "ffn_rms")
                V.tensor_copy(stat[:, 0:1], stat[:, 0:1]).then_inc(s("x_read"), 1)
                for t in range(TILES):
                    for half_ in range(2):
                        dve.wait_ge(*after("ffn_hi", l, 2 * t + half_ + 1))
                        V.tensor_tensor(hT_lo[:, 4 * half_:4 * half_ + 4, P * t:P * t + P],
                                        ps[:, 6 + half_, :].rearrange("p (c t) -> p c t", c=4),
                                        hT_hi[:, 4 * half_:4 * half_ + 4, P * t:P * t + P],
                                        ALU.subtract).then_inc(s("ffn_lo"), 1)
                dve.sem_inc(s("u_turned"), RING)
                for g in range(2, PHEADS):
                    dve.wait_ge(*after("wq_hi", l, g + 1))
                    dve.wait_ge(*after("qry", l, g - 1))
                    V.tensor_tensor(wq_lo[g % 2][:, :, :], wq[:, :, 2 * P * g:2 * P * g + 2 * P],
                                    wq_hi[g % 2][:, :, :], ALU.subtract).then_inc(s("wq_lo"), 1)
                dve.wait_ge(*after("x_kept", l, 32))
                with dve.Fori(0, NKEYS // U_STEP) as it:
                    def turn(b):
                        dve.wait_ge(*after(f"u_in{b % RING}", l, it * (U_STEP // RING * 64) + 64 * (b // RING + 1)))
                        dve.wait_ge(*after("u_lo", l, it * U_STEP + (b + 1)))
                        V.transpose(uT[b % 4][:, :], ring[b % RING][:, :]).then_inc(s("u_turned"), 1)

                    rs = s("route_step")
                    n_ = [0]

                    def R(ins):
                        n_[0] += 1
                        ins.then_inc(rs, 1)
                        dve.wait_ge(rs, n_[0])

                    def top16(src, spare, vals, idx):
                        R(V.max(vals[:, 0:8], src))
                        V.max_index(idx[:, 0:8], vals[:, 0:8], src)
                        R(V.match_replace(spare, vals[:, 0:8], src, -3e38))
                        R(V.max(vals[:, 8:16], spare))
                        R(V.max_index(idx[:, 8:16], vals[:, 8:16], spare))

                    turn(0)
                    dve.wait_ge(*after("S_out", l, 8))
                    R(V.tensor_copy(fix[:, :, :], S[:, bass.ds(it, 1), :, :].rearrange("p a h n -> p (a h) n")))
                    top16(fix[:, 0, :], cut[:, 0:NKEYS], topv[:, 0, :], topi[:, 0, :])
                    turn(1)
                    top16(fix[:, 1, :], cut[:, 0:NKEYS], topv[:, 1, :], topi[:, 1, :])
                    turn(2)
                    R(V.tensor_tensor(cand[:, :, :], spread(topv[:, 0, :], 2, TOPK), spread(topv[:, 1, :], 1, TOPK),
                                      ALU.add))
                    flat = cand[:, :, :].rearrange("p a b -> p (a b)")
                    top16(flat, cut[:, :], topv[:, 2, :], topi[:, 2, :])
                    turn(3)
                    V.tensor_copy(topf[:, 0:2, :], topi[:, 0:2, :])
                    R(V.tensor_scalar(topb[:, :], topi[:, 2, :], 4, None, ALU.logical_shift_right))
                    R(V.tensor_copy(topf[:, 2, :], topb[:, :]))
                    pick(R, 0, routes[:, 0, bass.ds(it * TOPK, TOPK)])
                    turn(4)
                    R(V.tensor_scalar(topb[:, :], topi[:, 2, :], 15, None, ALU.bitwise_and))
                    R(V.tensor_copy(topf[:, 2, :], topb[:, :]))
                    pick(R, 1, routes[:, 1, bass.ds(it * TOPK, TOPK)])
                    turn(5)
                    R(V.tensor_copy(routes[:, 2, bass.ds(it * TOPK, TOPK)], topv[:, 2, :]))
                    turn(6)
                    turn(7)
                    dve.sem_clear(rs)
                dve.wait_ge(*after("u_turned", l, NKEYS + RING))
                dve.sem_inc(s("v_lo"), RING)
                gt = routes[:, 2, :].rearrange("p (n k) -> p n k", k=TOPK)
                gs = cut[:, 0:T].rearrange("p (n k) -> p n k", k=TOPK)
                L(V.tensor_tensor(gs, gt, spread(gt[:, :, 0], 2, TOPK), ALU.subtract))
                V.tensor_copy(cand[:, 0, :], gs[:, :, 0]).then_inc(s("gate_in"), 1)
                dve.wait_ge(*after("gate_exp", l, 1))
                L(V.tensor_reduce(topf[:, 0, :], gs, AX, ALU.add))
                L(V.reciprocal(topf[:, 1, :], topf[:, 0, :]))
                V.tensor_tensor(gt, gs, spread(topf[:, 1, :], 2, TOPK), ALU.mult).then_inc(s("routed"), 1)
                dve.wait_ge(*after("routes_T", l, 1))
                dve.wait_ge(*after("u_gelu", l, NKEYS // 2 + 4))
                dve.sem_inc(s("gated"), 4)
                dve.sem_inc(s("hot_dve"), 4)

                def take(it, d):
                    dve.wait_ge(*after("hot_dve", l, it * 4 + (4 * d + 4)))
                    dve.sem_inc(s("dve_held"), 1)
                    V.tensor_copy(cols["dve"][:, :, :], routes_T[:, 1:3, bass.ds(it * 16 + 16 * d, 16)]
                                  ).then_inc(s("cols_dve"), 1)
                    dve.wait_ge(*after("cols_dve", l, it + (d + 1)))

                def rows(it, d, b):
                    dve.wait_ge(*after("gate_mult", l, it * 4 + (4 * d + b + 1)))
                    if b % 2 == 0:
                        c = cols["dve"][:, :, 4 * b:4 * b + 1]
                        V.tensor_scalar(one_2[:, b, 0, :], iota[:, :], c[:, 0, :], c[:, 1, :],
                                        ALU.is_equal, ALU.mult)
                    V.tensor_tensor(one_1[:, b, :, :], spread(iota[:, :], 1, 4),
                                    spread(routes_T[:, 0, bass.ds(it * 16 + (16 * d + 4 * b), 4)], 2, NKEYS),
                                    ALU.is_equal).then_inc(s("hot_dve"), 1)

                def times(it, b):
                    dve.wait_ge(*after("gate_mult", l, it * 4 + (b + 5)))
                    w = W[:, :, bass.ds(it * 16 + 4 * b, 4)].rearrange("p j t -> p t j")
                    V.tensor_tensor(w, w, ps[:, b, :].rearrange("p (t j) -> p t j", t=4),
                                    ALU.mult).then_inc(s("gated"), 1)

                def gate_turn(it, last):
                    rows(it, 0, 2)
                    times(it, 0)
                    rows(it, 0, 3)
                    times(it, 1)
                    if not last:
                        take(it, 1)
                        rows(it, 1, 0)
                    times(it, 2)
                    if not last:
                        rows(it, 1, 1)
                    times(it, 3)

                take(0, 0)
                rows(0, 0, 0)
                rows(0, 0, 1)
                with dve.Fori(0, T // 16 - 1) as it:
                    gate_turn(it, False)
                gate_turn(T // 16 - 1, True)
                dve.wait_ge(*after("gated", l, T // 4 + 4))
                V.memset(zeros[:, :].bitcast(F32), 0.0).then_inc(s("zeros"), 1)

                def split_v(blk, b):
                    dve.wait_ge(*after("v_hi", l, blk + 1))
                    V.tensor_tensor(w_lo[b][:, :], W[:, bass.ds(blk, 1), :].rearrange("p a t -> p (a t)"),
                                    w_hi[b][:, :], ALU.subtract)
                    dve.wait_ge(*after("v_mult", l, blk + 3))
                    V.tensor_tensor(lo[b % 2][:, :], ring[b][:, :], hi[b][:, :],
                                    ALU.subtract).then_inc(s("v_lo"), 1)

                with dve.Fori(0, (V_PLAIN if l == 0 else NKEYS) // V_STEP) as it:
                    for b in range(V_STEP):
                        split_v(it * V_STEP + b, b)
                if l == 0:
                    dve.sem_inc(s("ada_1_used"), 2)
                    for third in range(3):
                        dve.wait_ge(*after(f"ada_1_b{third}", 0, 16))
                        a1 = acc_1[:, 4 * third:4 * third + 4, :].rearrange("p m n -> p (m n)")
                        with dve.Fori(0, KC // 2) as it:
                            for b in range(2 * V_STEP):
                                split_v(it * 2 * V_STEP + (V_PLAIN + 2 * V_STEP * (KC // 2) * third + b), b % V_STEP)
                                if b % V_STEP == 1:
                                    r = b // V_STEP
                                    dve.wait_ge(*after(f"ada_1_in{r}", 0, it * 16 + (16 * (KC // 2) * third + 16)))
                                    dve.wait_ge(*after("ada_1_used", 0, it * 2 + (KC * third + r + 2)))
                                    V.scalar_tensor_tensor(a1, ada_1[r][:, :], silu[:, bass.ds(it * 2 + r, 1)], a1,
                                                           ALU.mult, ALU.add).then_inc(s("ada_1_used"), 1)
                dve.wait_ge(*after("v_all", l, 1))
                dve.wait_ge(*after("x_back", l, 32))
                for t in range(TILES):
                    L(V.tensor_tensor(yg[:, t, :], ps[:, 4 + 2 * t:6 + 2 * t, :].rearrange("p a n -> p (a n)"),
                                      gate_b[:, :], ALU.mult))
                    L(V.tensor_tensor(xs[:, t, :], x_back[:, t, :], yg[:, t, :], ALU.add))
                    V.tensor_copy(ssq[:, 0, 0:1], xs[:, t, 0:1]).then_inc(layer_done, 1)

        @block.scalar
        def _(act):
            A = nc.scalar.activation
            L = lambda ins: link(act, "act", ins)

            for l in range(LAYERS):
                if l == 0:
                    act.wait_ge(*after("c_in", 0, 16))
                    A(cond[:, 1, :], cond[:, 0, :], ACT.Exp, scale=-1.0).then_inc(s("c_exp"), 1)

                def ada_out(n0, n1):
                    for n in range(n0, n1):
                        act.wait_ge(*after("ada_sum", l, n + 1))
                        A(mod[:, n // 2, 512 * (n % 2):512 * (n % 2) + 512], ps[:, ada_bank(l, n), :], ACT.Copy,
                          scale=-1.0).then_inc(s("ada_done"), 1)

                def rms(t, dst, done):
                    L(A(dst[:, t, :], xs[:, t, :], ACT.Square, accum_out=stat[:, t:t + 1]))
                    L(A(stat[:, 2 + t:3 + t], stat[:, t:t + 1], ACT.Copy, scale=1.0 / D, bias=EPS))
                    A(stat[:, 2 + t:3 + t], stat[:, 2 + t:3 + t], ACT.Sqrt).then_inc(done, 1)

                def w_in_part(i):
                    n, u = PIECES[l][i]
                    if u == 0:
                        act.wait_ge(*after(f"w_in{n}", l, 16))
                    if i >= 2:
                        act.wait_ge(*after("w_in_mult", l, i - 1))
                    A(piece_hi(l, n, i), piece(w_in(l, n), l, n, u), ACT.Copy).then_inc(s("w_in_hi"), 1)

                if l:
                    act.wait_ge(*after("ada_1_used", 0, 3 * KC + 2))
                    w_in_part(0)
                    w_in_part(1)
                ada_out(0, 4)
                if l == 0:
                    act.wait_ge(x_in, 16)
                for t in range(TILES):
                    if l:
                        act.wait_ge(layer_done, (l - 1) * TILES + t + 1)
                    rms(t, h, s("mix_rms"))
                if l:
                    ada_out(4, 12)
                for n in range(4):
                    act.wait_ge(*after("mix_T", l, n + 1))
                    t, half = n // 2, n % 2
                    A(mix_hi[:, 4 * half:4 * half + 4, P * t:P * t + P],
                      ps[:, 4 + n, :].rearrange("p (c t) -> p c t", c=4), ACT.Copy).then_inc(s("mix_hi"), 1)
                def proj_out(i):
                    n, u = PIECES[l][i]
                    act.wait_ge(*after("w_in_mult", l, i + 1))
                    if n < TOKEN_SETS[l]:
                        m = SETS[l][n][1]
                        for t in range(2 if u == 3 else 0):
                            A(tok[n][:, t, 0:m], ps[:, (2 * n + t) % 8, 0:m], ACT.Copy).then_inc(s("proj_out"), 1)
                    elif u % 2:
                        A(qk_T[n - 1][:, u - 1:u + 1, :],
                          ps[:, (2 * n + u // 2) % 8, :].rearrange("p (a t) -> p a t", a=2), ACT.Copy,
                          scale=SCALE if n == 3 else 1.0).then_inc(s("proj_out"), 1)

                last = len(PIECES[l])
                for i in range(2 * l, last + 2):
                    if i < last:
                        w_in_part(i)
                    if i >= 2:
                        proj_out(i - 2)
                    if i in ROOTS[l]:
                        pair = ROOTS[l][i]
                        c0, c1 = 32 * pair, 32 * pair + (20 if l == 0 else 32)
                        act.wait_ge(*after("ssq", l, pair + 1))
                        L(A(ssq[:, 1, c0:c1], ssq[:, 0, c0:c1], ACT.Copy, scale=1.0 / HD, bias=EPS))
                        A(ssq[:, 1, c0:c1], ssq[:, 1, c0:c1], ACT.Sqrt).then_inc(s("qk_rms"), 1)
                for n, (_, _, heads, _) in enumerate(NORMS[l]):
                    for t in range(TILES):
                        act.wait_ge(*after("qk_turned", l, 2 * n + t + 1))
                        w = heads * HD // P if heads == 8 else 2
                        A(qk_T[n][:, 0:w, P * t:P * t + P],
                          ps[:, (2 * n + t) % 4, 0:P * w].rearrange("p (a t) -> p a t", a=w),
                          ACT.Copy).then_inc(s("qk_T"), 1)
                def exps(q):
                    buf, top = sc[q % 2], smax[q % 2]
                    if l == 0 and q >= 2:
                        act.wait_ge(*after("scores", l, q + 1))
                        if q > 2:
                            act.wait_ge(*after("masked", l, q))
                        L(A(e_abs[:, :, :], ps[:, 0:4, 0:TRI], ACT.Abs))
                        L(A(e_abs[:, :, :], e_abs[:, :, :], ACT.Exp, scale=-1.0))
                        A(e_abs[:, :, :], e_abs[:, :, :], ACT.Ln, bias=1.0).then_inc(s("ln_done"), 1)
                        return
                    act.wait_ge(*after("max", l, q + 1))
                    if l == 0:
                        A(top[:, 2, :, :], top[:, 2, :, :], ACT.Exp)
                    for i in range(4):
                        A(buf[:, i, 0:P], buf[:, i, 0:P], ACT.Exp, bias=top[:, 0, i, 0:1], scale=SCALE,
                          accum_out=top[:, 1, i, 0:1])
                        last = A(buf[:, i, P:TRI], buf[:, i, P:TRI], ACT.Exp, bias=top[:, 0, i, 1:2], scale=SCALE,
                                 accum_out=top[:, 1, i, 1:2])
                    last.then_inc(s("exp"), 1)

                exps(0)
                for q in range(4):
                    early = q < 3 and not (l and q == 2)
                    if early:
                        exps(q + 1)
                    if l == 0 and q >= 2:
                        act.wait_ge(*after("log_w", l, q - 1))
                        A(pT[:, :, :], pT[:, :, :], ACT.Exp).then_inc(s("pT"), 1)
                    else:
                        act.wait_ge(*after("p_turned", l, q + 1))
                        A(pT[:, :, :], ps[:, p_bank(q):p_bank(q) + 4, 0:TRI], ACT.Copy).then_inc(s("pT"), 1)
                    if q < 3 and not early:
                        exps(q + 1)
                    act.wait_ge(*after("y", l, q + 1))
                    A(yT[:, 2 * q:2 * q + 2, :], ps[:, 4:6, 0:T], ACT.Copy).then_inc(s("y_out"), 1)
                    if l == 0 and q >= 2:
                        ada_out(4 * q - 4, 4 * q)
                def wq_part(g):
                    A(wq_hi[g % 2][:, :, :], wq[:, :, 2 * P * g:2 * P * g + 2 * P], ACT.Copy).then_inc(s("wq_hi"), 1)

                act.wait_ge(*after("mixed", l, 1))
                rms(0, hf, s("ffn_rms"))
                act.wait_ge(*after("w_out_mult", l, TILES))
                act.wait_ge(*after("wq", l, 64))
                wq_part(0)
                act.wait_ge(*after("mixed", l, TILES))
                rms(1, hf, s("ffn_rms"))
                for n in range(4):
                    act.wait_ge(*after("ffn_T", l, n + 1))
                    t, half = n // 2, n % 2
                    src = ps[:, 6 + half, :].rearrange("p (c t) -> p c t", c=4)
                    A(hT_hi[:, 4 * half:4 * half + 4, P * t:P * t + P], src, ACT.Copy).then_inc(s("ffn_hi"), 1)
                wq_part(1)
                act.wait_ge(*after("subk_turned", l, 1))
                A(subk_T[:, :, :], ps[:, 4, 0:2 * P].rearrange("p (a n) -> p a n", a=2), ACT.Copy
                  ).then_inc(s("subk_T"), 1)
                for g in range(PHEADS):
                    act.wait_ge(*after("qry", l, g + 1))
                    if g < PHEADS - 2:
                        wq_part(g + 2)
                    A(qryT[:, 2 * g:2 * g + 2, :], ps[:, g % 4, :].rearrange("p (a t) -> p a t", a=2),
                      ACT.Copy).then_inc(s("qry_out"), 1)
                def u_hi(it, b):
                    act.wait_ge(*after("u_turned", l, it * U_STEP + (b + 1 + RING)))
                    act.wait_ge(*after("u_mult", l, it * U_STEP + (b + 1)))
                    A(hi[b % 4][:, :].rearrange("p (c g i) -> p c g i", c=KC, g=4),
                      uT[b % 4][:, :].rearrange("p (g c i) -> p c g i", g=4, c=KC), ACT.Copy
                      ).then_inc(s("u_hi"), 1)

                def gelu(it, pair):
                    act.wait_ge(*after("u_mult", l, it * U_STEP + (2 * pair + 6)))
                    act.sem_inc(s("act_held"), 1)
                    A(W[:, bass.ds(it * U_STEP + 2 * pair, 2), :],
                      ps[:, pair, :].rearrange("p (a t) -> p a t", a=2), ACT.Gelu).then_inc(s("u_gelu"), 1)

                def turn(it, last):
                    for b in range(3, U_STEP + 3):
                        if b < U_STEP or not last:
                            u_hi(it, b)
                        if last and b == U_STEP + 1:
                            act.wait_ge(*after("gate_in", l, 1))
                            A(cut[:, 0:T], cut[:, 0:T], ACT.Exp).then_inc(s("gate_exp"), 1)
                        if b % 2:
                            gelu(it, b // 2 - 1)

                act.wait_ge(*after("x_kept", l, 32))
                for n in range(8):
                    act.wait_ge(*after("S_mult", l, n + 1))
                    A(S[:, 2 * n:2 * n + 2, :, :], ps[:, 4 + n % 4, :].rearrange("p (a h n) -> p a h n", a=2, h=2),
                      ACT.Copy).then_inc(s("S_out"), 1)
                    if n == 5:
                        u_hi(0, 0)
                act.sem_inc(s("u_gelu"), 4)
                for b in range(1, 3):
                    u_hi(0, b)
                with act.Fori(0, NKEYS // U_STEP - 1) as it:
                    turn(it, False)
                turn(NKEYS // U_STEP - 1, True)
                act.wait_ge(*after("routes_turned", l, 1))
                A(routes_T[:, :, :], ps[:, 4:7, 0:T], ACT.Copy).then_inc(s("routes_T"), 1)
                act.wait_ge(*after("routes_T", l, 1))
                act.sem_inc(s("hot_act"), 4)
                with act.Fori(0, T // 16) as it:
                    act.wait_ge(*after("hot_act", l, it * 4 + 4))
                    act.sem_inc(s("act_held"), 1)
                    A(cols["act"][:, 0, :], routes_T[:, 1, bass.ds(it * 16, 16)], ACT.Copy, scale=-1.0)
                    A(cols["act"][:, 1, :], routes_T[:, 2, bass.ds(it * 16, 16)], ACT.Copy).then_inc(s("cols_act"), 1)
                    act.wait_ge(*after("cols_act", l, it + 1))
                    for b in range(4):
                        for k in range(2):
                            n = 4 * b + 1 + k
                            last = A(gap[:, b, k, :], iota[:, :], ACT.Abs, bias=cols["act"][:, 0, n:n + 1])
                    last.then_inc(s("gap"), 1)
                    for b in range(4):
                        act.wait_ge(*after("gate_mult", l, it * 4 + (b + 1)))
                        act.sem_inc(s("act_held"), 1)
                        if b == 0:
                            act.wait_ge(*after("gap", l, it + 1))
                            act.sem_inc(s("act_held"), 1)
                        for k in range(2):
                            n = 4 * b + 1 + k
                            last = A(one_2[:, b, 1 + k, :], gap[:, b, k, :], ACT.Relu,
                                     bias=cols["act"][:, 1, n:n + 1], scale=-BIG)
                        last.then_inc(s("hot_act"), 1)
                act.wait_ge(*after("gated", l, T // 4 + 4))
                with act.Fori(0, NKEYS // V_STEP) as it:
                    for b in range(V_STEP):
                        act.wait_ge(*after("v_mult", l, it * V_STEP + (b + 1)))
                        act.sem_inc(s("act_held"), 1)
                        A(w_hi[b][:, :], W[:, bass.ds(it * V_STEP + b, 1), :].rearrange("p a t -> p (a t)"),
                          ACT.Copy)
                        act.wait_ge(*after(f"v_in{b % RING}", l, it * 16 + 16))
                        A(hi[b][:, :], ring[b % RING][:, :], ACT.Copy).then_inc(s("v_hi"), 1)

        @block.gpsimd
        def _(pool):
            nc.gpsimd.memset(acc_b[:, :, :], 0.0).then_inc(s("acc_b_zero"), 1)
            for l in range(LAYERS):
                if l:
                    pool.wait_ge(layer_done, l * TILES)
                for i, (n, u) in enumerate(PIECES[l]):
                    pool.wait_ge(*after("w_in_hi", l, i + 1))
                    nc.gpsimd.tensor_tensor(piece(w_in_lo[l][n], l, n, u), piece(w_in(l, n), l, n, u),
                                            piece_hi(l, n, i), ALU.subtract).then_inc(s("w_in_lo"), 1)
                for g in range(2):
                    pool.wait_ge(*after("wq_hi", l, g + 1))
                    nc.gpsimd.tensor_tensor(wq_lo[g][:, :, :], wq[:, :, 2 * P * g:2 * P * g + 2 * P],
                                            wq_hi[g][:, :, :], ALU.subtract).then_inc(s("wq_lo_pool"), 1)
                pool.wait_ge(*after("x_kept", l, 32))
                pool.sem_inc(s("u_lo"), 4)
                with pool.Fori(0, NKEYS // U_STEP) as it:
                    for b in range(U_STEP):
                        pool.wait_ge(*after("u_mult", l, it * U_STEP + (b + 3)))
                        pool.wait_ge(*after("u_hi", l, it * U_STEP + (b + 1)))
                        nc.gpsimd.tensor_tensor(
                            lo[b % 2][:, :].rearrange("p (c g i) -> p c g i", c=KC, g=4),
                            uT[b % 4][:, :].rearrange("p (g c i) -> p c g i", g=4, c=KC),
                            hi[b % 4][:, :].rearrange("p (c g i) -> p c g i", c=KC, g=4),
                            ALU.subtract).then_inc(s("u_lo"), 1)
                pool.wait_ge(*after("routes_T", l, 1))
                pool.sem_inc(s("hot_pool"), 4)
                with pool.Fori(0, T // 16) as it:
                    pool.wait_ge(*after("hot_pool", l, it * 4 + 4))
                    pool.sem_inc(s("pool_held"), 1)
                    nc.gpsimd.tensor_copy(cols["pool"][:, :, :], routes_T[:, 1:3, bass.ds(it * 16, 16)]
                                          ).then_inc(s("cols_pool"), 1)
                    pool.wait_ge(*after("cols_pool", l, it + 1))
                    pool.sem_inc(s("pool_held"), 1)
                    for b in range(4):
                        pool.wait_ge(*after("gate_mult", l, it * 4 + (b + 1)))
                        pool.sem_inc(s("pool_held"), 1)
                        for k in (0, 3) if b % 2 else (3,):
                            c = cols["pool"][:, :, 4 * b + k:4 * b + k + 1]
                            last = nc.gpsimd.tensor_scalar(one_2[:, b, k, :], iota[:, :], c[:, 0, :], c[:, 1, :],
                                                           ALU.is_equal, ALU.mult)
                        last.then_inc(s("hot_pool"), 1)
                if l == 0:
                    for third in range(3):
                        pool.wait_ge(*after("v_lo", 0, 16 + 8 * third + RING))
                        nc.gpsimd.memset(acc_1[:, 4 * third:4 * third + 4, :], 0.0).then_inc(s("acc_1_zero"), 1)


_INS = ['x', 'c', 'ada_w', 'ada_b', 'norm_mix_g', 'norm_ffn_g', 'w_in_ab', 'w_out_ab', 'sinks_a', 'qnorm_a',
        'knorm_a', 'w_in_cd', 'w_out_cd', 'qnorm_c', 'knorm_c', 'qnorm_d', 'knorm_d', 'peer_wq',
        'peer_subkeys', 'peer_u', 'peer_v']


def kernel(**inputs):
    import concourse.bacc as _bacc
    from concourse.bass_utils import run_bass_kernel_spmd as _run

    nc = _bacc.Bacc("TRN2", target_bir_lowering=False, num_devices=1)
    arrays, args = {}, []
    for name in _INS:
        a = np.ascontiguousarray(inputs[name])
        arrays[f"in_{name}"] = a
        args.append(nc.dram_tensor(f"in_{name}", a.shape, mybir.dt.from_np(a.dtype), kind="ExternalInput").ap())
    arrays["const"] = constants()
    args.append(nc.dram_tensor("const", (P, CONST_N), F32, kind="ExternalInput").ap())
    args.append(nc.dram_tensor("out", (1, T, D), F32, kind="ExternalOutput").ap())
    trunk_kernel(nc, *args)
    r = _run(nc, [arrays], core_ids=[0])
    return r.results[0]["out"]
```
